# Optimizing a Trainium2 kernel written in Bass

```python
import jax, jax.numpy as jnp
from jax import lax
import numpy as np
import math

D_MODEL = 1024
BATCH = 1
SEQ = 256
DEPTH = 2

N_A_LAYERS = DEPTH // 2
N_B_LAYERS = DEPTH - N_A_LAYERS
D_FF = 2816
D_RNN = 1344
N_LRU_BLOCKS = 16
LRU_BLOCK = D_RNN // N_LRU_BLOCKS
CONV_WIDTH = 4
LRU_C = 8.0
N_HEADS = 16
HEAD_DIM = 64
D_ATTN = N_HEADS * HEAD_DIM
Q_BLOCK = 128
EPS = 1e-6


def rms_norm(x, g):
    xf = x.astype(jnp.float32)
    y = xf * lax.rsqrt(jnp.mean(xf * xf, axis=-1, keepdims=True) + EPS)
    return (y * g.astype(jnp.float32)).astype(x.dtype)

def swiglu(x, w_gate, w_up, w_down):
    return (jax.nn.silu(x @ w_gate) * (x @ w_up)) @ w_down

def causal_depthwise_conv(x, w, b):
    S = x.shape[1]
    xp = jnp.pad(x, ((0, 0), (CONV_WIDTH - 1, 0), (0, 0)))
    y = b
    for k in range(CONV_WIDTH):
        y = y + xp[:, k:k + S] * w[k]
    return y

def rg_lru(x, w_a, b_a, w_x, b_x, lam):
    Bn, S, _ = x.shape
    xb = x.reshape(Bn, S, N_LRU_BLOCKS, LRU_BLOCK)
    r = jax.nn.sigmoid(jnp.einsum('bsnc,ncd->bsnd', xb, w_a).reshape(Bn, S, D_RNN) + b_a)
    i = jax.nn.sigmoid(jnp.einsum('bsnc,ncd->bsnd', xb, w_x).reshape(Bn, S, D_RNN) + b_x)
    log_a = -LRU_C * r.astype(jnp.float32) * jax.nn.softplus(-lam.astype(jnp.float32))
    a = jnp.exp(log_a)
    u = jnp.sqrt(-jnp.expm1(2.0 * log_a)) * (i * x).astype(jnp.float32)

    def combine(c1, c2):
        a1, b1 = c1
        a2, b2 = c2
        return a1 * a2, a2 * b1 + b2

    _, h = lax.associative_scan(combine, (a, u), axis=1)
    return h.astype(x.dtype)

def recurrent_block(x, w_in, conv_w, conv_b, w_a, b_a, w_x, b_x, lam, w_out):
    gx = x @ w_in
    gate, rec = gx[..., :D_RNN], gx[..., D_RNN:]
    rec = causal_depthwise_conv(rec, conv_w, conv_b)
    rec = rg_lru(rec, w_a, b_a, w_x, b_x, lam)
    return (jax.nn.gelu(gate) * rec) @ w_out

def shared_kv(h, g, w_kv, w_f, b_f):
    Bn, S, _ = h.shape
    hn = rms_norm(h, g)
    kv = (hn @ w_kv).reshape(Bn, S, 2, N_HEADS, HEAD_DIM)
    k = kv[:, :, 0].transpose(0, 2, 1, 3)
    v = kv[:, :, 1].transpose(0, 2, 1, 3)
    log_f = jax.nn.log_sigmoid((hn @ w_f + b_f).astype(jnp.float32))
    c = jnp.cumsum(log_f, axis=1).transpose(0, 2, 1)
    return k, v, c

def forgetting_attention(xq, w_q, w_o, k, v, c):
    Bn, S, _ = xq.shape
    q = (xq @ w_q).reshape(Bn, S, N_HEADS, HEAD_DIM).transpose(0, 2, 1, 3) * (HEAD_DIM ** -0.5)
    outs = []
    for blk in range(S // Q_BLOCK):
        q0 = blk * Q_BLOCK
        end = q0 + Q_BLOCK
        logits = jnp.einsum('bhqd,bhkd->bhqk', q[:, :, q0:end], k[:, :, :end]).astype(jnp.float32)
        logits = logits + c[:, :, q0:end, None] - c[:, :, None, :end]
        qpos = q0 + jnp.arange(Q_BLOCK)
        kpos = jnp.arange(end)
        logits = jnp.where(kpos[None, :] <= qpos[:, None], logits, -jnp.inf)
        p = jax.nn.softmax(logits, axis=-1).astype(v.dtype)
        outs.append(jnp.einsum('bhqk,bhkd->bhqd', p, v[:, :, :end]))
    o = jnp.concatenate(outs, axis=2).transpose(0, 2, 1, 3).reshape(Bn, S, D_ATTN)
    return o @ w_o

def first_inputs(seed: int = 0) -> dict:
    key = jax.random.key(seed)
    ks = iter(jax.random.split(key, 40))
    f32 = jnp.float32

    def nrm(shape, fan_in):
        return jax.random.normal(next(ks), shape, f32) * (fan_in ** -0.5)

    def gain(shape):
        return 1.0 + 0.05 * jax.random.normal(next(ks), shape, f32)

    def small(shape):
        return 0.02 * jax.random.normal(next(ks), shape, f32)

    L, NA, NB = DEPTH, N_A_LAYERS, N_B_LAYERS
    x = jax.random.normal(next(ks), (BATCH, SEQ, D_MODEL), f32)
    u = jax.random.uniform(next(ks), (NA, D_RNN), f32, minval=0.9, maxval=0.999)
    a0 = u ** (1.0 / LRU_C)
    rg_lambda = jnp.log(a0) - jnp.log1p(-a0)
    return {
        "x": x,
        "ffn1_pre_g": gain((L, D_MODEL)),
        "ffn1_w_gate": nrm((L, D_MODEL, D_FF), D_MODEL),
        "ffn1_w_up": nrm((L, D_MODEL, D_FF), D_MODEL),
        "ffn1_w_down": nrm((L, D_FF, D_MODEL), D_FF),
        "ffn1_post_g": gain((L, D_MODEL)),
        "mix_pre_g": gain((L, D_MODEL)),
        "mix_post_g": gain((L, D_MODEL)),
        "ffn2_pre_g": gain((L, D_MODEL)),
        "ffn2_w_gate": nrm((L, D_MODEL, D_FF), D_MODEL),
        "ffn2_w_up": nrm((L, D_MODEL, D_FF), D_MODEL),
        "ffn2_w_down": nrm((L, D_FF, D_MODEL), D_FF),
        "ffn2_post_g": gain((L, D_MODEL)),
        "rg_w_in": nrm((NA, D_MODEL, 2 * D_RNN), D_MODEL),
        "rg_conv_w": nrm((NA, CONV_WIDTH, D_RNN), CONV_WIDTH),
        "rg_conv_b": small((NA, D_RNN)),
        "rg_w_a": nrm((NA, N_LRU_BLOCKS, LRU_BLOCK, LRU_BLOCK), LRU_BLOCK),
        "rg_b_a": small((NA, D_RNN)),
        "rg_w_x": nrm((NA, N_LRU_BLOCKS, LRU_BLOCK, LRU_BLOCK), LRU_BLOCK),
        "rg_b_x": small((NA, D_RNN)),
        "rg_lambda": rg_lambda,
        "rg_w_out": nrm((NA, D_RNN, D_MODEL), D_RNN),
        "kv_norm_g": gain((D_MODEL,)),
        "w_kv": nrm((D_MODEL, 2 * D_ATTN), D_MODEL),
        "w_fgate": nrm((D_MODEL, N_HEADS), D_MODEL),
        "b_fgate": jax.random.uniform(next(ks), (N_HEADS,), f32, minval=1.0, maxval=4.0),
        "attn_w_q": nrm((NB, D_MODEL, D_ATTN), D_MODEL),
        "attn_w_o": nrm((NB, D_ATTN, D_MODEL), D_ATTN),
    }

def first_block(x, ffn1_pre_g, ffn1_w_gate, ffn1_w_up, ffn1_w_down, ffn1_post_g,
              mix_pre_g, mix_post_g,
              ffn2_pre_g, ffn2_w_gate, ffn2_w_up, ffn2_w_down, ffn2_post_g,
              rg_w_in, rg_conv_w, rg_conv_b, rg_w_a, rg_b_a, rg_w_x, rg_b_x, rg_lambda, rg_w_out,
              kv_norm_g, w_kv, w_fgate, b_fgate, attn_w_q, attn_w_o):
    h = x
    k = v = c = None
    for layer in range(DEPTH):
        if layer == N_A_LAYERS:
            k, v, c = shared_kv(h, kv_norm_g, w_kv, w_fgate, b_fgate)
        f = swiglu(rms_norm(h, ffn1_pre_g[layer]), ffn1_w_gate[layer], ffn1_w_up[layer], ffn1_w_down[layer])
        h = h + 0.5 * rms_norm(f, ffn1_post_g[layer])
        hn = rms_norm(h, mix_pre_g[layer])
        if layer < N_A_LAYERS:
            j = layer
            m = recurrent_block(hn, rg_w_in[j], rg_conv_w[j], rg_conv_b[j], rg_w_a[j], rg_b_a[j],
                                rg_w_x[j], rg_b_x[j], rg_lambda[j], rg_w_out[j])
        else:
            j = layer - N_A_LAYERS
            m = forgetting_attention(hn, attn_w_q[j], attn_w_o[j], k, v, c)
        h = h + rms_norm(m, mix_post_g[layer])
        f = swiglu(rms_norm(h, ffn2_pre_g[layer]), ffn2_w_gate[layer], ffn2_w_up[layer], ffn2_w_down[layer])
        h = h + 0.5 * rms_norm(f, ffn2_post_g[layer])
    return h


DEPTH_2 = 4

N_MIXERS = 3
GDN_HEADS = 8
GDN_DK = 128
GDN_DV = 128
GDN_CONV = 4
GDN_CHUNK = 64
SC_WIDTH = 3
NSA_HEADS = 16
NSA_KV_HEADS = 4
NSA_GROUP = NSA_HEADS // NSA_KV_HEADS
NSA_DH = 64
CMP_BLOCK = 32
CMP_STRIDE = 16
CMP_HIDDEN = 256
SLC_BLOCK = 64
SLC_TOPK = 16
N_LOCAL = 2
WINDOW = 512
NSA_Q_BLOCK = 32
ROPE_THETA = 10000.0
NEG = -1e30
FORCE = 1e9
N_GDN = (DEPTH_2 + 2) // 3
N_SC = (DEPTH_2 + 1) // 3
N_NSA = DEPTH_2 // 3


def rmsnorm(x, w):
    xf = x.astype(jnp.float32)
    y = xf * lax.rsqrt(jnp.mean(xf * xf, -1, keepdims=True) + EPS)
    return (y * w.astype(jnp.float32)).astype(x.dtype)

def l2norm(x):
    xf = x.astype(jnp.float32)
    return xf * lax.rsqrt(jnp.sum(xf * xf, -1, keepdims=True) + EPS)

def causal_depthwise_conv_2(x, w):
    width = w.shape[0]
    S = x.shape[1]
    xp = jnp.pad(x, ((0, 0), (width - 1, 0), (0, 0)))
    y = xp[:, 0:S] * w[0]
    for j in range(1, width):
        y = y + xp[:, j:j + S] * w[j]
    return y

def swiglu_2(h, w_gate_up, w_down):
    g, u = jnp.split(h @ w_gate_up, 2, axis=-1)
    return (jax.nn.silu(g) * u) @ w_down

def rope_tables(positions, dim):
    inv = 1.0 / (ROPE_THETA ** (jnp.arange(0, dim, 2, dtype=jnp.float32) / dim))
    ang = positions.astype(jnp.float32)[..., None] * inv
    ang = jnp.concatenate([ang, ang], axis=-1)[:, :, None, :]
    return jnp.cos(ang), jnp.sin(ang)

def apply_rope(x, cos, sin):
    x1, x2 = jnp.split(x, 2, axis=-1)
    rot = jnp.concatenate([-x2, x1], axis=-1)
    return (x * cos + rot * sin).astype(x.dtype)

def gated_delta_rule_chunked(q, k, v, g, beta):
    B, S, H, dk = q.shape
    dv = v.shape[-1]
    C = GDN_CHUNK
    N = S // C

    def to_chunks(t):
        return jnp.moveaxis(t.reshape((B, N, C, H) + t.shape[3:]), 3, 1)

    q = to_chunks(q) * (dk ** -0.5)
    k = to_chunks(k)
    v = to_chunks(v)
    g = to_chunks(g)
    beta = to_chunks(beta)
    gc = jnp.cumsum(g, axis=-1)
    causal = jnp.tril(jnp.ones((C, C), bool))
    strict = jnp.tril(jnp.ones((C, C), bool), -1)
    decay = jnp.exp(jnp.where(causal, gc[..., :, None] - gc[..., None, :], -jnp.inf))
    k_beta = k * beta[..., None]
    A = jnp.where(strict, jnp.einsum('bhncd,bhned->bhnce', k_beta, k) * decay, 0.0)
    eye = jnp.eye(C, dtype=jnp.float32)
    u = lax.linalg.triangular_solve(eye + A, v * beta[..., None], left_side=True,
                                    lower=True, unit_diagonal=True)
    w = lax.linalg.triangular_solve(eye + A, k_beta * jnp.exp(gc)[..., None], left_side=True,
                                    lower=True, unit_diagonal=True)
    attn_intra = jnp.where(causal, jnp.einsum('bhncd,bhned->bhnce', q, k) * decay, 0.0)
    q_dec = q * jnp.exp(gc)[..., None]
    k_dec = k * jnp.exp(gc[..., -1:] - gc)[..., None]
    g_last = jnp.exp(gc[..., -1])
    xs = tuple(jnp.moveaxis(t, 2, 0) for t in (q_dec, k_dec, u, w, attn_intra, g_last))

    def step(state, inp):
        qd, kd, u_c, w_c, a_c, gl = inp
        v_new = u_c - jnp.einsum('bhcd,bhde->bhce', w_c, state)
        o = jnp.einsum('bhcd,bhde->bhce', qd, state) + jnp.einsum('bhce,bhef->bhcf', a_c, v_new)
        state = state * gl[..., None, None] + jnp.einsum('bhcd,bhce->bhde', kd, v_new)
        return state, o

    s0 = jnp.zeros((B, H, dk, dv), jnp.float32)
    _, o = lax.scan(step, s0, xs)
    return jnp.transpose(o, (1, 0, 3, 2, 4)).reshape(B, S, H, dv)

def gdn_mixer(h, w_in, conv_w, A_log, dt_bias, out_norm, w_out):
    B, S, _ = h.shape
    H, dk, dv = GDN_HEADS, GDN_DK, GDN_DV
    n_qkv = 2 * H * dk + H * dv
    proj = h @ w_in
    qkv, gate, a, b = jnp.split(proj, [n_qkv, n_qkv + H * dv, n_qkv + H * dv + H], axis=-1)
    qkv = jax.nn.silu(causal_depthwise_conv_2(qkv, conv_w))
    q, k, v = jnp.split(qkv, [H * dk, 2 * H * dk], axis=-1)
    q = l2norm(q.reshape(B, S, H, dk))
    k = l2norm(k.reshape(B, S, H, dk))
    v = v.reshape(B, S, H, dv).astype(jnp.float32)
    beta = jax.nn.sigmoid(b.astype(jnp.float32))
    g = -jnp.exp(A_log.astype(jnp.float32)) * jax.nn.softplus(
        a.astype(jnp.float32) + dt_bias.astype(jnp.float32))
    o = gated_delta_rule_chunked(q, k, v, g, beta)
    o = rmsnorm(o, out_norm) * jax.nn.silu(gate.reshape(B, S, H, dv).astype(jnp.float32))
    return o.reshape(B, S, H * dv).astype(h.dtype) @ w_out

def short_conv_mixer(h, w_in, conv_w, w_out):
    b_gate, c_gate, xin = jnp.split(h @ w_in, 3, axis=-1)
    y = causal_depthwise_conv_2(c_gate * xin, conv_w)
    return (b_gate * y) @ w_out

def nsa_mixer(h, cos, sin, w_in, q_norm, k_norm, cmp_pe, cmp_w1, cmp_b1, cmp_w2, cmp_b2, w_out):
    B, S, _ = h.shape
    H, Hk, G, dh = NSA_HEADS, NSA_KV_HEADS, NSA_GROUP, NSA_DH
    kvw = Hk * dh
    sizes = [H * dh] + [kvw] * 6
    splits = [int(s) for s in np.cumsum(sizes)]
    q, kc, vc, ks, vs, kw, vw, gates = jnp.split(h @ w_in, splits, axis=-1)
    q = rmsnorm(q.reshape(B, S, H, dh), q_norm)
    q_rot = apply_rope(q, cos, sin)
    ks = apply_rope(rmsnorm(ks.reshape(B, S, Hk, dh), k_norm[1]), cos, sin)
    kw = apply_rope(rmsnorm(kw.reshape(B, S, Hk, dh), k_norm[2]), cos, sin)
    vs = vs.reshape(B, S, Hk, dh)
    vw = vw.reshape(B, S, Hk, dh)
    gates = jax.nn.sigmoid(gates.reshape(B, S, H, 3).astype(jnp.float32))

    r = CMP_BLOCK // CMP_STRIDE
    n_chunks = S // CMP_STRIDE
    Nc = n_chunks - r + 1

    def compress(t, i):
        c = t.reshape(B, n_chunks, CMP_STRIDE, Hk, dh)
        blocks = jnp.concatenate([c[:, j:j + Nc] for j in range(r)], axis=2)
        blocks = blocks + cmp_pe[i][:, None, :]
        blocks = jnp.moveaxis(blocks, 3, 2).reshape(B, Nc, Hk, CMP_BLOCK * dh)
        hid = jax.nn.gelu(blocks @ cmp_w1[i] + cmp_b1[i])
        return hid @ cmp_w2[i] + cmp_b2[i]

    kc = rmsnorm(compress(kc.reshape(B, S, Hk, dh), 0), k_norm[0])
    vc = compress(vc.reshape(B, S, Hk, dh), 1)

    qn_t = q.reshape(B, S, Hk, G, dh).transpose(0, 2, 3, 1, 4)
    qr_t = q_rot.reshape(B, S, Hk, G, dh).transpose(0, 2, 3, 1, 4)
    kc_t = kc.transpose(0, 2, 1, 3)
    vc_t = vc.transpose(0, 2, 1, 3)
    Ns = S // SLC_BLOCK
    n_sel = min(SLC_TOPK, Ns)
    ks_blk = ks.transpose(0, 2, 1, 3).reshape(B, Hk, Ns, SLC_BLOCK, dh)
    vs_blk = vs.transpose(0, 2, 1, 3).reshape(B, Hk, Ns, SLC_BLOCK, dh)
    pad = ((0, 0), (0, 0), (WINDOW, 0), (0, 0))
    kw_pad = jnp.pad(kw.transpose(0, 2, 1, 3), pad)
    vw_pad = jnp.pad(vw.transpose(0, 2, 1, 3), pad)

    cmp_end = jnp.arange(Nc) * CMP_STRIDE + CMP_BLOCK - 1
    ci = jnp.arange(Nc)[:, None]
    sj = jnp.arange(Ns)[None, :]
    overlap = jnp.clip(jnp.minimum(ci * CMP_STRIDE + CMP_BLOCK, (sj + 1) * SLC_BLOCK)
                       - jnp.maximum(ci * CMP_STRIDE, sj * SLC_BLOCK), 0, None)
    overlap = overlap.astype(jnp.float32) / CMP_BLOCK
    blk_ids = jnp.arange(Ns)
    b_idx = jnp.arange(B)[:, None, None, None]
    h_idx = jnp.arange(Hk)[None, :, None, None]
    scale = dh ** -0.5
    QB = NSA_Q_BLOCK

    def block(i):
        s0 = i * QB
        tpos = s0 + jnp.arange(QB)
        qn = lax.dynamic_slice_in_dim(qn_t, s0, QB, axis=3).astype(jnp.float32)
        qr = lax.dynamic_slice_in_dim(qr_t, s0, QB, axis=3).astype(jnp.float32)
        sc = jnp.einsum('bhgqd,bhkd->bhgqk', qn, kc_t) * scale
        cmask = cmp_end[None, :] <= tpos[:, None]
        p_c = jax.nn.softmax(jnp.where(cmask, sc, NEG), axis=-1)
        p_c = jnp.where(cmask.any(-1)[:, None], p_c, 0.0)
        o_c = jnp.einsum('bhgqk,bhkd->bhgqd', p_c, vc_t)
        imp = jnp.einsum('bhgqc,cs->bhqs', p_c, overlap)
        svalid = (blk_ids * SLC_BLOCK)[None, :] <= tpos[:, None]
        dist = (tpos // SLC_BLOCK)[:, None] - blk_ids[None, :]
        forced = (blk_ids == 0)[None, :] | ((dist >= 0) & (dist < N_LOCAL))
        score = jnp.where(svalid & forced, FORCE, jnp.where(svalid, imp, -1.0))
        top_score, idx = lax.top_k(score, n_sel)
        sel_valid = top_score >= 0.0
        kb = ks_blk[b_idx, h_idx, idx]
        vb = vs_blk[b_idx, h_idx, idx]
        ss = jnp.einsum('bhgqd,bhqnkd->bhgqnk', qr, kb) * scale
        kpos = idx[..., None] * SLC_BLOCK + jnp.arange(SLC_BLOCK)
        smask = sel_valid[..., None] & (kpos <= tpos[:, None, None])
        ss = jnp.where(smask[:, :, None], ss, NEG)
        p_s = jax.nn.softmax(ss.reshape(B, Hk, G, QB, n_sel * SLC_BLOCK), axis=-1)
        p_s = p_s.reshape(B, Hk, G, QB, n_sel, SLC_BLOCK)
        o_s = jnp.einsum('bhgqnk,bhqnkd->bhgqd', p_s, vb)
        kwin = lax.dynamic_slice_in_dim(kw_pad, s0, WINDOW + QB, axis=2)
        vwin = lax.dynamic_slice_in_dim(vw_pad, s0, WINDOW + QB, axis=2)
        wpos = s0 - WINDOW + jnp.arange(WINDOW + QB)
        wmask = ((wpos[None, :] <= tpos[:, None]) & (wpos[None, :] > tpos[:, None] - WINDOW)
                 & (wpos[None, :] >= 0))
        sw = jnp.einsum('bhgqd,bhkd->bhgqk', qr, kwin) * scale
        p_w = jax.nn.softmax(jnp.where(wmask, sw, NEG), axis=-1)
        o_w = jnp.einsum('bhgqk,bhkd->bhgqd', p_w, vwin)
        return o_c, o_s, o_w

    o_c, o_s, o_w = lax.map(block, jnp.arange(S // QB))

    def to_bshd(o):
        return jnp.transpose(o, (1, 0, 4, 2, 3, 5)).reshape(B, S, H, dh)

    o = (gates[..., 0:1] * to_bshd(o_c) + gates[..., 1:2] * to_bshd(o_s)
         + gates[..., 2:3] * to_bshd(o_w))
    return o.reshape(B, S, H * dh).astype(h.dtype) @ w_out

def second_inputs(seed: int = 0) -> dict:
    key = jax.random.key(seed)
    ks = jax.random.split(key, 26)
    f32 = jnp.float32
    D, F = D_MODEL, D_FF

    def nrm(k, shape, scale):
        return jax.random.normal(k, shape, f32) * scale

    def gain(k, shape):
        return 1.0 + 0.02 * jax.random.normal(k, shape, f32)

    gdn_in = 2 * GDN_HEADS * GDN_DK + 2 * GDN_HEADS * GDN_DV + 2 * GDN_HEADS
    nsa_in = NSA_HEADS * NSA_DH + 6 * NSA_KV_HEADS * NSA_DH + 3 * NSA_HEADS
    n_conv = 2 * GDN_HEADS * GDN_DK + GDN_HEADS * GDN_DV
    dt = jnp.exp(jax.random.uniform(ks[7], (N_GDN, GDN_HEADS), f32,
                                    minval=math.log(1e-3), maxval=math.log(1e-1)))
    return {
        "x": jax.random.normal(ks[0], (BATCH, SEQ, D), f32),
        "positions": jnp.broadcast_to(jnp.arange(SEQ, dtype=jnp.int32), (BATCH, SEQ)),
        "ffn_norm": gain(ks[1], (DEPTH_2, 2, D)),
        "ffn_w_gate_up": nrm(ks[2], (DEPTH_2, 2, D, 2 * F), D ** -0.5),
        "ffn_w_down": nrm(ks[3], (DEPTH_2, 2, F, D), F ** -0.5),
        "mixer_norm": gain(ks[4], (DEPTH_2, D)),
        "gdn_w_in": nrm(ks[5], (N_GDN, D, gdn_in), D ** -0.5),
        "gdn_conv_w": nrm(ks[6], (N_GDN, GDN_CONV, n_conv), GDN_CONV ** -0.5),
        "gdn_A_log": jnp.log(jax.random.uniform(ks[8], (N_GDN, GDN_HEADS), f32, minval=1.0, maxval=16.0)),
        "gdn_dt_bias": dt + jnp.log(-jnp.expm1(-dt)),
        "gdn_out_norm": gain(ks[9], (N_GDN, GDN_DV)),
        "gdn_w_out": nrm(ks[10], (N_GDN, GDN_HEADS * GDN_DV, D), (GDN_HEADS * GDN_DV) ** -0.5),
        "sc_w_in": nrm(ks[11], (N_SC, D, 3 * D), D ** -0.5),
        "sc_conv_w": nrm(ks[12], (N_SC, SC_WIDTH, D), SC_WIDTH ** -0.5),
        "sc_w_out": nrm(ks[13], (N_SC, D, D), D ** -0.5),
        "nsa_w_in": nrm(ks[14], (N_NSA, D, nsa_in), D ** -0.5),
        "nsa_q_norm": gain(ks[15], (N_NSA, NSA_DH)),
        "nsa_k_norm": gain(ks[16], (N_NSA, 3, NSA_DH)),
        "nsa_cmp_pe": nrm(ks[17], (N_NSA, 2, CMP_BLOCK, NSA_DH), 0.02),
        "nsa_cmp_w1": nrm(ks[18], (N_NSA, 2, CMP_BLOCK * NSA_DH, CMP_HIDDEN), (CMP_BLOCK * NSA_DH) ** -0.5),
        "nsa_cmp_b1": nrm(ks[19], (N_NSA, 2, CMP_HIDDEN), 0.01),
        "nsa_cmp_w2": nrm(ks[20], (N_NSA, 2, CMP_HIDDEN, NSA_DH), CMP_HIDDEN ** -0.5),
        "nsa_cmp_b2": nrm(ks[21], (N_NSA, 2, NSA_DH), 0.01),
        "nsa_w_out": nrm(ks[22], (N_NSA, NSA_HEADS * NSA_DH, D), (NSA_HEADS * NSA_DH) ** -0.5),
    }

def second_block(x, positions, ffn_norm, ffn_w_gate_up, ffn_w_down, mixer_norm,
              gdn_w_in, gdn_conv_w, gdn_A_log, gdn_dt_bias, gdn_out_norm, gdn_w_out,
              sc_w_in, sc_conv_w, sc_w_out,
              nsa_w_in, nsa_q_norm, nsa_k_norm, nsa_cmp_pe, nsa_cmp_w1, nsa_cmp_b1,
              nsa_cmp_w2, nsa_cmp_b2, nsa_w_out):
    cos, sin = rope_tables(positions, NSA_DH)
    h = x
    for layer in range(DEPTH_2):
        h = h + 0.5 * swiglu_2(rmsnorm(h, ffn_norm[layer, 0]), ffn_w_gate_up[layer, 0], ffn_w_down[layer, 0])
        hn = rmsnorm(h, mixer_norm[layer])
        kind = layer % N_MIXERS
        j = layer // N_MIXERS
        if kind == 0:
            mix = gdn_mixer(hn, gdn_w_in[j], gdn_conv_w[j], gdn_A_log[j], gdn_dt_bias[j],
                            gdn_out_norm[j], gdn_w_out[j])
        elif kind == 1:
            mix = short_conv_mixer(hn, sc_w_in[j], sc_conv_w[j], sc_w_out[j])
        else:
            mix = nsa_mixer(hn, cos, sin, nsa_w_in[j], nsa_q_norm[j], nsa_k_norm[j], nsa_cmp_pe[j],
                            nsa_cmp_w1[j], nsa_cmp_b1[j], nsa_cmp_w2[j], nsa_cmp_b2[j], nsa_w_out[j])
        h = h + mix
        h = h + 0.5 * swiglu_2(rmsnorm(h, ffn_norm[layer, 1]), ffn_w_gate_up[layer, 1], ffn_w_down[layer, 1])
    return h


def setup_inputs(seed=0):
    out = dict(first_inputs(seed))
    for name, value in second_inputs(seed + 1).items():
        if name != "x":
            out[name + "_2"] = value
    return out


def reference(
    x, ffn1_pre_g, ffn1_w_gate, ffn1_w_up, ffn1_w_down, ffn1_post_g, mix_pre_g, mix_post_g,
    ffn2_pre_g, ffn2_w_gate, ffn2_w_up, ffn2_w_down, ffn2_post_g, rg_w_in, rg_conv_w, rg_conv_b,
    rg_w_a, rg_b_a, rg_w_x, rg_b_x, rg_lambda, rg_w_out, kv_norm_g, w_kv, w_fgate, b_fgate,
    attn_w_q, attn_w_o, positions_2, ffn_norm_2, ffn_w_gate_up_2, ffn_w_down_2, mixer_norm_2,
    gdn_w_in_2, gdn_conv_w_2, gdn_A_log_2, gdn_dt_bias_2, gdn_out_norm_2, gdn_w_out_2,
    sc_w_in_2, sc_conv_w_2, sc_w_out_2, nsa_w_in_2, nsa_q_norm_2, nsa_k_norm_2, nsa_cmp_pe_2,
    nsa_cmp_w1_2, nsa_cmp_b1_2, nsa_cmp_w2_2, nsa_cmp_b2_2, nsa_w_out_2,
):
    x = first_block(
        x, ffn1_pre_g, ffn1_w_gate, ffn1_w_up, ffn1_w_down, ffn1_post_g, mix_pre_g, mix_post_g,
        ffn2_pre_g, ffn2_w_gate, ffn2_w_up, ffn2_w_down, ffn2_post_g, rg_w_in, rg_conv_w,
        rg_conv_b, rg_w_a, rg_b_a, rg_w_x, rg_b_x, rg_lambda, rg_w_out, kv_norm_g, w_kv,
        w_fgate, b_fgate, attn_w_q, attn_w_o,
    )
    return second_block(
        x, positions_2, ffn_norm_2, ffn_w_gate_up_2, ffn_w_down_2, mixer_norm_2, gdn_w_in_2,
        gdn_conv_w_2, gdn_A_log_2, gdn_dt_bias_2, gdn_out_norm_2, gdn_w_out_2, sc_w_in_2,
        sc_conv_w_2, sc_w_out_2, nsa_w_in_2, nsa_q_norm_2, nsa_k_norm_2, nsa_cmp_pe_2,
        nsa_cmp_w1_2, nsa_cmp_b1_2, nsa_cmp_w2_2, nsa_cmp_b2_2, nsa_w_out_2,
    )


_drawn_inputs = setup_inputs


def setup_inputs(seed=0):
    import zlib

    import numpy as np

    out = dict(_drawn_inputs(seed))
    spreads = {}
    factors = {'rg_b_a': 8.0,
     'rg_b_x': 6.519,
     'ffn_norm_2': 4.465,
     'gdn_out_norm_2': 7.334,
     'nsa_q_norm_2': 200.0,
     'nsa_k_norm_2': 200.0,
     'nsa_cmp_pe_2': 55.238,
     'nsa_cmp_b1_2': 180.12,
     'nsa_cmp_b2_2': 64.0}
    for name, (base, spread) in spreads.items():
        noise = np.random.default_rng([zlib.crc32(name.encode()), seed]).standard_normal(out[name].shape)
        drawn = base * np.exp(spread * noise) if base else spread * noise
        out[name] = __import__('jax').numpy.asarray(drawn.astype(out[name].dtype))
    for name, factor in factors.items():
        out[name] = (out[name] * factor).astype(out[name].dtype)
    return out
```

```python
from contextlib import ExitStack

import concourse.bass as bass
from concourse import mybir

F32 = mybir.dt.float32
F32R = mybir.dt.float32r
ALU = mybir.AluOpType
ACT = mybir.ActivationFunctionType
AX = mybir.AxisListType.X

P = 128
D_MODEL = 1024
SEQ = 256
TOKS = SEQ // P
KD = D_MODEL // P
D_FF = 2816
FCOLS = 256
CHUNKS = D_FF // FCOLS
RING = 3
SLAB = 2048
PCOLS = SLAB // KD
EPS = 1e-6
ARENA = 16384

ACC, GU, HT = 0, 4, 6
NORM_BANKS = (6, 7, 2, 3)


class Core:

    def __init__(self, nc, ctx):
        self.nc, self.ctx = nc, ctx
        self.sems = {}

        def sb(name, shape, dt=F32):
            return ctx.enter_context(nc.sbuf_tensor(name, shape, dt))

        self.sb = sb
        self.h = sb("h", [P, TOKS, D_MODEL])
        self.xn = sb("xn", [P, TOKS, D_MODEL])
        self.xT_hi = sb("xT_hi", [P, 2 * KD, SEQ], F32R)
        self.xT_lo = sb("xT_lo", [P, 2 * KD, SEQ], F32R)
        self.arena = sb("arena", [P, ARENA])
        self.mix_out = sb("mix_out", [P, TOKS, D_MODEL])
        self.raw = [sb(f"raw{r}", [P, SLAB]) for r in range(RING)]
        self.w_hi = [sb(f"w_hi{r}", [P, SLAB], F32R) for r in range(RING)]
        self.w_lo = [sb(f"w_lo{r}", [P, SLAB], F32R) for r in range(RING)]
        self.silu = sb("silu", [P, TOKS, FCOLS])
        self.hid = sb("hid", [P, TOKS, FCOLS])
        self.hidT_hi = sb("hidT_hi", [P, FCOLS // P, SEQ], F32R)
        self.hidT_lo = sb("hidT_lo", [P, FCOLS // P, SEQ], F32R)
        self.post_gain = sb("post_gain", [P, D_MODEL])
        self.ssq = sb("ssq", [P, TOKS * 2])
        self.ms = sb("ms", [P, TOKS])
        self.rms = sb("rms", [P, TOKS])
        self.rstd = sb("rstd", [P, TOKS])
        self.ident = sb("ident", [P, P])
        self.nsa_pos = sb("nsa_pos", [P, TOKS], mybir.dt.int32)
        self.ones = sb("ones", [P, P])
        self.upper = sb("upper", [P, P])
        self.causal = sb("causal", [P, 3 * P])
        self.bank = [ctx.enter_context(nc.psum_tensor(f"bank{b}", [P, 512], F32)) for b in range(8)]

    def sem(self, name):
        if name not in self.sems:
            self.sems[name] = self.ctx.enter_context(self.nc.semaphore(name))
        return self.sems[name]


class Chain:

    def __init__(self, eng, sem):
        self.eng, self.sem, self.n, self.past = eng, sem, 0, 0

    def __call__(self, ins):
        self.n += 1
        ins.then_inc(self.sem, 1)
        self.eng.wait_ge(self.sem, self.past + self.n)



def slab_number(base, i):
    return base + RING * i, base % RING, base // RING + i


def act_split(c, act, s):
    n, r, before = s
    if isinstance(n, int) and n >= c.slabs:
        return
    act.wait_ge(c.raw_landed[r], 32 * before + 32)
    if not (isinstance(n, int) and n < RING):
        act.wait_ge(c.sem("slab_used"), n - RING + 1)
    c.nc.scalar.activation(c.w_hi[r][:], c.raw[r][:], ACT.Copy).then_inc(c.sem("w_hi_split"), 1)


def dve_split(c, dve, s):
    n, r, before = s
    if isinstance(n, int) and n >= c.slabs:
        return
    dve.wait_ge(c.sem("w_hi_split"), n + 1)
    c.nc.vector.tensor_tensor(c.w_lo[r][:], c.raw[r][:], c.w_hi[r][:].bitcast(F32),
                              ALU.subtract).then_inc(c.sem("w_lo_split"), 1)


def sp_load(c, sp, s, pairs):
    n, r, before = s
    if not (isinstance(n, int) and n < RING):
        sp.wait_ge(c.sem("w_lo_split"), n - RING + 1)
    for dst, src in pairs:
        sp.dma_start(dst, src).then_inc(c.raw_landed[r], 16)


def pe_matmul3(c, out, x_hi, x_lo, w_hi, w_lo, start, stop, swap=False):
    mm = c.nc.tensor.matmul
    if swap:
        mm(out, w_hi, x_hi, start=start, stop=False)
        mm(out, w_hi, x_lo, start=False, stop=False)
        return mm(out, w_lo, x_hi, start=False, stop=stop)
    mm(out, x_hi, w_hi, start=start, stop=False)
    mm(out, x_hi, w_lo, start=False, stop=False)
    return mm(out, x_lo, w_hi, start=False, stop=stop)



def act_norm(c, act, st):
    n = st.norm
    if st.updates:
        act.wait_ge(c.sem("h_updated"), st.updates)
    else:
        act.wait_ge(c.sem("x_loaded"), 16)
    for t in range(TOKS):
        c.nc.scalar.activation(c.xn[:, t, :], c.h[:, t, :], ACT.Square,
                               accum_out=c.ssq[:, t:t + 1]).then_inc(c.sem("squares_summed"), 1)
    act.wait_ge(c.sem("mean_square"), n + 1)
    c.nc.scalar.activation(c.rms[:], c.ms[:], ACT.Sqrt).then_inc(c.sem("rms_ready"), 1)
    for k in range(KD):
        act.wait_ge(c.sem("xn_transposed"), 4 * n + k // 2 + 1)
        if k == 0 and n == 0:
            act.wait_ge(c.sem("gains_loaded"), 16)
        c.nc.scalar.activation(c.xT_hi[:, k, :], c.bank[NORM_BANKS[k // 2]][:, (k % 2) * SEQ:(k % 2 + 1) * SEQ],
                               ACT.Copy, scale=c.gains[:, n * KD + k:n * KD + k + 1]
                               ).then_inc(c.sem("xT_hi_ready"), 1)


def dve_norm(c, dve, st):
    n = st.norm
    dve.wait_ge(c.sem("squares_summed"), 2 * n + 2)
    c.nc.vector.tensor_scalar(c.ms[:], c.ssq[:, 0:TOKS], 1.0 / D_MODEL, EPS, ALU.mult, ALU.add
                              ).then_inc(c.sem("mean_square"), 1)
    dve.wait_ge(c.sem("rms_ready"), n + 1)
    c.chain(c.nc.vector.reciprocal(c.rstd[:], c.rms[:]))
    for t in range(TOKS):
        c.nc.vector.tensor_scalar(c.xn[:, t, :], c.h[:, t, :], c.rstd[:, t:t + 1], None, ALU.mult
                                  ).then_inc(c.sem("xn_ready"), 1)
    for k in range(KD):
        dve.wait_ge(c.sem("xT_hi_ready"), KD * n + 2 * (k // 2) + 2)
        if k == 0 and n == 0:
            dve.wait_ge(c.sem("gains_loaded"), 16)
        c.nc.vector.scalar_tensor_tensor(
            c.xT_lo[:, k, :], c.bank[NORM_BANKS[k // 2]][:, (k % 2) * SEQ:(k % 2 + 1) * SEQ],
            c.gains[:, n * KD + k:n * KD + k + 1], c.xT_hi[:, k, :].bitcast(F32), ALU.mult, ALU.subtract
        ).then_inc(c.sem("xT_lo_ready"), 1)


def pe_norm(c, pe, st):
    n = st.norm
    if n == 0:
        pe.wait_ge(c.sem("masks_made"), MASK_STEPS)
    pe.wait_ge(c.sem("xn_ready"), 2 * n + 2)
    for g in range(KD // 2):
        for k in (2 * g, 2 * g + 1):
            for t in range(TOKS):
                last = c.nc.tensor.transpose(
                    c.bank[NORM_BANKS[g]][:, (k % 2) * SEQ + t * P:(k % 2) * SEQ + (t + 1) * P],
                    c.xn[:, t, k * P:(k + 1) * P], c.ident[:])
        last.then_inc(c.sem("xn_transposed"), 1)



def ffn_views(c, st):
    def gate_up(r, half, j):
        raw = c.raw[r][:].rearrange("p (k n) -> p k n", k=KD // 2)
        rows = slice(half * D_MODEL // 2, (half + 1) * D_MODEL // 2)
        return [(raw[:, :, s * FCOLS:(s + 1) * FCOLS],
                 w[rows, bass.ds(off + j * FCOLS, FCOLS)].rearrange("(k p) n -> p k n", p=P))
                for s, (w, off) in enumerate((st.gate, st.up))]

    def down(r, j):
        raw = c.raw[r][:].rearrange("p (k n) -> p k n", k=FCOLS // P)
        return [(raw[:, q, :], st.down[bass.ds(j * FCOLS + q * P, P), :]) for q in range(FCOLS // P)]
    return gate_up, down


def sp_ffn(c, sp, st):
    gate_up, down = ffn_views(c, st)
    b = st.slab
    sp_load(c, sp, slab_number(b, 0), gate_up(b % RING, 0, 0))
    sp_load(c, sp, slab_number(b + 1, 0), gate_up((b + 1) % RING, 1, 0))
    with c.nc.sync.Fori(1, CHUNKS) as j:
        sp_load(c, sp, slab_number(b - 1, j), gate_up((b - 1) % RING, 0, j))
        sp_load(c, sp, slab_number(b, j), gate_up(b % RING, 1, j))
        sp_load(c, sp, slab_number(b + 1, j), down((b + 1) % RING, j - 1))
    e = b + 3 * CHUNKS - 1
    sp_load(c, sp, slab_number(e, 0), down(e % RING, CHUNKS - 1))


def pool_load_post_gain(c, pool, st):
    if st.post is not None:
        if st.updates:
            pool.wait_ge(c.sem("h_updated"), st.updates)
        pool.dma_start(c.post_gain[:], st.post.partition_broadcast(P)).then_inc(c.sem("post_gain_loaded"), 16)


def pe_ffn(c, pe, st):
    b, f0 = st.slab, st.ffn * CHUNKS
    tensor = c.nc.tensor

    def gate_up(s, half, chunk, first_norm=None):
        n, r, _ = s
        pe.wait_ge(c.sem("w_lo_split"), n + 1)
        for k4 in range(KD // 2):
            k = half * (KD // 2) + k4
            if first_norm is not None:
                pe.wait_ge(c.sem("xT_lo_ready"), KD * first_norm + k + 1)
            for t in range(TOKS):
                tok, w = slice(t * P, (t + 1) * P), slice(k4 * 512, (k4 + 1) * 512)
                last = pe_matmul3(c, c.bank[GU + t][:], c.xT_hi[:, k, tok], c.xT_lo[:, k, tok],
                                  c.w_hi[r][:, w], c.w_lo[r][:, w], k == 0, k == KD - 1)
        last.then_inc(c.sem("slab_used"), 1)

    def transpose_hidden(chunk):
        pe.wait_ge(c.sem("hidden_ready"), 2 * chunk + 2)
        for q in range(FCOLS // P):
            for t in range(TOKS):
                last = tensor.transpose(c.bank[HT][:, q * SEQ + t * P:q * SEQ + (t + 1) * P],
                                        c.hid[:, t, q * P:(q + 1) * P], c.ident[:])
        last.then_inc(c.sem("hidden_transposed"), 1)

    def down(s, chunk, start, stop):
        n, r, _ = s
        pe.wait_ge(c.sem("w_lo_split"), n + 1)
        pe.wait_ge(c.sem("hiddenT_lo_ready"), chunk + 1)
        for q in range(FCOLS // P):
            for t in range(TOKS):
                for m in range(2):
                    tok, w = slice(t * P, (t + 1) * P), slice(q * 1024 + m * 512, q * 1024 + (m + 1) * 512)
                    last = pe_matmul3(c, c.bank[ACC + 2 * t + m][:], c.hidT_hi[:, q, tok], c.hidT_lo[:, q, tok],
                                      c.w_hi[r][:, w], c.w_lo[r][:, w], start and q == 0, stop and q == FCOLS // P - 1)
        last.then_inc(c.sem("slab_used"), 1)

    gate_up(slab_number(b, 0), 0, f0, st.norm)
    gate_up(slab_number(b + 1, 0), 1, f0, st.norm)

    def body(j, start):
        pe.wait_ge(c.sem("hidden_ready"), 2 * (f0 - 1 + j) + 2)
        gate_up(slab_number(b - 1, j), 0, f0 + j)
        transpose_hidden(f0 - 1 + j)
        gate_up(slab_number(b, j), 1, f0 + j)
        down(slab_number(b + 1, j), f0 - 1 + j, start, False)

    body(1, True)
    with tensor.Fori(2, CHUNKS) as j:
        body(j, False)
    transpose_hidden(f0 + CHUNKS - 1)
    e = b + 3 * CHUNKS - 1
    down(slab_number(e, 0), f0 + CHUNKS - 1, False, True)


def act_ffn(c, act, st):
    b, f0 = st.slab, st.ffn * CHUNKS

    def silu(s_used, chunk):
        act.wait_ge(c.sem("slab_used"), s_used)
        for t in range(TOKS):
            c.nc.scalar.activation(c.silu[:, t, :], c.bank[GU + t][:, 0:FCOLS], ACT.Silu
                                   ).then_inc(c.sem("silu_ready"), 1)

    def hidden_hi(chunk):
        act.wait_ge(c.sem("hidden_transposed"), chunk + 1)
        c.nc.scalar.activation(c.hidT_hi[:].rearrange("p q t -> p (q t)"), c.bank[HT][:], ACT.Copy
                               ).then_inc(c.sem("hiddenT_hi_ready"), 1)

    act_split(c, act, slab_number(b + 3, 0))
    silu(b + 2, f0)
    act_split(c, act, slab_number(b + 4, 0))

    def body(j):
        hidden_hi(f0 - 1 + j)
        act_split(c, act, slab_number(b + 2, j))
        silu(b + 3 * j + 2, f0 + j)
        act_split(c, act, slab_number(b + 3, j))
        act_split(c, act, slab_number(b + 4, j))

    with c.nc.scalar.Fori(1, CHUNKS - 1) as j:
        body(j)
    body(CHUNKS - 1)
    hidden_hi(f0 + CHUNKS - 1)
    act_residual(c, act, st)
    act_split(c, act, slab_number(b + 3 * CHUNKS + 2, 0))


def dve_ffn(c, dve, st):
    b, f0 = st.slab, st.ffn * CHUNKS
    vector = c.nc.vector

    def hidden(chunk):
        for t in range(TOKS):
            dve.wait_ge(c.sem("silu_ready"), 2 * chunk + t + 1)
            vector.tensor_tensor(c.hid[:, t, :], c.silu[:, t, :], c.bank[GU + t][:, FCOLS:2 * FCOLS], ALU.mult
                                 ).then_inc(c.sem("hidden_ready"), 1)

    def hidden_lo(chunk):
        dve.wait_ge(c.sem("hiddenT_hi_ready"), chunk + 1)
        vector.tensor_tensor(c.hidT_lo[:].rearrange("p q t -> p (q t)"), c.bank[HT][:],
                             c.hidT_hi[:].rearrange("p q t -> p (q t)").bitcast(F32), ALU.subtract
                             ).then_inc(c.sem("hiddenT_lo_ready"), 1)

    dve_split(c, dve, slab_number(b + 3, 0))
    hidden(f0)
    dve_split(c, dve, slab_number(b + 4, 0))

    def body(j):
        hidden_lo(f0 - 1 + j)
        dve_split(c, dve, slab_number(b + 2, j))
        hidden(f0 + j)
        dve_split(c, dve, slab_number(b + 3, j))
        dve_split(c, dve, slab_number(b + 4, j))

    with vector.Fori(1, CHUNKS - 1) as j:
        body(j)
    body(CHUNKS - 1)
    hidden_lo(f0 + CHUNKS - 1)
    dve_residual(c, dve, st)
    dve_split(c, dve, slab_number(b + 3 * CHUNKS + 2, 0))



def residual_sources(c, st):
    parts = [(t, m) for t in range(TOKS) for m in range(2)]
    if st.kind == "ffn":
        return [(t, m, c.bank[ACC + 2 * t + m][:]) for t, m in parts], "slab_used", st.slab + 3 * CHUNKS
    return [(t, m, c.mix_out[:, t, m * 512:(m + 1) * 512]) for t, m in parts], "projection_read", st.step_end


def act_residual(c, act, st):
    if st.post is None:
        return
    parts, done, count = residual_sources(c, st)
    act.wait_ge(c.sem(done), count)
    for t, m, src in parts:
        c.nc.scalar.activation(c.xn[:, t, m * 512:(m + 1) * 512], src, ACT.Square,
                               accum_out=c.ssq[:, 2 * t + m:2 * t + m + 1]).then_inc(c.sem("post_squares"), 1)
    act.wait_ge(c.sem("post_mean_square"), st.post_index + 1)
    c.nc.scalar.activation(c.rms[:], c.ms[:], ACT.Sqrt).then_inc(c.sem("post_rms"), 1)


def dve_residual(c, dve, st):
    parts, done, count = residual_sources(c, st)
    vector, factor = c.nc.vector, 0.5 if st.kind == "ffn" else 1.0
    if st.post is None:
        dve.wait_ge(c.sem(done), count)
        for t, m, src in parts:
            out = c.h[:, t, m * 512:(m + 1) * 512]
            last = vector.scalar_tensor_tensor(out, src, factor, out, ALU.mult, ALU.add)
    else:
        dve.wait_ge(c.sem("post_squares"), 4 * st.post_index + 4)
        c.chain(vector.tensor_tensor(c.ms[:], c.ssq[:, 0:4:2], c.ssq[:, 1:4:2], ALU.add))
        vector.tensor_scalar(c.ms[:], c.ms[:], 1.0 / D_MODEL, EPS, ALU.mult, ALU.add
                             ).then_inc(c.sem("post_mean_square"), 1)
        dve.wait_ge(c.sem("post_rms"), st.post_index + 1)
        c.chain(vector.reciprocal(c.rstd[:], c.rms[:]))
        dve.wait_ge(c.sem("post_gain_loaded"), 16 * st.post_index + 16)
        for t, m, src in parts:
            cols = slice(m * 512, (m + 1) * 512)
            c.chain(vector.scalar_tensor_tensor(c.xn[:, t, cols], src, c.rstd[:, t:t + 1],
                                                c.post_gain[:, cols], ALU.mult, ALU.mult))
            last = vector.scalar_tensor_tensor(c.h[:, t, cols], c.xn[:, t, cols], factor, c.h[:, t, cols],
                                               ALU.mult, ALU.add)
    last.then_inc(c.sem("h_updated"), 1)



class Projection:

    def __init__(self, w, col0, steps, form, width=PCOLS, kp=P, slabs=1, operand_cols=(0, SEQ)):
        self.w, self.col0, self.steps, self.form, self.width = w, col0, steps, form, width
        self.kp, self.slabs, self.cols = kp, slabs, operand_cols


def step_loop(engine, pr, one):
    peeled = 1 if pr.step < 3 or pr.slab < RING else 0
    looped = pr.steps // 3 if pr.steps >= 6 and pr.slabs == 1 else 0

    def straight(s):
        one(s, [slab_number(pr.slab + s * pr.slabs + q, 0) for q in range(pr.slabs)], (pr.step + s) % 3, pr.step + s)

    if looped > peeled:
        for s in range(3 * peeled):
            straight(s)
        with engine.Fori(peeled, looped) as i:
            for r in range(3):
                one(3 * i + r, [slab_number(pr.slab + r, i)], (pr.step + r) % 3, pr.step + r + 3 * i)
    for s in range(3 * looped if looped > peeled else 0, pr.steps):
        straight(s)


def sp_project(c, sp, pr):
    def one(s, slabs, bank, g):
        for q, slab in enumerate(slabs):
            n = KD // 2
            raw = c.raw[slab[1]][0:pr.kp, 0:KD * pr.width].rearrange("p (k n) -> p k n", k=KD)
            row = q * KD * pr.kp
            sp_load(c, sp, slab, [(raw[:, f * n:(f + 1) * n, :],
                                   pr.w[row + f * n * pr.kp:row + (f + 1) * n * pr.kp,
                                        bass.ds(pr.col0 + s * pr.width, pr.width)].rearrange("(k p) n -> p k n", p=pr.kp))
                                  for f in range(2)])
    step_loop(c.nc.sync, pr, one)


def pe_project(c, pe, pr):
    def one(s, slabs, bank, g):
        if not isinstance(g, int) or g >= 3:
            pe.wait_ge(c.sem("projection_read"), g - 2)
        for n, r, _ in slabs:
            pe.wait_ge(c.sem("w_lo_split"), n + 1)
        kt = KD * len(slabs)
        lo, hi = pr.cols
        tiles = TOKS if pr.form == "tok" else 2
        for tile in range(tiles):
            for k in range(kt):
                r = slabs[k // KD][1]
                base = (k % KD) * pr.width
                first, end = k == 0, k == kt - 1
                if pr.form == "tok":
                    x = slice(tile * P, (tile + 1) * P)
                    w = slice(base, base + pr.width)
                    out = c.bank[bank][:, tile * pr.width:(tile + 1) * pr.width]
                else:
                    x = slice(lo, hi)
                    w = slice(base + tile * pr.width // 2, base + (tile + 1) * pr.width // 2)
                    out = c.bank[bank][0:pr.width // 2, tile * (hi - lo):(tile + 1) * (hi - lo)]
                last = pe_matmul3(c, out, c.xT_hi[0:pr.kp, k, x], c.xT_lo[0:pr.kp, k, x],
                                  c.w_hi[r][0:pr.kp, w], c.w_lo[r][0:pr.kp, w], first, end, pr.form == "feat")
                if tile == tiles - 1 and k % KD == KD - 1:
                    last.then_inc(c.sem("slab_used"), 1)
    step_loop(c.nc.tensor, pr, one)


def act_project(c, act, pr):
    def one(s, slabs, bank, g):
        for n, r, before in slabs:
            act_split(c, act, (n + RING, r, before + 1))
    step_loop(c.nc.scalar, pr, one)


def dve_project(c, dve, pr, read):
    def one(s, slabs, bank, g):
        n, r, _ = slabs[-1]
        dve.wait_ge(c.sem("slab_used"), n + 1)
        if pr.form == "tok":
            view = c.bank[bank][:, 0:TOKS * pr.width].rearrange("p (t n) -> p t n", t=TOKS)
        else:
            view = c.bank[bank][0:pr.width // 2, 0:2 * (pr.cols[1] - pr.cols[0])].rearrange("p (t n) -> p t n", t=2)
        read(s, view).then_inc(c.sem("projection_read"), 1)
        for n, r, before in slabs:
            dve_split(c, dve, (n + RING, r, before + 1))
    step_loop(c.nc.vector, pr, one)


def dve_add_to_h(c, pr):
    def read(s, view):
        out = c.h[:, :, bass.ds(s * pr.width, pr.width)]
        return c.nc.vector.tensor_tensor(out, view, out, ALU.add)
    return read


def act_operand_hi(c, act, src, tiles, kp, name):
    c.nc.scalar.activation(c.xT_hi[0:kp, 0:tiles, :].rearrange("p k t -> p (k t)"), src, ACT.Copy
                           ).then_inc(c.sem(name), 1)


def dve_operand_lo(c, dve, src, tiles, kp, name):
    c.nc.vector.tensor_tensor(c.xT_lo[0:kp, 0:tiles, :].rearrange("p k t -> p (k t)"), src,
                              c.xT_hi[0:kp, 0:tiles, :].rearrange("p k t -> p (k t)").bitcast(F32), ALU.subtract
                              ).then_inc(c.sem(name), 1)



MASK_STEPS = 7
MASKED = -1e30

def pool_masks(c, pool):
    g = c.nc.gpsimd
    c.mask_sets = 0

    def step(ins):
        c.mask_sets += 1
        ins.then_inc(c.sem("masks_made"), 1)
        pool.wait_ge(c.sem("masks_made"), c.mask_sets)

    step(g.memset(c.ident[:], 0.0))
    step(g.affine_select(out=c.ident[:], in_=c.ident[:], compare_op=ALU.not_equal, fill=1.0, base=0,
                         pattern=[[-1, P]], channel_multiplier=1))
    step(g.memset(c.ones[:], 1.0))
    step(g.affine_select(out=c.upper[:], in_=c.ones[:], compare_op=ALU.is_ge, fill=0.0, base=0,
                         pattern=[[1, P]], channel_multiplier=-1))
    step(g.memset(c.causal[:], 0.0))
    for lo in (0, 2 * P):
        part = c.causal[:, lo:lo + P]
        step(g.affine_select(out=part, in_=part, compare_op=ALU.is_ge, fill=MASKED, base=0,
                             pattern=[[-1, P]], channel_multiplier=1))
    assert c.mask_sets == MASK_STEPS



def arena(c, off, *shape):
    n = 1
    for d in shape[1:]:
        n *= d
    assert off + n <= ARENA
    v = c.arena[0:shape[0], off:off + n]
    if len(shape) == 3:
        return v.rearrange("p (a b) -> p a b", a=shape[1])
    if len(shape) == 4:
        return v.rearrange("p (a b d) -> p a b d", a=shape[1], b=shape[2])
    return v


SC_TAPS = 3


def sc_views(c):
    class V:
        bcx = arena(c, 0, P, 3 * KD, SEQ)
        z = arena(c, 6144, P, KD, SEQ)
        y = arena(c, 8192, P, KD, SEQ)
        taps = arena(c, 10240, P, KD, SC_TAPS)
    return V


def pool_sc(c, pool, st):
    v = sc_views(c)
    pool.wait_ge(c.sem("h_updated"), st.updates)
    pool.dma_start(v.taps.rearrange("p a b -> p (a b)"), c.small["sc_taps"]).then_inc(c.sem("sc_taps_loaded"), 16)


def pe_sc(c, pe, st):
    w_in, w_out = st.projections
    pe.wait_ge(c.sem("xT_lo_ready"), KD * (st.norm + 1))
    pe_project(c, pe, w_in)
    pe.wait_ge(c.sem("sc_gated_lo"), 1)
    pe_project(c, pe, w_out)


def act_sc(c, act, st):
    v = sc_views(c)
    act_project(c, act, st.projections[0])
    act.wait_ge(c.sem("sc_gated"), 1)
    act_operand_hi(c, act, v.z.rearrange("p k t -> p (k t)"), KD, P, "sc_gated_hi")
    act_project(c, act, st.projections[1])


def dve_sc(c, dve, st):
    v, vector, chain = sc_views(c), c.nc.vector, c.chain
    w_in, w_out = st.projections
    dve_project(c, dve, w_in, lambda s, view: vector.tensor_copy(v.bcx[:, bass.ds(s * 2, 2), :], view))
    dve.wait_ge(c.sem("projection_read"), w_in.step + w_in.steps)
    chain(vector.tensor_tensor(v.z, v.bcx[:, KD:2 * KD, :], v.bcx[:, 2 * KD:3 * KD, :], ALU.mult))
    dve.wait_ge(c.sem("sc_taps_loaded"), 16)
    for k in range(KD):
        last = vector.tensor_scalar(v.y[:, k, :], v.z[:, k, :], v.taps[:, k, SC_TAPS - 1:SC_TAPS], None, ALU.mult)
    chain(last)
    for j in range(SC_TAPS - 2, -1, -1):
        back = SC_TAPS - 1 - j
        for k in range(KD):
            last = vector.scalar_tensor_tensor(v.y[:, k, back:], v.z[:, k, 0:SEQ - back], v.taps[:, k, j:j + 1],
                                               v.y[:, k, back:], ALU.mult, ALU.add)
        chain(last)
    vector.tensor_tensor(v.z, v.bcx[:, 0:KD, :], v.y, ALU.mult).then_inc(c.sem("sc_gated"), 1)
    dve.wait_ge(c.sem("sc_gated_hi"), 1)
    dve_operand_lo(c, dve, v.z.rearrange("p k t -> p (k t)"), KD, P, "sc_gated_lo")
    dve_project(c, dve, w_out, dve_add_to_h(c, w_out))
    dve.wait_ge(c.sem("projection_read"), w_out.step + w_out.steps)
    vector.tensor_copy(c.ms[:], c.ms[:]).then_inc(c.sem("h_updated"), 1)



LOG1P_TERMS = 7


def dve_softplus_begin(c, x, mag, ready):
    c.nc.vector.scalar_tensor_tensor(mag, x, -1.0, x, ALU.mult, ALU.max).then_inc(c.sem(ready), 1)


def act_softplus_exp(c, act, mag, e, ready, count, done):
    act.wait_ge(c.sem(ready), count)
    c.nc.scalar.activation(e, mag, ACT.Exp, scale=-1.0).then_inc(c.sem(done), 1)


def dve_softplus_end(c, dve, x, e, s, s2, q, out, done, count):
    v, chain = c.nc.vector, c.chain
    dve.wait_ge(c.sem(done), count)
    chain(v.tensor_scalar(s, e, 2.0, None, ALU.add))
    chain(v.reciprocal(s, s))
    chain(v.tensor_tensor(s, s, e, ALU.mult))
    chain(v.tensor_tensor(s2, s, s, ALU.mult))
    chain(v.tensor_scalar(q, s2, 1.0 / (2 * LOG1P_TERMS + 1), None, ALU.mult))
    for term in range(LOG1P_TERMS - 1, 0, -1):
        chain(v.scalar_tensor_tensor(q, q, 1.0 / (2 * term + 1), s2, ALU.add, ALU.mult))
    chain(v.scalar_tensor_tensor(q, q, 1.0, s, ALU.add, ALU.mult))
    chain(v.tensor_scalar(s, x, 0.0, None, ALU.max))
    chain(v.scalar_tensor_tensor(out, q, 2.0, s, ALU.mult, ALU.add))



D_RNN = 1344
LRU_BLOCKS = 16
LRU_W = D_RNN // LRU_BLOCKS
LRU_TAPS = 4
LRU_C = 8.0


def rg_views(c):
    small = c.silu[0:LRU_W, :, :].rearrange("p a b -> p (a b)")
    temp = c.hid[0:LRU_W, :, :].rearrange("p a b -> p (a b)")
    n = LRU_BLOCKS

    class V:
        gx = arena(c, 0, LRU_W, 2 * n, SEQ)
        gate = arena(c, 0, LRU_W, n, SEQ)
        rec = arena(c, 4096, LRU_W, n, SEQ)
        y = arena(c, 8192, LRU_W, n, SEQ)
        i = arena(c, 12288, LRU_W, n, SEQ)
        taps = small[:, 0:n * LRU_TAPS].rearrange("p (n j) -> p n j", n=n)
        conv_b, b_a, b_x, lam = (small[:, n * (LRU_TAPS + q):n * (LRU_TAPS + q + 1)] for q in range(4))
        packed = small[:, 0:n * (LRU_TAPS + 4)]
        w_a = c.mix_out[0:LRU_W, :, :].rearrange("p a b -> p (a b)")[:, 0:D_RNN]
        w_x = c.xn[0:LRU_W, :, :].rearrange("p a b -> p (a b)")[:, 0:D_RNN]
        neg, mag, e, s, s2, q, sp, minus_sp = (temp[:, n * j:n * (j + 1)] for j in range(8))
    return V


def pool_rg(c, pool, st):
    v = rg_views(c)
    pool.wait_ge(c.sem("h_updated"), st.updates)
    pool.dma_start(v.packed, c.small["rg_small"]).then_inc(c.sem("rg_small_loaded"), 16)
    pool.dma_start(v.w_a.rearrange("p (n d) -> p n d", n=LRU_BLOCKS), c.small["rg_w_a"].rearrange("n p d -> p n d")
                   ).then_inc(c.sem("rg_w_a_loaded"), 16)
    pool_load_post_gain(c, pool, st)
    pool.wait_ge(c.sem("xn_transposed"), 4 * (st.norm + 1))
    pool.dma_start(v.w_x.rearrange("p (n d) -> p n d", n=LRU_BLOCKS), c.small["rg_w_x"].rearrange("n p d -> p n d")
                   ).then_inc(c.sem("rg_w_x_loaded"), 16)


def pe_rg(c, pe, st):
    v = rg_views(c)
    pe.wait_ge(c.sem("xT_lo_ready"), KD * (st.norm + 1))
    pe_project(c, pe, st.projections[0])
    pe.wait_ge(c.sem("rg_convolved"), 1)
    pe.wait_ge(c.sem("rg_w_a_loaded"), 16)
    pe.wait_ge(c.sem("rg_w_x_loaded"), 16)
    for g in range(LRU_BLOCKS // 2):
        if g >= 2:
            pe.wait_ge(c.sem("rg_gates_read"), g - 1)
        for w, b in ((v.w_a, 4 + g % 2), (v.w_x, 6 + g % 2)):
            for n in (2 * g, 2 * g + 1):
                last = c.nc.tensor.matmul(c.bank[b][0:LRU_W, (n % 2) * SEQ:(n % 2 + 1) * SEQ],
                                          w[:, n * LRU_W:(n + 1) * LRU_W], v.y[:, n, :], start=True, stop=True)
        last.then_inc(c.sem("rg_gates"), 1)
    pe.wait_ge(c.sem("rg_operand_lo"), 1)
    pe_project(c, pe, st.projections[1])


def act_rg(c, act, st):
    v, scalar, n_all = rg_views(c), c.nc.scalar, LRU_BLOCKS
    w_in, w_out = st.projections
    act_softplus_exp(c, act, v.mag, v.e, "rg_lambda_mag", 1, "rg_lambda_exp")
    act_project(c, act, w_in)
    act.wait_ge(c.sem("projection_read"), w_in.step + w_in.steps)
    for n in range(n_all):
        last = scalar.activation(v.y[:, n, :], v.rec[:, n, :], ACT.Identity,
                                 scale=v.taps[:, n, LRU_TAPS - 1:LRU_TAPS], bias=v.conv_b[:, n:n + 1])
    last.then_inc(c.sem("rg_first_tap"), 1)
    scalar.activation(v.gate, v.gate, ACT.Gelu_apprx_tanh).then_inc(c.sem("rg_gelu"), 1)
    for g in range(n_all // 2):
        act.wait_ge(c.sem("rg_gates"), g + 1)
        for out, b, bias in ((v.rec, 4 + g % 2, v.b_a), (v.i, 6 + g % 2, v.b_x)):
            for n in (2 * g, 2 * g + 1):
                last = scalar.activation(out[:, n, :], c.bank[b][0:LRU_W, (n % 2) * SEQ:(n % 2 + 1) * SEQ],
                                         ACT.Sigmoid, bias=bias[:, n:n + 1])
        last.then_inc(c.sem("rg_gates_read"), 1)
    act.wait_ge(c.sem("rg_gated_input"), 1)
    for n in range(n_all):
        last = scalar.activation(v.y[:, n, :], v.rec[:, n, :], ACT.Tanh, scale=v.sp[:, n:n + 1])
    last.then_inc(c.sem("rg_tanh"), 1)
    act.wait_ge(c.sem("rg_tanh"), 1)
    for n in range(n_all):
        last = scalar.activation(v.rec[:, n, :], v.rec[:, n, :], ACT.Exp, scale=v.minus_sp[:, n:n + 1])
    last.then_inc(c.sem("rg_a"), 1)
    act.wait_ge(c.sem("rg_one_minus_a2"), 1)
    scalar.activation(v.y, v.y, ACT.Sqrt).then_inc(c.sem("rg_scale"), 1)
    act.wait_ge(c.sem("rg_operand"), 1)
    act_operand_hi(c, act, v.y.rearrange("p k t -> p (k t)"), n_all, LRU_W, "rg_operand_hi")
    act_project(c, act, w_out)
    act_residual(c, act, st)


def dve_rg(c, dve, st):
    v, vector, chain, n_all = rg_views(c), c.nc.vector, c.chain, LRU_BLOCKS
    w_in, w_out = st.projections
    dve.wait_ge(c.sem("rg_small_loaded"), 16)
    chain(vector.tensor_scalar(v.neg, v.lam, -1.0, None, ALU.mult))
    dve_softplus_begin(c, v.neg, v.mag, "rg_lambda_mag")
    dve_softplus_end(c, dve, v.neg, v.e, v.s, v.s2, v.q, v.sp, "rg_lambda_exp", 1)
    chain(vector.tensor_scalar(v.sp, v.sp, LRU_C, None, ALU.mult))
    chain(vector.tensor_scalar(v.minus_sp, v.sp, -1.0, None, ALU.mult))
    dve_project(c, dve, w_in, lambda s, view: vector.tensor_copy(v.gx[:, bass.ds(s * 2, 2), :], view))
    dve.wait_ge(c.sem("rg_first_tap"), 1)
    for j in range(LRU_TAPS - 2, -1, -1):
        back = LRU_TAPS - 1 - j
        for n in range(n_all):
            last = vector.scalar_tensor_tensor(v.y[:, n, back:], v.rec[:, n, 0:SEQ - back], v.taps[:, n, j:j + 1],
                                               v.y[:, n, back:], ALU.mult, ALU.add)
        chain(last)
    vector.tensor_copy(v.q, v.q).then_inc(c.sem("rg_convolved"), 1)
    dve.wait_ge(c.sem("rg_gates_read"), n_all // 2)
    vector.tensor_tensor(v.i, v.i, v.y, ALU.mult).then_inc(c.sem("rg_gated_input"), 1)
    dve.wait_ge(c.sem("rg_a"), 1)
    square = [c.bank[g][0:LRU_W, :].rearrange("p (n t) -> p n t", n=2) for g in range(n_all // 2)]
    for g in range(n_all // 2):
        last = vector.tensor_tensor(square[g], v.rec[:, 2 * g:2 * g + 2, :], v.rec[:, 2 * g:2 * g + 2, :], ALU.mult)
    chain(last)
    for g in range(n_all // 2):
        part = v.y[:, 2 * g:2 * g + 2, :]
        last = vector.scalar_tensor_tensor(part, square[g], 1.0, part, ALU.add, ALU.mult)
    last.then_inc(c.sem("rg_one_minus_a2"), 1)
    dve.wait_ge(c.sem("rg_scale"), 1)
    chain(vector.tensor_tensor(v.i, v.i, v.y, ALU.mult))
    for n in range(n_all):
        last = vector.tensor_tensor_scan(v.y[:, n, :], v.rec[:, n, :], v.i[:, n, :], 0.0, ALU.mult, ALU.add)
    chain(last)
    vector.tensor_tensor(v.y, v.y, v.gate, ALU.mult).then_inc(c.sem("rg_operand"), 1)
    dve.wait_ge(c.sem("rg_operand_hi"), 1)
    dve_operand_lo(c, dve, v.y.rearrange("p k t -> p (k t)"), n_all, LRU_W, "rg_operand_lo")
    dve_project(c, dve, w_out, lambda s, view: vector.tensor_copy(c.mix_out[:, :, bass.ds(s * w_out.width, w_out.width)], view))
    dve_residual(c, dve, st)



def pe_to_operand(c, pe, st, src, ready, count):
    m = st.operand
    pe.wait_ge(c.sem(ready), count)
    for g in range(KD // 2):
        for k in (2 * g, 2 * g + 1):
            for t in range(TOKS):
                last = c.nc.tensor.transpose(
                    c.bank[NORM_BANKS[g]][:, (k % 2) * SEQ + t * P:(k % 2) * SEQ + (t + 1) * P],
                    src[:, t, k * P:(k + 1) * P], c.ident[:])
        last.then_inc(c.sem("mix_transposed"), 1)


def act_to_operand(c, act, st):
    for g in range(KD // 2):
        act.wait_ge(c.sem("mix_transposed"), 4 * st.operand + g + 1)
        c.nc.scalar.activation(c.xT_hi[:, 2 * g:2 * g + 2, :].rearrange("p k t -> p (k t)"),
                               c.bank[NORM_BANKS[g]][:], ACT.Copy).then_inc(c.sem("mix_hi"), 1)


def dve_to_operand(c, dve, st):
    for g in range(KD // 2):
        dve.wait_ge(c.sem("mix_hi"), 4 * st.operand + g + 1)
        c.nc.vector.tensor_tensor(c.xT_lo[:, 2 * g:2 * g + 2, :].rearrange("p k t -> p (k t)"),
                                  c.bank[NORM_BANKS[g]][:],
                                  c.xT_hi[:, 2 * g:2 * g + 2, :].rearrange("p k t -> p (k t)").bitcast(F32),
                                  ALU.subtract).then_inc(c.sem("mix_lo"), 1)



HEADS = 16
HEAD_DIM = D_MODEL // HEADS
KEYS = P + 2 * P
S_BANK, PT_BANK, O_BANK = (4, 5), (6, 7), (2, 3)


class Heads:

    def __init__(self, c, off):
        self.s = [arena(c, off + KEYS * b, P, KEYS) for b in range(2)]
        self.p = [arena(c, off + KEYS * (2 + b), P, KEYS) for b in range(2)]
        self.pT = [arena(c, off + KEYS * (4 + b), P, KEYS) for b in range(2)]
        off += 6 * KEYS
        self.neg_max = arena(c, off, P, HEADS, TOKS)
        self.sum = arena(c, off + 32, P, HEADS, TOKS)
        self.coef = arena(c, off + 64, P, HEADS, TOKS)


def pe_heads(c, pe, a, first):
    tensor = c.nc.tensor

    def scores(h):
        g = first + h
        if g >= 2:
            pe.wait_ge(c.sem("scores_read"), g - 1)
        bank, q, k = c.bank[S_BANK[h % 2]], a.qT(h), a.kT(h)
        decay = a.minus_cT is not None
        for lo, n, t in ((0, P, 0), (P, 2 * P, 1)):
            last = tensor.matmul(bank[:, lo:lo + n], q[:, t * P:(t + 1) * P], k[:, 0:n], start=True, stop=not decay)
            if decay:
                last = tensor.matmul(bank[:, lo:lo + n], c.ident[0:HEADS, h:h + 1].broadcast_to([HEADS, P]), a.minus_cT[:, 0:n], start=False, stop=True)
        last.then_inc(c.sem("scores_done"), 1)

    def weighted(h):
        g, b = first + h, h % 2
        pe.wait_ge(c.sem("probs_ready"), g + 1)
        if g >= 2:
            pe.wait_ge(c.sem("probsT_ready"), g - 1)
        for j in range(3):
            last = tensor.transpose(c.bank[PT_BANK[b]][:, j * P:(j + 1) * P], a.w.p[b][:, j * P:(j + 1) * P], c.ident[:])
        last.then_inc(c.sem("probs_transposed"), 1)
        pe.wait_ge(c.sem("probsT_ready"), g + 1)
        if g >= 2:
            pe.wait_ge(c.sem("head_out_read"), g - 1)
        out, pT = c.bank[O_BANK[b]], a.w.pT[b]
        tensor.matmul(out[:, 0:HEAD_DIM], pT[:, 0:P], a.value(0, h), start=True, stop=True)
        tensor.matmul(out[:, HEAD_DIM:2 * HEAD_DIM], pT[:, P:2 * P], a.value(0, h), start=True, stop=False)
        tensor.matmul(out[:, HEAD_DIM:2 * HEAD_DIM], pT[:, 2 * P:3 * P], a.value(1, h), start=False, stop=True
                      ).then_inc(c.sem("head_out"), 1)

    scores(0)
    for h in range(HEADS):
        if h + 1 < HEADS:
            scores(h + 1)
        weighted(h)


def act_heads(c, act, a, first):
    def exps(h):
        g, b = first + h, h % 2
        act.wait_ge(c.sem("scores_read"), g + 1)
        if g >= 2:
            act.wait_ge(c.sem("probs_transposed"), g - 1)
        for t, lo, n in ((0, 0, P), (1, P, 2 * P)):
            last = c.nc.scalar.activation(a.w.p[b][:, lo:lo + n], a.w.s[b][:, lo:lo + n], ACT.Exp,
                                          bias=a.w.neg_max[:, h, t:t + 1], accum_out=a.w.sum[:, h, t:t + 1])
        last.then_inc(c.sem("probs_ready"), 1)

    exps(0)
    for h in range(HEADS):
        if h + 1 < HEADS:
            exps(h + 1)
        g, b = first + h, h % 2
        act.wait_ge(c.sem("probs_transposed"), g + 1)
        if g >= 2:
            act.wait_ge(c.sem("head_out"), g - 1)
        c.nc.scalar.activation(a.w.pT[b], c.bank[PT_BANK[b]][:, 0:KEYS], ACT.Copy).then_inc(c.sem("probsT_ready"), 1)


def dve_heads(c, dve, a, first):
    vector, chain = c.nc.vector, c.chain

    def masked(h):
        g, b = first + h, h % 2
        dve.wait_ge(c.sem("scores_done"), g + 1)
        if g >= 2:
            dve.wait_ge(c.sem("probs_ready"), g - 1)
        for t, lo, n in ((0, 0, P), (1, P, 2 * P)):
            add = a.c_q[:, t, h:h + 1] if a.c_q is not None else 0.0
            last = vector.scalar_tensor_tensor(a.w.s[b][:, lo:lo + n], c.bank[S_BANK[b]][:, lo:lo + n], add,
                                               c.causal[:, lo:lo + n], ALU.add, ALU.add)
        chain(last)
        for t, lo, n in ((0, 0, P), (1, P, 2 * P)):
            last = vector.tensor_reduce(a.w.neg_max[:, h, t:t + 1], a.w.s[b][:, lo:lo + n], AX, ALU.max, negate=True)
        last.then_inc(c.sem("scores_read"), 1)

    def out(h):
        g, b = first + h, h % 2
        dve.wait_ge(c.sem("head_out"), g + 1)
        chain(vector.reciprocal(a.w.coef[:, h, :], a.w.sum[:, h, :]))
        if a.gate is not None:
            chain(vector.tensor_tensor(a.w.coef[:, h, :], a.w.coef[:, h, :], a.gate(h), ALU.mult))
        for t in range(TOKS):
            src, dst = c.bank[O_BANK[b]][:, t * HEAD_DIM:(t + 1) * HEAD_DIM], a.out(t, h)
            if a.adds:
                last = vector.scalar_tensor_tensor(dst, src, a.w.coef[:, h, t:t + 1], dst, ALU.mult, ALU.add)
            else:
                last = vector.tensor_scalar(dst, src, a.w.coef[:, h, t:t + 1], None, ALU.mult)
        last.then_inc(c.sem("head_out_read"), 1)

    masked(0)
    for h in range(HEADS):
        if h + 1 < HEADS:
            masked(h + 1)
        out(h)



def fa_views(c):
    class V:
        kT = arena(c, 0, P, KD, SEQ)
        v = arena(c, 2048, P, TOKS, D_MODEL)
        qT = arena(c, 4096, P, KD, SEQ)
        o = arena(c, 6144, P, TOKS, D_MODEL)
        b_f = arena(c, 10240, P, HEADS)
        minus_f, mag, e, s, s2, q, minus_lf, c_q = (arena(c, 10256 + 32 * j, P, TOKS, HEADS) for j in range(8))
        minus_cT = arena(c, 10512, HEADS, SEQ)
        heads = Heads(c, 10768)
    return V


def pool_kv(c, pool, st):
    pool.wait_ge(c.sem("h_updated"), st.updates)
    pool.dma_start(fa_views(c).b_f, c.small["b_fgate"].partition_broadcast(P)).then_inc(c.sem("b_f_loaded"), 16)


def pe_kv(c, pe, st):
    v, tensor = fa_views(c), c.nc.tensor
    pe.wait_ge(c.sem("xT_lo_ready"), KD * (st.norm + 1))
    for pr in st.projections:
        pe_project(c, pe, pr)
    pe.wait_ge(c.sem("log_f_ready"), 1)
    out = c.bank[7]
    tensor.matmul(out[:, 0:HEADS], c.upper[:], v.minus_lf[:, 0, :], start=True, stop=True)
    tensor.matmul(out[:, HEADS:2 * HEADS], c.ones[:], v.minus_lf[:, 0, :], start=True, stop=False)
    tensor.matmul(out[:, HEADS:2 * HEADS], c.upper[:], v.minus_lf[:, 1, :], start=False, stop=True
                  ).then_inc(c.sem("log_f_summed"), 1)
    pe.wait_ge(c.sem("minus_c_ready"), 1)
    for t in range(TOKS):
        last = tensor.transpose(c.bank[6][0:HEADS, t * P:(t + 1) * P], v.minus_lf[:, t, :], c.ident[:])
    last.then_inc(c.sem("minus_c_transposed"), 1)


def act_kv(c, act, st):
    v = fa_views(c)
    for pr in st.projections:
        act_project(c, act, pr)
    act_softplus_exp(c, act, v.mag, v.e, "f_mag", 1, "f_exp")


def dve_kv(c, dve, st):
    v, vector, chain = fa_views(c), c.nc.vector, c.chain
    k, val, f = st.projections
    dve_project(c, dve, k, lambda s, view: vector.tensor_copy(v.kT[:, bass.ds(s * 2, 2), :], view))
    dve_project(c, dve, val, lambda s, view: vector.tensor_copy(v.v[:, :, bass.ds(s * PCOLS, PCOLS)], view))
    dve.wait_ge(c.sem("b_f_loaded"), 16)
    dve_project(c, dve, f, lambda s, view: vector.tensor_tensor(
        v.minus_f, view, v.b_f.unsqueeze(1).broadcast_to([P, TOKS, HEADS]), ALU.add))
    dve.wait_ge(c.sem("projection_read"), f.step + 1)
    chain(vector.tensor_scalar(v.minus_f, v.minus_f, -1.0, None, ALU.mult))
    dve_softplus_begin(c, v.minus_f, v.mag, "f_mag")
    dve_softplus_end(c, dve, v.minus_f, v.e, v.s, v.s2, v.q, v.minus_lf, "f_exp", 1)
    vector.tensor_copy(v.q, v.q).then_inc(c.sem("log_f_ready"), 1)
    dve.wait_ge(c.sem("log_f_summed"), 1)
    minus_c = c.bank[7][:, 0:TOKS * HEADS].rearrange("p (t h) -> p t h", t=TOKS)
    vector.tensor_scalar(v.c_q, minus_c, -1.0, None, ALU.mult)
    vector.tensor_copy(v.minus_lf, minus_c).then_inc(c.sem("minus_c_ready"), 1)
    dve.wait_ge(c.sem("minus_c_transposed"), 1)
    chain(vector.tensor_copy(v.minus_cT, c.bank[6][0:HEADS, 0:SEQ]))


def fa_heads(c):
    f = fa_views(c)

    class A:
        w, minus_cT, c_q, gate, adds = f.heads, f.minus_cT, f.c_q, None, False

        @staticmethod
        def qT(h):
            return f.qT[h % 2 * HEAD_DIM:(h % 2 + 1) * HEAD_DIM, h // 2, :]

        @staticmethod
        def kT(h):
            return f.kT[h % 2 * HEAD_DIM:(h % 2 + 1) * HEAD_DIM, h // 2, :]

        @staticmethod
        def value(t, h):
            return f.v[:, t, h * HEAD_DIM:(h + 1) * HEAD_DIM]

        @staticmethod
        def out(t, h):
            return f.o[:, t, h * HEAD_DIM:(h + 1) * HEAD_DIM]
    return A


def pe_fa(c, pe, st):
    v = fa_views(c)
    pe.wait_ge(c.sem("xT_lo_ready"), KD * (st.norm + 1))
    pe_project(c, pe, st.projections[0])
    pe.wait_ge(c.sem("projection_read"), st.projections[1].step)
    pe_heads(c, pe, fa_heads(c), st.heads)
    pe_to_operand(c, pe, st, v.o, "head_out_read", st.heads + HEADS)
    pe.wait_ge(c.sem("mix_lo"), 4 * (st.operand + 1))
    pe_project(c, pe, st.projections[1])


def act_fa(c, act, st):
    act_project(c, act, st.projections[0])
    act_heads(c, act, fa_heads(c), st.heads)
    act_to_operand(c, act, st)
    act_project(c, act, st.projections[1])
    act_residual(c, act, st)


def dve_fa(c, dve, st):
    v, vector = fa_views(c), c.nc.vector
    w_q, w_o = st.projections
    dve_project(c, dve, w_q, lambda s, view: vector.tensor_scalar(v.qT[:, bass.ds(s * 2, 2), :], view,
                                                                  HEAD_DIM ** -0.5, None, ALU.mult))
    dve_heads(c, dve, fa_heads(c), st.heads)
    dve_to_operand(c, dve, st)
    dve_project(c, dve, w_o, lambda s, view: vector.tensor_copy(c.mix_out[:, :, bass.ds(s * PCOLS, PCOLS)], view))
    dve_residual(c, dve, st)



G_HEADS = 8
G_DIM = 128
G_CHUNK = 64
G_TAPS = 4
LEVELS = (1, 2, 4, 8, 16, 32)


def gdn_views(c):
    used = [12288]

    def small(parts, *free):
        n = 1
        for d in free:
            n *= d
        used[0] += n
        assert used[0] <= 13312
        return arena(c, used[0] - n, parts, *free)

    def tile(n):
        return arena(c, n * 1024 if n < 6 else 13312 + (n - 6) * 1024, P, G_HEADS, P)

    masks = c.post_gain[:, :].rearrange("p (m i) -> p m i", m=8)

    class V:
        raw = arena(c, 0, P, 24, SEQ)
        cv = arena(c, 6144, P, 24, SEQ)
        sq = arena(c, 0, P, 16, SEQ)
        kbe, kd, vb, X, Y, AT, attnT, T, decay = (tile(n) for n in range(9))
        u, wT = X, AT
        state = c.xn[:, 0, :].rearrange("p (h d) -> p h d", h=G_HEADS)
        o = c.xn[:, 1, :].rearrange("p (h d) -> p h d", h=G_HEADS)
        gate = c.mix_out
        pair = [masks[:, m, :] for m in range(6)]
        lower, upper = masks[:, 6, :], masks[:, 7, :]
        ab = small(P, TOKS, 2 * G_HEADS)
        beta = small(P, TOKS, G_HEADS)
        x, mag, e, s, s2, q, g = (small(P, TOKS, G_HEADS) for _ in range(7))
        qk_r = small(P, TOKS, 16)
        qk_rT = small(16, SEQ)
        log_decay, eg, kds, beg = (small(P, G_HEADS) for _ in range(4))
        gcT = small(G_HEADS, P)
        elast = small(P, G_HEADS, 2)
        a_log, dt = small(P, G_HEADS), small(P, G_HEADS)
        out_norm = small(P, G_DIM)
        taps = small(P, 24, G_TAPS)
        o_r = small(P, G_HEADS)
    return V


def flat(ap):
    return ap.rearrange("p a b -> p (a b)")


def over(ap, n):
    return ap.unsqueeze(2).broadcast_to([ap.shape[0], ap.shape[1], n])


def per_head(ap, heads=G_HEADS):
    return ap.unsqueeze(1).broadcast_to([ap.shape[0], heads, ap.shape[1]])


def half_heads(ap, b):
    return ap[:, 4 * b:4 * b + 4, :]


def bank_heads(c, b):
    return c.bank[b][:].rearrange("p (h d) -> p h d", h=4)


def pool_gdn(c, pool, st):
    v, g, u = gdn_views(c), c.nc.gpsimd, st.turn
    pool.wait_ge(c.sem("h_updated"), st.updates)
    for dst, src in ((flat(v.taps), c.small["gdn_taps"][u]), (v.a_log, c.small["gdn_A_log"][u].partition_broadcast(P)),
                     (v.dt, c.small["gdn_dt_bias"][u].partition_broadcast(P)),
                     (v.out_norm, c.small["gdn_out_norm"][u].partition_broadcast(P))):
        pool.dma_start(dst, src).then_inc(c.sem("gdn_small_loaded"), 16)
    if u:
        return
    made = [0]

    def step(ins):
        made[0] += 1
        ins.then_inc(c.sem("gdn_masks"), 1)
        pool.wait_ge(c.sem("gdn_masks"), made[0])

    def blocks(out, b):
        view = out.rearrange("p (a r) -> p a r", r=b)
        step(g.memset(out, 1.0))
        step(g.affine_select(out=view, in_=view, compare_op=ALU.is_ge, fill=0.0, base=0,
                             pattern=[[-b, P // b], [0, b]], channel_multiplier=1))
        step(g.affine_select(out=view, in_=view, compare_op=ALU.is_ge, fill=0.0, base=b - 1,
                             pattern=[[b, P // b], [0, b]], channel_multiplier=-1))

    for m, b in enumerate(LEVELS):
        blocks(v.pair[m], b)
    blocks(v.lower, G_CHUNK)
    step(g.affine_select(out=v.upper, in_=v.lower, compare_op=ALU.is_ge, fill=0.0, base=0,
                         pattern=[[1, P]], channel_multiplier=-1))
    for m in range(len(LEVELS) - 1):
        step(g.tensor_tensor(out=v.pair[m], in0=v.pair[m + 1], in1=v.pair[m], op=ALU.subtract))
    step(g.tensor_tensor(out=v.pair[5], in0=v.lower, in1=v.pair[5], op=ALU.subtract))
    step(g.affine_select(out=v.lower, in_=v.lower, compare_op=ALU.is_ge, fill=0.0, base=0,
                         pattern=[[-1, P]], channel_multiplier=1))
    assert made[0] == GDN_MASK_STEPS


GDN_MASK_STEPS = 3 * 7 + 1 + 5 + 1 + 1


def pe_gdn(c, pe, st):
    v, tensor, u = gdn_views(c), c.nc.tensor, st.turn
    heads = range(G_HEADS)
    mm, tr = tensor.matmul, tensor.transpose
    pe.wait_ge(c.sem("xT_lo_ready"), KD * (st.norm + 1))
    for pr in st.projections[0:3]:
        pe_project(c, pe, pr)
    pe.wait_ge(c.sem("gdn_squares"), u + 1)
    for t in range(TOKS):
        for n in range(16):
            last = mm(c.bank[3][:, t * 16 + n:t * 16 + n + 1], v.sq[:, n, t * P:(t + 1) * P], c.ones[:, 0:1],
                      start=True, stop=True)
    last.then_inc(c.sem("gdn_norms"), 1)
    pe.wait_ge(c.sem("gdn_qk_r"), u + 1)
    for t in range(TOKS):
        last = tr(c.bank[3][0:16, t * P:(t + 1) * P], v.qk_r[:, t, :], c.ident[:])
    last.then_inc(c.sem("gdn_qk_r_transposed"), 1)
    pe.wait_ge(c.sem("gdn_qk_rT"), u + 1)
    for p in range(8):
        if p >= 4:
            pe.wait_ge(c.sem("gdn_scaled"), 8 * u + p - 3)
        for n in (2 * p, 2 * p + 1):
            last = mm(c.bank[4 + p % 4][:, (n % 2) * SEQ:(n % 2 + 1) * SEQ],
                      c.ident[0:16, n:n + 1].broadcast_to([16, P]), v.qk_rT, start=True, stop=True)
        last.then_inc(c.sem("gdn_factors"), 1)
    if u == 0:
        pe.wait_ge(c.sem("gdn_masks"), GDN_MASK_STEPS)
    pe.wait_ge(c.sem("gdn_scaled"), 8 * u + 8)
    pe.wait_ge(c.sem("gdn_g_ready"), u + 1)
    for t in range(TOKS):
        z, tok = TOKS * u + t, slice(t * P, (t + 1) * P)
        if z:
            pe.wait_ge(c.sem("gdn_out"), z)
        mm(c.bank[3][:, 0:G_HEADS], v.upper, v.g[:, t, :], start=True, stop=True)
        mm(c.bank[3][:, G_HEADS:2 * G_HEADS], v.lower, v.g[:, t, :], start=True, stop=True
           ).then_inc(c.sem("gdn_gc"), 1)
        for h in heads:
            tr(c.bank[4 + h // 4][:, (h % 4) * P:(h % 4 + 1) * P], v.cv[:, 8 + h, tok], c.ident[:])
        for h in heads:
            last = tr(c.bank[6 + h // 4][:, (h % 4) * P:(h % 4 + 1) * P], v.cv[:, 16 + h, tok], c.ident[:])
        last.then_inc(c.sem("gdn_kv_transposed"), 1)
        pe.wait_ge(c.sem("gdn_gc_sums"), z + 1)
        tr(c.bank[3][0:G_HEADS, 0:P], v.log_decay, c.ident[:]).then_inc(c.sem("gdn_gc_transposed"), 1)
        pe.wait_ge(c.sem("gdn_gcT"), z + 1)
        for h in heads:
            last = mm(c.bank[h // 4][:, (h % 4) * P:(h % 4 + 1) * P],
                      c.ident[0:G_HEADS, h:h + 1].broadcast_to([G_HEADS, P]), v.gcT, start=True, stop=True)
        last.then_inc(c.sem("gdn_gc_spread"), 1)
        pe.wait_ge(c.sem("gdn_kv_read"), z + 1)
        for h in heads:
            mm(c.bank[4 + h // 4][:, (h % 4) * P:(h % 4 + 1) * P], v.cv[:, 8 + h, tok], v.cv[:, 8 + h, tok],
               start=True, stop=True)
        for h in heads:
            last = mm(c.bank[6 + h // 4][:, (h % 4) * P:(h % 4 + 1) * P], v.cv[:, h, tok], v.cv[:, 8 + h, tok],
                      start=True, stop=True)
        last.then_inc(c.sem("gdn_products"), 1)
        pe.wait_ge(c.sem("gdn_masked"), z + 1)
        for h in heads:
            tr(c.bank[h // 4][:, (h % 4) * P:(h % 4 + 1) * P], v.T[:, h, :], c.ident[:])
        for h in heads:
            last = tr(c.bank[2 + h // 4][:, (h % 4) * P:(h % 4 + 1) * P], v.attnT[:, h, :], c.ident[:])
        last.then_inc(c.sem("gdn_transposed"), 1)
        for m in range(1, len(LEVELS)):
            w = 5 * z + m
            pe.wait_ge(c.sem("gdn_level_ready"), w)
            for h in heads:
                last = mm(c.bank[h // 4][:, (h % 4) * P:(h % 4 + 1) * P], v.decay[:, h, :], v.X[:, h, :],
                          start=True, stop=True)
            last.then_inc(c.sem("gdn_ax"), 1)
            pe.wait_ge(c.sem("gdn_T_ready"), w)
            for h in heads:
                last = mm(c.bank[4 + h // 4][:, (h % 4) * P:(h % 4 + 1) * P], v.T[:, h, :], v.Y[:, h, :],
                          start=True, stop=True)
            last.then_inc(c.sem("gdn_yt"), 1)
            if m < len(LEVELS) - 1:
                for h in heads:
                    last = mm(c.bank[6 + h // 4][:, (h % 4) * P:(h % 4 + 1) * P], v.Y[:, h, :], v.T[:, h, :],
                              start=True, stop=True)
                last.then_inc(c.sem("gdn_xt"), 1)
        pe.wait_ge(c.sem("gdn_inverse"), z + 1)
        for h in heads:
            mm(c.bank[h // 4][:, (h % 4) * P:(h % 4 + 1) * P], v.Y[:, h, :], v.vb[:, h, :], start=True, stop=True)
        for h in heads:
            last = mm(c.bank[2 + h // 4][:, (h % 4) * P:(h % 4 + 1) * P], v.kbe[:, h, :], v.Y[:, h, :],
                      start=True, stop=True)
        last.then_inc(c.sem("gdn_uw"), 1)
        for k in range(2):
            x, row = 2 * z + k, slice(G_CHUNK * k, G_CHUNK * (k + 1))
            ctok = slice(t * P + G_CHUNK * k, t * P + G_CHUNK * (k + 1))
            pe.wait_ge(c.sem("gdn_state"), x + 1)
            if k == 0:
                pe.wait_ge(c.sem("gdn_uw_read"), z + 1)
            for h in heads:
                last = mm(c.bank[h // 4][row, (h % 4) * P:(h % 4 + 1) * P], v.wT[:, h, row], v.state[:, h, :],
                          start=True, stop=True)
            last.then_inc(c.sem("gdn_ws"), 1)
            for h in heads:
                mm(c.bank[2 + h // 4][row, (h % 4) * P:(h % 4 + 1) * P], v.cv[:, h, ctok], v.state[:, h, :],
                   start=True, stop=True)
            pe.wait_ge(c.sem("gdn_v_new"), x + 1)
            for h in heads:
                last = mm(c.bank[6 + h // 4][:, (h % 4) * P:(h % 4 + 1) * P], v.kd[row, h, :], v.T[row, h, :],
                          start=True, stop=True)
            last.then_inc(c.sem("gdn_kv_new"), 1)
            for h in heads:
                last = mm(c.bank[4 + h // 4][row, (h % 4) * P:(h % 4 + 1) * P], v.attnT[row, h, row], v.T[row, h, :],
                          start=True, stop=True)
            if k == 1:
                last.then_inc(c.sem("gdn_o"), 1)
    pe_to_operand(c, pe, st, c.mix_out, "gdn_out", 2 * u + 2)
    pe.wait_ge(c.sem("mix_lo"), 4 * (st.operand + 1))
    pe_project(c, pe, st.projections[3])


def act_gdn(c, act, st):
    v, scalar, u = gdn_views(c), c.nc.scalar, st.turn
    qkv, gate, ab, w_out = st.projections
    for pr in (qkv, gate, ab):
        act_project(c, act, pr)
    act.wait_ge(c.sem("gdn_small_loaded"), 64 * (u + 1))
    act.wait_ge(c.sem("projection_read"), ab.step + 1)
    for n in range(24):
        last = scalar.activation(v.cv[:, n, :], v.raw[:, n, :], ACT.Copy, scale=v.taps[:, n, G_TAPS - 1:G_TAPS])
    last.then_inc(c.sem("gdn_first_tap"), 1)
    scalar.activation(v.a_log, v.a_log, ACT.Exp).then_inc(c.sem("gdn_exp_a"), 1)
    act_softplus_exp(c, act, v.mag, v.e, "gdn_mag", u + 1, "gdn_exp")
    scalar.activation(v.beta, v.ab[:, :, G_HEADS:2 * G_HEADS], ACT.Sigmoid).then_inc(c.sem("gdn_beta"), 1)
    scalar.activation(v.gate[:], v.gate[:], ACT.Silu).then_inc(c.sem("gdn_silu_gate"), 1)
    for part in range(3):
        act.wait_ge(c.sem("gdn_convolved"), 3 * u + part + 1)
        tiles = v.cv[:, 8 * part:8 * part + 8, :]
        scalar.activation(tiles, tiles, ACT.Silu).then_inc(c.sem("gdn_activated"), 1)
    act.wait_ge(c.sem("gdn_qk_ms"), u + 1)
    scalar.activation(v.qk_r, v.qk_r, ACT.Sqrt).then_inc(c.sem("gdn_qk_root"), 1)
    for t in range(TOKS):
        z = TOKS * u + t
        act.wait_ge(c.sem("gdn_gc_sums"), z + 1)
        scalar.activation(v.eg, v.log_decay, ACT.Exp).then_inc(c.sem("gdn_eg"), 1)
        scalar.activation(v.kds, v.kds, ACT.Exp).then_inc(c.sem("gdn_kds"), 1)
        act.wait_ge(c.sem("gdn_gc_transposed"), z + 1)
        scalar.activation(v.gcT, c.bank[3][0:G_HEADS, 0:P], ACT.Copy).then_inc(c.sem("gdn_gcT"), 1)
        act.wait_ge(c.sem("gdn_gc_spread"), z + 1)
        for b in range(2):
            last = scalar.activation(half_heads(v.elast, b), bank_heads(c, b)[:, :, G_CHUNK - 1::G_CHUNK], ACT.Exp)
        last.then_inc(c.sem("gdn_elast"), 1)
        act.wait_ge(c.sem("gdn_gaps"), z + 1)
        scalar.activation(flat(v.decay), flat(v.decay), ACT.Exp, scale=-1.0).then_inc(c.sem("gdn_decay"), 1)
        act.wait_ge(c.sem("gdn_transposed"), z + 1)
        for b in range(2):
            last = scalar.activation(half_heads(v.attnT, b), bank_heads(c, 2 + b), ACT.Copy)
        last.then_inc(c.sem("gdn_attnT"), 1)
        for m in range(1, len(LEVELS)):
            w = 5 * z + m
            act.wait_ge(c.sem("gdn_ax"), w)
            for b in range(2):
                last = scalar.activation(half_heads(v.T, b), bank_heads(c, b), ACT.Copy)
            last.then_inc(c.sem("gdn_T_ready"), 1)
        act.wait_ge(c.sem("gdn_uw"), z + 1)
        for b in range(2):
            last = scalar.activation(half_heads(v.wT, b), bank_heads(c, 2 + b), ACT.Copy)
        last.then_inc(c.sem("gdn_wT"), 1)
        act.wait_ge(c.sem("gdn_o_ms"), z + 1)
        scalar.activation(v.o_r, v.o_r, ACT.Sqrt).then_inc(c.sem("gdn_o_root"), 1)
    act_to_operand(c, act, st)
    act_project(c, act, w_out)


def dve_gdn(c, dve, st):
    v, vector, chain, u = gdn_views(c), c.nc.vector, c.chain, st.turn
    qkv, gate, ab, w_out = st.projections
    tt, tsc, stt = vector.tensor_tensor, vector.tensor_scalar, vector.scalar_tensor_tensor
    dve_project(c, dve, qkv, lambda s, view: vector.tensor_copy(v.raw[:, bass.ds(s * 2, 2), :], view))
    dve_project(c, dve, gate, lambda s, view: vector.tensor_copy(v.gate[:, :, bass.ds(s * PCOLS, PCOLS)], view))
    dve_project(c, dve, ab, lambda s, view: vector.tensor_copy(v.ab, view))
    dve.wait_ge(c.sem("projection_read"), ab.step + 1)
    dve.wait_ge(c.sem("gdn_small_loaded"), 64 * (u + 1))
    chain(tt(v.x, v.ab[:, :, 0:G_HEADS], per_head(v.dt, TOKS), ALU.add))
    dve_softplus_begin(c, v.x, v.mag, "gdn_mag")
    dve.wait_ge(c.sem("gdn_first_tap"), u + 1)
    for part in range(3):
        for j in range(G_TAPS - 2, -1, -1):
            back = G_TAPS - 1 - j
            for n in range(8 * part, 8 * part + 8):
                last = stt(v.cv[:, n, back:], v.raw[:, n, 0:SEQ - back], v.taps[:, n, j:j + 1], v.cv[:, n, back:],
                           ALU.mult, ALU.add)
            if j:
                chain(last)
        last.then_inc(c.sem("gdn_convolved"), 1)
    dve_softplus_end(c, dve, v.x, v.e, v.s, v.s2, v.q, v.g, "gdn_exp", u + 1)
    dve.wait_ge(c.sem("gdn_exp_a"), u + 1)
    stt(v.g, v.g, -1.0, per_head(v.a_log, TOKS), ALU.mult, ALU.mult).then_inc(c.sem("gdn_g_ready"), 1)
    dve.wait_ge(c.sem("gdn_activated"), 3 * u + 2)
    tt(v.sq, v.cv[:, 0:16, :], v.cv[:, 0:16, :], ALU.mult).then_inc(c.sem("gdn_squares"), 1)
    dve.wait_ge(c.sem("gdn_norms"), u + 1)
    tsc(v.qk_r, c.bank[3][:, 0:32].rearrange("p (t n) -> p t n", t=TOKS), EPS, None, ALU.add
        ).then_inc(c.sem("gdn_qk_ms"), 1)
    dve.wait_ge(c.sem("gdn_qk_root"), u + 1)
    chain(vector.reciprocal(v.qk_r, v.qk_r))
    tsc(v.qk_r[:, :, 0:G_HEADS], v.qk_r[:, :, 0:G_HEADS], G_DIM ** -0.5, None, ALU.mult).then_inc(c.sem("gdn_qk_r"), 1)
    dve.wait_ge(c.sem("gdn_qk_r_transposed"), u + 1)
    vector.tensor_copy(v.qk_rT, c.bank[3][0:16, 0:SEQ]).then_inc(c.sem("gdn_qk_rT"), 1)
    for p in range(8):
        dve.wait_ge(c.sem("gdn_factors"), 8 * u + p + 1)
        tiles = v.cv[:, 2 * p:2 * p + 2, :]
        tt(tiles, tiles, c.bank[4 + p % 4][:].rearrange("p (n t) -> p n t", n=2), ALU.mult
           ).then_inc(c.sem("gdn_scaled"), 1)
    dve.wait_ge(c.sem("gdn_activated"), 3 * u + 3)
    vector.memset(flat(v.state), 0.0).then_inc(c.sem("gdn_state"), 1)
    for t in range(TOKS):
        z = TOKS * u + t
        dve.wait_ge(c.sem("gdn_gc"), z + 1)
        vector.tensor_copy(v.log_decay, c.bank[3][:, 0:G_HEADS])
        tt(v.kds, c.bank[3][:, G_HEADS:2 * G_HEADS], v.g[:, t, :], ALU.subtract).then_inc(c.sem("gdn_gc_sums"), 1)
        dve.wait_ge(c.sem("gdn_eg"), z + 1)
        dve.wait_ge(c.sem("gdn_beta"), u + 1)
        chain(tt(v.beg, v.beta[:, t, :], v.eg, ALU.mult))
        dve.wait_ge(c.sem("gdn_kds"), z + 1)
        dve.wait_ge(c.sem("gdn_kv_transposed"), z + 1)
        for b in range(2):
            tt(half_heads(v.kbe, b), bank_heads(c, 4 + b), over(v.beg[:, 4 * b:4 * b + 4], P), ALU.mult)
            tt(half_heads(v.kd, b), bank_heads(c, 4 + b), over(v.kds[:, 4 * b:4 * b + 4], P), ALU.mult)
            last = tt(half_heads(v.vb, b), bank_heads(c, 6 + b), over(v.beta[:, t, 4 * b:4 * b + 4], P), ALU.mult)
        last.then_inc(c.sem("gdn_kv_read"), 1)
        dve.wait_ge(c.sem("gdn_elast"), z + 1)
        for h in range(G_HEADS):
            last = tsc(v.decay[:, h, :], c.bank[h // 4][:, (h % 4) * P:(h % 4 + 1) * P], v.log_decay[:, h:h + 1], 0.0,
                       ALU.subtract, ALU.max)
        last.then_inc(c.sem("gdn_gaps"), 1)
        dve.wait_ge(c.sem("gdn_decay"), z + 1)
        if z == 0:
            dve.wait_ge(c.sem("gdn_masks"), GDN_MASK_STEPS)
        chain(tt(v.decay, v.decay, per_head(v.lower), ALU.mult))
        dve.wait_ge(c.sem("gdn_products"), z + 1)
        for b in range(2):
            tt(half_heads(v.attnT, b), bank_heads(c, 6 + b), half_heads(v.decay, b), ALU.mult)
            last = tt(half_heads(v.T, b), bank_heads(c, 4 + b), half_heads(v.decay, b), ALU.mult)
        chain(last)
        tt(v.T, v.T, over(v.beta[:, t, :], P), ALU.mult).then_inc(c.sem("gdn_masked"), 1)
        dve.wait_ge(c.sem("gdn_masked"), z + 1)
        chain(tt(v.X, v.T, per_head(v.pair[0]), ALU.mult))
        last = stt(v.X, v.X, -1.0, per_head(c.ident[:]), ALU.mult, ALU.add)
        dve.wait_ge(c.sem("gdn_attnT"), z + 1)
        for b in range(2):
            last = vector.tensor_copy(half_heads(v.AT, b), bank_heads(c, b))
        chain(last)
        chain(tt(v.Y, v.AT, per_head(v.pair[0]), ALU.mult))
        chain(stt(v.Y, v.Y, -1.0, per_head(c.ident[:]), ALU.mult, ALU.add))
        for m in range(1, len(LEVELS)):
            w = 5 * z + m
            tt(v.decay, v.AT, per_head(v.pair[m]), ALU.mult).then_inc(c.sem("gdn_level_ready"), 1)
            dve.wait_ge(c.sem("gdn_yt"), w)
            if m < len(LEVELS) - 1:
                dve.wait_ge(c.sem("gdn_xt"), 4 * z + m)
            for b in range(2):
                last = tt(half_heads(v.Y, b), half_heads(v.Y, b), bank_heads(c, 4 + b), ALU.subtract)
            if m < len(LEVELS) - 1:
                for b in range(2):
                    last = tt(half_heads(v.X, b), half_heads(v.X, b), bank_heads(c, 6 + b), ALU.subtract)
                chain(last)
        last.then_inc(c.sem("gdn_inverse"), 1)
        dve.wait_ge(c.sem("gdn_wT"), z + 1)
        for b in range(2):
            last = vector.tensor_copy(half_heads(v.u, b), bank_heads(c, b))
        last.then_inc(c.sem("gdn_uw_read"), 1)
        dve.wait_ge(c.sem("gdn_uw_read"), z + 1)
        for k in range(2):
            x, row = 2 * z + k, slice(G_CHUNK * k, G_CHUNK * (k + 1))
            dve.wait_ge(c.sem("gdn_ws"), x + 1)
            for b in range(2):
                last = tt(half_heads(v.T, b)[row], half_heads(v.u, b)[row], bank_heads(c, b)[row], ALU.subtract)
            last.then_inc(c.sem("gdn_v_new"), 1)
            dve.wait_ge(c.sem("gdn_kv_new"), x + 1)
            chain(tt(v.state, v.state, over(v.elast[:, :, k], P), ALU.mult))
            for b in range(2):
                last = tt(half_heads(v.state, b), half_heads(v.state, b), bank_heads(c, 6 + b), ALU.add)
            if x % 4 < 3:
                last.then_inc(c.sem("gdn_state"), 1)
        dve.wait_ge(c.sem("gdn_o"), z + 1)
        for b in range(2):
            last = tt(half_heads(v.o, b), bank_heads(c, 2 + b), over(v.eg[:, 4 * b:4 * b + 4], P), ALU.mult)
        chain(last)
        for b in range(2):
            last = tt(half_heads(v.o, b), half_heads(v.o, b), bank_heads(c, 4 + b), ALU.add)
        chain(last)
        chain(tt(v.T, v.o, v.o, ALU.mult))
        chain(vector.tensor_reduce(v.o_r, v.T, AX, ALU.add))
        tsc(v.o_r, v.o_r, 1.0 / G_DIM, EPS, ALU.mult, ALU.add).then_inc(c.sem("gdn_o_ms"), 1)
        dve.wait_ge(c.sem("gdn_o_root"), z + 1)
        chain(vector.reciprocal(v.o_r, v.o_r))
        chain(tt(v.o, v.o, over(v.o_r, P), ALU.mult))
        chain(tt(v.o, v.o, per_head(v.out_norm), ALU.mult))
        dve.wait_ge(c.sem("gdn_silu_gate"), u + 1)
        gated = v.gate[:, t, :].rearrange("p (h d) -> p h d", h=G_HEADS)
        tt(gated, gated, v.o, ALU.mult).then_inc(c.sem("gdn_out"), 1)
    dve_to_operand(c, dve, st)
    dve_project(c, dve, w_out, dve_add_to_h(c, w_out))
    dve.wait_ge(c.sem("projection_read"), w_out.step + w_out.steps)
    vector.tensor_copy(c.ms[:], c.ms[:]).then_inc(c.sem("h_updated"), 1)



N_KV = 4
N_GROUP = HEADS // N_KV
CMP_BLOCK, CMP_STRIDE = 32, 16
N_CMP = SEQ // CMP_STRIDE - CMP_BLOCK // CMP_STRIDE + 1
CMP_TILES = CMP_BLOCK * HEAD_DIM // P
CMP_COLS = N_KV * N_CMP
PAD = 32
Q_COLS, KC, VC, KS, VS, KW, VW, GATES = 1024, 1024, 1280, 1536, 1792, 2048, 2304, 2560
NSA_IN = GATES + 3 * HEADS
PI = 3.141592653589793
ROUND = 12582912.0
TURN_A, TURN_B = 6.28125, 0.0019350051879882812
TURN_C = 2 * PI - TURN_A - TURN_B


def nsa_views(c):
    used = [15456]

    def small(parts, *free):
        n = 1
        for d in free:
            n *= d
        used[0] += n
        return arena(c, used[0] - n, parts, *free)

    silu, hid = flat(c.silu[:]), flat(c.hid[:])
    mix, xn = flat(c.mix_out[:]), flat(c.xn[:])

    class V:
        p = arena(c, 0, P, TOKS, NSA_IN)
        qr = arena(c, 5216, P, TOKS, D_MODEL)
        kT = [arena(c, 5216 + 1024 * j, P, N_KV, SEQ) for j in range(2)]
        qnT = arena(c, 7264, P, KD, SEQ)
        qrT = arena(c, 9312, P, KD, SEQ)
        dup = [arena(c, 11360 + 1024 * j, P, TOKS * N_KV, 2 * HEAD_DIM) for j in range(4)]
        heads = Heads(c, 11360)
        blk = mix.rearrange("p (k n) -> p k n", k=CMP_TILES)
        pc = mix[:, 0:1024].rearrange("p (a n) -> p a n", n=PAD)
        pcT = mix[:, 1024:2048].rearrange("p (a q) -> p a q", q=P)
        vcd = xn[:, 0:1024].rearrange("p (g n) -> p g n", g=N_KV)
        tmp = [xn[:, 1024 + 512 * j:1536 + 512 * j] for j in range(2)]
        w2 = small(P, 4, HEAD_DIM)
        hidT = [small(P, 2, CMP_COLS) for _ in range(2)]
        cos, sin = small(P, TOKS, 32), small(P, TOKS, 32)
        gates = small(P, TOKS, 3 * HEADS)
        b1 = small(P, 4)
        ms = silu[:, 0:48].rearrange("p (t n) -> p t n", t=TOKS)
        sc = hid[:, 0:480].rearrange("p (a n) -> p a n", n=N_CMP)
        q_norm, k_norm = silu[:, 64:128], silu[:, 128:320].rearrange("p (a n) -> p a n", a=3)
        b2 = silu[:, 320:448].rearrange("p (a n) -> p a n", a=2)
        pe = silu[:, 448:480].rearrange("p (a n) -> p a n", a=2)
        inv = silu[:, 480:512]
        ang, turns = (flat(c.hid[:])[:, 64 * j:64 * (j + 1)].rearrange("p (t n) -> p t n", t=TOKS) for j in (0, 1))
        posf = hid[:, 128:130]
        kcn = arena(c, 5728, N_CMP, N_KV, HEAD_DIM)
        kc2 = arena(c, 5216, N_CMP, N_KV, 2 * HEAD_DIM)
        kc_ms = hid[:, 500:504]
        small_0 = flat(small(P, 160, 1))
        cmax, csum = small_0[:, 0:32], small_0[:, 32:64]
        cmask = small_0[:, 64:64 + TOKS * N_CMP].rearrange("p (t n) -> p t n", t=TOKS)
        seen = small_0[:, 94:96]
        kcT = small_0[:, 96:96 + 64].rearrange("p (g n) -> p g n", g=N_KV)
        pos = c.nsa_pos[:]
    assert used[0] <= ARENA, used
    return V


def pool_nsa(c, pool, st):
    v, g = nsa_views(c), c.nc.gpsimd
    pool.wait_ge(c.sem("h_updated"), st.updates)
    s = c.small
    for dst, src in ((v.pos, s["positions"]), (v.inv, s["inv_freq"].partition_broadcast(P)),
                     (v.q_norm, s["nsa_q_norm"].partition_broadcast(P)),
                     (flat(v.k_norm), s["nsa_k_norm"].partition_broadcast(P)),
                     (flat(v.b2), s["nsa_b2"].partition_broadcast(P)), (flat(v.pe), s["nsa_pe"]),
                     (v.w2, s["nsa_w2"].rearrange("(a p) n -> p a n", p=P)), (v.b1, s["nsa_b1"])):
        pool.dma_start(dst, src).then_inc(c.sem("nsa_small_loaded"), 16)
    n = [0]

    def step(ins):
        n[0] += 1
        ins.then_inc(c.sem("nsa_masks"), 1)
        pool.wait_ge(c.sem("nsa_masks"), n[0])

    step(g.memset(v.small_0[:, 64:96], 0.0))
    for t in range(TOKS):
        part = v.cmask[:, t, :]
        step(g.affine_select(out=part, in_=part, compare_op=ALU.is_ge, fill=MASKED, base=P * t - CMP_BLOCK + 1,
                             pattern=[[-CMP_STRIDE, N_CMP]], channel_multiplier=1))
    step(g.memset(v.seen, 1.0))
    step(g.affine_select(out=v.seen, in_=v.seen, compare_op=ALU.is_ge, fill=0.0, base=1 - CMP_BLOCK,
                         pattern=[[P, TOKS]], channel_multiplier=1))
    assert n[0] == NSA_MASK_STEPS


NSA_MASK_STEPS = 5


def nsa_heads(c, branch):
    f = nsa_views(c)
    gates = f.gates.rearrange("p t (h i) -> p t h i", i=3)
    v0 = (VS, VW)[branch]

    class A:
        w, minus_cT, c_q, adds = f.heads, None, None, True

        @staticmethod
        def gate(h):
            return gates[:, :, h, branch + 1]

        @staticmethod
        def qT(h):
            return f.qrT[h % 2 * HEAD_DIM:(h % 2 + 1) * HEAD_DIM, h // 2, :]

        @staticmethod
        def kT(h):
            return f.kT[branch][h % 2 * HEAD_DIM:(h % 2 + 1) * HEAD_DIM, h // N_GROUP, :]

        @staticmethod
        def value(t, h):
            at = v0 + h // N_GROUP * HEAD_DIM
            return f.p[:, t, at:at + HEAD_DIM]

        @staticmethod
        def out(t, h):
            return f.p[:, t, h * HEAD_DIM:(h + 1) * HEAD_DIM]
    return A


NSA_BANKS = (4, 5, 6, 7)


def pe_nsa(c, pe, st):
    v, tensor = nsa_views(c), c.nc.tensor
    mm, tr = tensor.matmul, tensor.transpose
    w_in, w_gates, w1k, w1v, w_out = st.projections

    def transpose_wide(src):
        for k in range(KD):
            for t in range(TOKS):
                last = tr(c.bank[NSA_BANKS[k // 2]][:, (k % 2) * SEQ + t * P:(k % 2) * SEQ + (t + 1) * P],
                          src[:, t, k * P:(k + 1) * P], c.ident[:])
        return last

    def transpose_dup(src, banks):
        for h in range(N_KV):
            for t in range(TOKS):
                last = tr(c.bank[banks[h // 2]][:, (h % 2) * SEQ + t * P:(h % 2) * SEQ + (t + 1) * P],
                          src[:, t * N_KV + h, :], c.ident[:])
        return last

    pe.wait_ge(c.sem("xT_lo_ready"), KD * (st.norm + 1))
    pe_project(c, pe, w_in)
    pe_project(c, pe, w_gates)
    pe.wait_ge(c.sem("nsa_c_dup"), 1)
    transpose_dup(v.dup[0], NSA_BANKS[0:2])
    transpose_dup(v.dup[1], NSA_BANKS[2:4]).then_inc(c.sem("nsa_transposed"), 1)
    pe.wait_ge(c.sem("nsa_blk_lo"), 1)
    pe_project(c, pe, w1k)
    pe_project(c, pe, w1v)
    pe.wait_ge(c.sem("nsa_qn"), 1)
    transpose_wide(v.p).then_inc(c.sem("nsa_transposed"), 1)
    pe.wait_ge(c.sem("nsa_hidden"), 1)
    out = c.bank[3]
    for h in range(N_KV):
        for k in range(2):
            mm(out[0:N_CMP, h * HEAD_DIM:(h + 1) * HEAD_DIM], v.hidT[0][:, k, h * N_CMP:(h + 1) * N_CMP],
               v.w2[:, k, :], start=k == 0, stop=k == 1)
    for i in range(N_GROUP):
        for h in range(N_KV):
            for k in range(2):
                last = mm(out[PAD * i:PAD * i + N_CMP, 256 + h * HEAD_DIM:256 + (h + 1) * HEAD_DIM],
                          v.hidT[1][:, k, h * N_CMP:(h + 1) * N_CMP], v.w2[:, 2 + k, :], start=k == 0, stop=k == 1)
    last.then_inc(c.sem("nsa_compressed"), 1)
    pe.wait_ge(c.sem("nsa_kc_normed"), 1)
    for h in range(N_KV):
        last = tr(out[:, h * 16:h * 16 + N_CMP], v.kc2[:, h, :], c.ident[0:N_CMP, 0:N_CMP])
    last.then_inc(c.sem("nsa_kc_transposed"), 1)
    pe.wait_ge(c.sem("nsa_qr"), 1)
    pe.wait_ge(c.sem("nsa_brought"), 1)
    transpose_wide(v.qr).then_inc(c.sem("nsa_transposed"), 1)
    pe.wait_ge(c.sem("nsa_k_dup"), 1)
    pe.wait_ge(c.sem("nsa_brought"), 2)
    transpose_dup(v.dup[2], NSA_BANKS[0:2])
    transpose_dup(v.dup[3], NSA_BANKS[2:4]).then_inc(c.sem("nsa_transposed"), 1)
    pe.wait_ge(c.sem("nsa_kcT"), 1)
    pe.wait_ge(c.sem("nsa_brought"), 3)
    for t in range(TOKS):
        for h in range(HEADS):
            half = slice(h % 2 * HEAD_DIM, (h % 2 + 1) * HEAD_DIM)
            at = (t * HEADS + h) // 2 * 16
            last = mm(c.bank[4 + h % 2][:, at:at + N_CMP], v.qnT[half, h // 2, t * P:(t + 1) * P],
                      v.kcT[half, h // N_GROUP, 0:N_CMP], start=True, stop=True)
    last.then_inc(c.sem("nsa_c_scores"), 1)
    pe.wait_ge(c.sem("nsa_c_probs"), 1)
    for a in range(TOKS * N_KV):
        last = tr(c.bank[6 + a // N_KV][:, a % N_KV * P:(a % N_KV + 1) * P],
                  flat(v.pc)[:, a * P:(a + 1) * P], c.ident[:])
    last.then_inc(c.sem("nsa_c_probs_transposed"), 1)
    pe.wait_ge(c.sem("nsa_c_probsT"), 1)
    for a in range(TOKS * N_KV):
        last = mm(c.bank[2 + a // 2][:, a % 2 * 256:(a % 2 + 1) * 256], v.pcT[:, a, :], v.vcd[:, a % N_KV, :],
                  start=True, stop=True)
    last.then_inc(c.sem("nsa_c_out"), 1)
    pe.wait_ge(c.sem("nsa_c_added"), 1)
    pe_heads(c, pe, nsa_heads(c, 0), st.heads)
    pe_heads(c, pe, nsa_heads(c, 1), st.heads + HEADS)
    pe_to_operand(c, pe, st, v.p, "head_out_read", st.heads + 2 * HEADS)
    pe.wait_ge(c.sem("mix_lo"), 4 * (st.operand + 1))
    pe_project(c, pe, w_out)


def act_nsa(c, act, st):
    v, scalar = nsa_views(c), c.nc.scalar
    w_in, w_gates, w1k, w1v, w_out = st.projections
    act_project(c, act, w_in)
    act_project(c, act, w_gates)
    act.wait_ge(c.sem("nsa_angles"), 1)
    scalar.activation(v.sin, v.turns, ACT.Sin).then_inc(c.sem("nsa_sin_cos"), 1)
    scalar.activation(v.cos, v.ang, ACT.Sin).then_inc(c.sem("nsa_sin_cos"), 1)
    act.wait_ge(c.sem("nsa_blk"), 1)
    scalar.activation(c.xT_hi[:, 0:CMP_TILES, 0:2 * CMP_COLS], v.blk[:, :, 0:2 * CMP_COLS], ACT.Copy
                      ).then_inc(c.sem("nsa_blk_hi"), 1)
    act_project(c, act, w1k)
    act_project(c, act, w1v)
    act.wait_ge(c.sem("nsa_ms"), 1)
    scalar.activation(v.ms, v.ms, ACT.Sqrt).then_inc(c.sem("nsa_root"), 1)
    act.wait_ge(c.sem("projection_read"), w1v.step + 1)
    for i in range(2):
        for k in range(2):
            last = scalar.activation(v.hidT[i][:, k, :], v.hidT[i][:, k, :], ACT.Gelu_apprx_tanh,
                                     bias=v.b1[:, 2 * i + k:2 * i + k + 1])
    last.then_inc(c.sem("nsa_hidden"), 1)
    act.wait_ge(c.sem("nsa_gates_in"), 1)
    scalar.activation(v.gates, v.p[:, :, GATES:NSA_IN], ACT.Sigmoid).then_inc(c.sem("nsa_gates"), 1)

    def bring(dst, transposed, scale=1.0):
        act.wait_ge(c.sem("nsa_transposed"), transposed)
        for b in range(4):
            last = scalar.activation(dst(b), c.bank[NSA_BANKS[b]][:], ACT.Copy, scale=scale)
        last.then_inc(c.sem("nsa_brought"), 1)

    bring(lambda b: flat(v.qnT[:, 2 * b:2 * b + 2, :]), 2, HEAD_DIM ** -0.5)
    act.wait_ge(c.sem("nsa_ms"), 2)
    scalar.activation(v.kc_ms[0:N_CMP], v.kc_ms[0:N_CMP], ACT.Sqrt).then_inc(c.sem("nsa_root"), 1)
    bring(lambda b: flat(v.qrT[:, 2 * b:2 * b + 2, :]), 3, HEAD_DIM ** -0.5)
    bring(lambda b: flat(v.kT[b // 2][:, 2 * (b % 2):2 * (b % 2) + 2, :]), 4)
    act.wait_ge(c.sem("nsa_c_shifted"), 1)
    scalar.activation(v.sc, v.sc, ACT.Exp).then_inc(c.sem("nsa_c_exp"), 1)
    act.wait_ge(c.sem("nsa_c_probs_transposed"), 1)
    for t in range(TOKS):
        last = scalar.activation(flat(v.pcT[:, N_KV * t:N_KV * (t + 1), :]), c.bank[6 + t][:], ACT.Copy)
    last.then_inc(c.sem("nsa_c_probsT"), 1)
    act_heads(c, act, nsa_heads(c, 0), st.heads)
    act_heads(c, act, nsa_heads(c, 1), st.heads + HEADS)
    act_to_operand(c, act, st)
    act_project(c, act, w_out)


def dve_nsa(c, dve, st):
    v, vector, chain = nsa_views(c), c.nc.vector, c.chain
    w_in, w_gates, w1k, w1v, w_out = st.projections
    tt, tsc, stt, copy = vector.tensor_tensor, vector.tensor_scalar, vector.scalar_tensor_tensor, vector.tensor_copy
    dve_project(c, dve, w_in, lambda s, view: copy(v.p[:, :, bass.ds(s * PCOLS, PCOLS)], view))
    dve_project(c, dve, w_gates, lambda s, view: copy(v.p[:, :, GATES:NSA_IN], view))
    dve.wait_ge(c.sem("projection_read"), w_gates.step + 1)
    vector.memset(v.vcd, 0.0).then_inc(c.sem("nsa_gates_in"), 1)

    def by_head(lo, n, t=None):
        part = v.p[:, :, lo:lo + n * HEAD_DIM] if t is None else v.p[:, t, lo:lo + n * HEAD_DIM]
        return part.rearrange("p t (h d) -> p t h d" if t is None else "p (h d) -> p h d", d=HEAD_DIM)

    for j, lo in ((0, KC), (1, VC)):
        for t in range(TOKS):
            for r in range(2):
                last = copy(v.dup[j][:, t * N_KV:(t + 1) * N_KV, r * HEAD_DIM:(r + 1) * HEAD_DIM], by_head(lo, N_KV, t))
    last.then_inc(c.sem("nsa_c_dup"), 1)

    dve.wait_ge(c.sem("nsa_small_loaded"), 128)
    chain(copy(v.posf, v.pos))
    for t in range(TOKS):
        last = tsc(v.ang[:, t, :], v.inv, v.posf[:, t:t + 1], None, ALU.mult)
    chain(last)
    chain(tsc(v.turns, v.ang, 1.0 / (2 * PI), None, ALU.mult))
    chain(tsc(v.turns, v.turns, ROUND, None, ALU.add))
    chain(tsc(v.turns, v.turns, -ROUND, None, ALU.add))
    for part in (TURN_A, TURN_B, TURN_C):
        chain(stt(v.ang, v.turns, -part, v.ang, ALU.mult, ALU.add))
    chain(tsc(v.turns, v.ang, 3.1415925, -3.1415925, ALU.min, ALU.max))
    chain(stt(v.ang, v.turns, -1.0, v.turns, ALU.mult, ALU.max))
    tsc(v.ang, v.ang, -1.0, PI / 2, ALU.mult, ALU.add).then_inc(c.sem("nsa_angles"), 1)

    dve.wait_ge(c.sem("nsa_transposed"), 1)
    for i in range(2):
        for b in range(2):
            for half in range(2):
                rows = slice(half * HEAD_DIM, (half + 1) * HEAD_DIM)
                src = c.bank[NSA_BANKS[2 * i + b]][rows].rearrange("p (h m s) -> p h m s", h=2, s=CMP_STRIDE)
                for kg in range(2):
                    at = i * CMP_COLS + 2 * b * N_CMP
                    ks = slice(kg * 8, kg * 8 + 8)
                    for hh in range(2):
                        out = v.blk[rows, ks, at + hh * N_CMP:at + (hh + 1) * N_CMP]
                        last = tt(out, src[:, hh, kg:kg + N_CMP, half::2].rearrange("p n k -> p k n"),
                                  over(v.pe[rows, i, ks], N_CMP), ALU.add)
    last.then_inc(c.sem("nsa_blk"), 1)
    dve.wait_ge(c.sem("nsa_blk_hi"), 1)
    tt(c.xT_lo[:, 0:CMP_TILES, 0:2 * CMP_COLS], v.blk[:, :, 0:2 * CMP_COLS],
       c.xT_hi[:, 0:CMP_TILES, 0:2 * CMP_COLS].bitcast(F32), ALU.subtract).then_inc(c.sem("nsa_blk_lo"), 1)

    sq = v.qr
    for t in range(TOKS):
        part = v.p[:, t, 0:Q_COLS]
        last = tt(sq[:, t, :], part, part, ALU.mult)
    chain(last)
    for t in range(TOKS):
        last = vector.tensor_reduce(v.ms[:, t, 0:HEADS], sq[:, t, :].rearrange("p (h d) -> p h d", d=HEAD_DIM), AX, ALU.add)
    chain(last)
    for t in range(TOKS):
        for j, lo in ((0, KS), (1, KW)):
            part = v.p[:, t, lo:lo + 256]
            last = tt(sq[:, t, 256 * j:256 * (j + 1)], part, part, ALU.mult)
    chain(last)
    for t in range(TOKS):
        last = vector.tensor_reduce(v.ms[:, t, HEADS:HEADS + 8],
                                    sq[:, t, 0:512].rearrange("p (h d) -> p h d", d=HEAD_DIM), AX, ALU.add)
    chain(last)
    tsc(v.ms, v.ms, 1.0 / HEAD_DIM, EPS, ALU.mult, ALU.add).then_inc(c.sem("nsa_ms"), 1)
    dve_project(c, dve, w1k, lambda s, view: copy(v.hidT[0], view))
    dve_project(c, dve, w1v, lambda s, view: copy(v.hidT[1], view))
    dve.wait_ge(c.sem("nsa_root"), 1)
    chain(vector.reciprocal(v.ms, v.ms))
    parts = [(by_head(lo, n, t), v.ms[:, t, a:a + n], n, g) for t in range(TOKS)
             for lo, n, a, g in ((0, HEADS, 0, v.q_norm), (KS, N_KV, HEADS, v.k_norm[:, 1, :]),
                                 (KW, N_KV, HEADS + N_KV, v.k_norm[:, 2, :]))]
    for x, r, n, g in parts:
        last = tt(x, x, over(r, HEAD_DIM), ALU.mult)
    chain(last)
    for x, r, n, g in parts:
        last = tt(x, x, per_head(g, n), ALU.mult)
    last.then_inc(c.sem("nsa_qn"), 1)

    dve.wait_ge(c.sem("nsa_compressed"), 1)
    comp = c.bank[3][:, 0:512].rearrange("p (a h d) -> p a h d", a=2, d=HEAD_DIM)
    chain(tt(v.kcn, comp[0:N_CMP, 0], per_head(v.b2[0:N_CMP, 0, :], N_KV), ALU.add))
    for i in range(N_GROUP):
        rows = slice(PAD * i, PAD * i + N_CMP)
        chain(tt(v.vcd[rows, :, i * HEAD_DIM:(i + 1) * HEAD_DIM], comp[rows, 1],
                 per_head(v.b2[rows, 1, :], N_KV), ALU.add))
    chain(tt(v.kc2[:, :, 0:HEAD_DIM], v.kcn, v.kcn, ALU.mult))
    chain(vector.tensor_reduce(v.kc_ms[0:N_CMP], v.kc2[:, :, 0:HEAD_DIM], AX, ALU.add))
    tsc(v.kc_ms[0:N_CMP], v.kc_ms[0:N_CMP], 1.0 / HEAD_DIM, EPS, ALU.mult, ALU.add).then_inc(c.sem("nsa_ms"), 1)
    dve.wait_ge(c.sem("nsa_root"), 2)
    chain(vector.reciprocal(v.kc_ms[0:N_CMP], v.kc_ms[0:N_CMP]))
    chain(tt(v.kcn, v.kcn, over(v.kc_ms[0:N_CMP], HEAD_DIM), ALU.mult))
    for r in range(2):
        last = tt(v.kc2[:, :, r * HEAD_DIM:(r + 1) * HEAD_DIM], v.kcn, per_head(v.k_norm[0:N_CMP, 0, :], N_KV), ALU.mult)
    last.then_inc(c.sem("nsa_kc_normed"), 1)
    dve.wait_ge(c.sem("nsa_kc_transposed"), 1)
    copy(v.kcT[:, :, 0:N_CMP], c.bank[3][:, 0:64].rearrange("p (g n) -> p g n", g=N_KV)[:, :, 0:N_CMP]
         ).then_inc(c.sem("nsa_kcT"), 1)

    dve.wait_ge(c.sem("nsa_sin_cos"), 2)
    half = HEAD_DIM // 2

    def rotate(x, dst, n, t):
        cos, sin = per_head(v.cos[:, t, :], n), per_head(v.sin[:, t, :], n)
        a, b = (v.tmp[j][:, 0:n * half].rearrange("p (h d) -> p h d", d=half) for j in range(2))
        x1, x2, o1, o2 = x[:, :, 0:half], x[:, :, half:HEAD_DIM], dst[:, :, 0:half], dst[:, :, half:HEAD_DIM]
        tt(a, x2, sin, ALU.mult)
        tt(b, x1, sin, ALU.mult)
        tt(o1, x1, cos, ALU.mult)
        chain(tt(o2, x2, cos, ALU.mult))
        tt(o1, o1, a, ALU.subtract)
        return tt(o2, o2, b, ALU.add)

    for t in range(TOKS):
        last = rotate(by_head(0, HEADS, t), v.qr[:, t, :].rearrange("p (h d) -> p h d", d=HEAD_DIM), HEADS, t)
        if t < TOKS - 1:
            chain(last)
    last.then_inc(c.sem("nsa_qr"), 1)
    dve.wait_ge(c.sem("nsa_qr"), 1)
    for j, lo in ((2, KS), (3, KW)):
        for t in range(TOKS):
            dst = v.dup[j][:, t * N_KV:(t + 1) * N_KV, :]
            chain(rotate(by_head(lo, N_KV, t), dst[:, :, 0:HEAD_DIM], N_KV, t))
            last = copy(dst[:, :, HEAD_DIM:2 * HEAD_DIM], dst[:, :, 0:HEAD_DIM])
    last.then_inc(c.sem("nsa_k_dup"), 1)

    dve.wait_ge(c.sem("nsa_c_scores"), 1)
    dve.wait_ge(c.sem("nsa_masks"), NSA_MASK_STEPS)
    for odd in range(2):
        scores = c.bank[4 + odd][:, 0:256].rearrange("p (t h n) -> p t h n", t=TOKS, n=16)
        for t in range(TOKS):
            last = tt(v.sc[:, t * HEADS + odd:(t + 1) * HEADS:2, :], scores[:, t, :, 0:N_CMP],
                      per_head(v.cmask[:, t, :], HEADS // 2), ALU.add)
    chain(last)
    chain(vector.tensor_reduce(v.cmax, v.sc, AX, ALU.max))
    tt(v.sc, v.sc, over(v.cmax, N_CMP), ALU.subtract).then_inc(c.sem("nsa_c_shifted"), 1)
    chain(vector.memset(v.pc, 0.0))
    dve.wait_ge(c.sem("nsa_c_exp"), 1)
    chain(vector.tensor_reduce(v.csum, v.sc, AX, ALU.add))
    chain(vector.reciprocal(v.csum, v.csum))
    dve.wait_ge(c.sem("nsa_gates"), 1)
    gate = v.gates.rearrange("p t (h i) -> p t h i", i=3)[:, :, :, 0]
    csum = v.csum.rearrange("p (t h) -> p t h", t=TOKS)
    chain(tt(csum, csum, gate, ALU.mult))
    chain(tt(csum, csum, over(v.seen, HEADS), ALU.mult))
    tt(v.pc[:, :, 0:N_CMP], v.sc, over(v.csum, N_CMP), ALU.mult).then_inc(c.sem("nsa_c_probs"), 1)
    dve.wait_ge(c.sem("nsa_c_out"), 1)
    for b in range(4):
        last = copy(v.p[:, b // 2, b % 2 * 512:(b % 2 + 1) * 512], c.bank[2 + b][:])
    last.then_inc(c.sem("nsa_c_added"), 1)
    dve.wait_ge(c.sem("nsa_c_added"), 1)
    dve_heads(c, dve, nsa_heads(c, 0), st.heads)
    dve.wait_ge(c.sem("head_out_read"), st.heads + HEADS)
    dve_heads(c, dve, nsa_heads(c, 1), st.heads + HEADS)
    dve_to_operand(c, dve, st)
    dve_project(c, dve, w_out, dve_add_to_h(c, w_out))
    dve.wait_ge(c.sem("projection_read"), w_out.step + w_out.steps)
    vector.tensor_copy(c.ms[:], c.ms[:]).then_inc(c.sem("h_updated"), 1)

def sp_projections(c, sp, st):
    for pr in st.projections:
        sp_project(c, sp, pr)


KINDS = ("ffn", "rg", "kv", "fa", "gdn", "sc", "nsa")
SP_STAGES = {k: sp_projections for k in KINDS} | {"ffn": sp_ffn}
PE_STAGES = dict(zip(KINDS, (pe_ffn, pe_rg, pe_kv, pe_fa, pe_gdn, pe_sc, pe_nsa)))
ACT_STAGES = dict(zip(KINDS, (act_ffn, act_rg, act_kv, act_fa, act_gdn, act_sc, act_nsa)))
DVE_STAGES = dict(zip(KINDS, (dve_ffn, dve_rg, dve_kv, dve_fa, dve_gdn, dve_sc, dve_nsa)))
POOL_STAGES = dict(zip(KINDS, (pool_load_post_gain, pool_rg, pool_kv, pool_load_post_gain, pool_gdn, pool_sc, pool_nsa)))


class Stage:

    def __init__(self, kind, projections=(), post=None, gate=None, up=None, down=None):
        self.kind, self.projections, self.post = kind, projections, post
        self.gate, self.up, self.down = gate, up, down


def number(stages):
    slab = norm = ffn = updates = post = step = operand = heads = 0
    seen = {}
    for st in stages:
        st.slab, st.norm, st.ffn, st.updates, st.post_index = slab, norm, ffn, updates, post
        st.turn = seen.get(st.kind, 0)
        seen[st.kind] = st.turn + 1
        st.operand, st.heads = operand, heads
        operand += st.kind in ("fa", "gdn", "nsa")
        heads += {"fa": HEADS, "nsa": 2 * HEADS}.get(st.kind, 0)
        for pr in st.projections:
            pr.slab, pr.step = slab, step
            slab, step = slab + pr.steps * pr.slabs, step + pr.steps
        st.step_end = step
        if st.kind == "ffn":
            slab, ffn = slab + 3 * CHUNKS, ffn + 1
        if st.kind != "kv":
            updates, post = updates + 1, post + (st.post is not None)
        norm += 1
    return slab, norm


def build(nc, stages, x, out, **small):
    slabs, norms = number(stages)
    with ExitStack() as ctx:
        c = Core(nc, ctx)
        c.slabs, c.small = slabs, small
        c.gains = c.sb("gain_cols", [P, small["gains"].shape[1]])
        c.raw_landed = [c.sem(f"raw_landed{r}") for r in range(RING)]
        block = ctx.enter_context(nc.Block())

        @block.sync
        def _(sp):
            sp.dma_start(c.h[:], x.rearrange("(t p) d -> p t d", p=P)).then_inc(c.sem("x_loaded"), 16)
            sp.dma_start(c.gains[:], small["gains"]).then_inc(c.sem("gains_loaded"), 16)
            for st in stages:
                SP_STAGES[st.kind](c, sp, st)
            sp.wait_ge(c.sem("h_updated"), stages[-1].updates + 1)
            sp.dma_start(out.rearrange("(t p) d -> p t d", p=P), c.h[:]).then_inc(c.sem("out_stored"), 16)
            sp.wait_ge(c.sem("out_stored"), 16)

        @block.gpsimd
        def _(pool):
            pool_masks(c, pool)
            for st in stages:
                POOL_STAGES[st.kind](c, pool, st)

        @block.scalar
        def _(act):
            for n in range(RING):
                act_split(c, act, slab_number(n, 0))
            for st in stages:
                act_norm(c, act, st)
                ACT_STAGES[st.kind](c, act, st)

        @block.vector
        def _(dve):
            c.chain = Chain(dve, c.sem("dve_chain"))
            for n in range(RING):
                dve_split(c, dve, slab_number(n, 0))
            for st in stages:
                dve_norm(c, dve, st)
                DVE_STAGES[st.kind](c, dve, st)

        @block.tensor
        def _(pe):
            for st in stages:
                pe_norm(c, pe, st)
                PE_STAGES[st.kind](c, pe, st)


def model(nc, x, out, w, small):
    P_ = Projection

    def ffn1(name, layer):
        return Stage("ffn", gate=(w[name + "_w_gate"][layer], 0), up=(w[name + "_w_up"][layer], 0),
                     down=w[name + "_w_down"][layer], post=w[name + "_post_g"][layer])

    def ffn2(layer, half):
        gate_up = w["ffn_w_gate_up_2"][layer, half]
        return Stage("ffn", gate=(gate_up, 0), up=(gate_up, D_FF), down=w["ffn_w_down_2"][layer, half])

    def gdn(turn):
        w_in = w["gdn_w_in_2"][turn]
        return Stage("gdn", projections=[P_(w_in, 0, 12, "feat"), P_(w_in, 3072, 4, "tok"),
                                         P_(w_in, 4096, 1, "tok", width=16), P_(w["gdn_w_out_2"][turn], 0, 4, "tok")])

    recurrent = Stage("rg", post=w["mix_post_g"][0],
                      projections=[P_(w["rg_w_in"][0], 0, 16, "feat", width=2 * LRU_W),
                                   P_(w["rg_w_out"][0], 0, 4, "tok", kp=LRU_W, slabs=2)])
    shared_kv = Stage("kv", projections=[P_(w["w_kv"], 0, 4, "feat"), P_(w["w_kv"], D_MODEL, 4, "tok"),
                                         P_(w["w_fgate"], 0, 1, "tok", width=HEADS)])
    forgetting = Stage("fa", post=w["mix_post_g"][1],
                       projections=[P_(w["attn_w_q"][0], 0, 4, "feat"), P_(w["attn_w_o"][0], 0, 4, "tok")])
    short_conv = Stage("sc", projections=[P_(w["sc_w_in_2"][0], 0, 12, "feat"), P_(w["sc_w_out_2"][0], 0, 4, "tok")])
    w_nsa, w_cmp = w["nsa_w_in_2"][0], w["nsa_cmp_w1_2"][0]
    sparse = Stage("nsa", projections=[P_(w_nsa, 0, 10, "tok"), P_(w_nsa, GATES, 1, "tok", width=3 * HEADS),
                                       P_(w_cmp[0], 0, 1, "feat", slabs=2, operand_cols=(0, CMP_COLS)),
                                       P_(w_cmp[1], 0, 1, "feat", slabs=2, operand_cols=(CMP_COLS, 2 * CMP_COLS)),
                                       P_(w["nsa_w_out_2"][0], 0, 4, "tok")])
    stages = [ffn1("ffn1", 0), recurrent, ffn1("ffn2", 0), shared_kv, ffn1("ffn1", 1), forgetting, ffn1("ffn2", 1)]
    for layer, mixer in enumerate((gdn(0), short_conv, sparse, gdn(1))):
        stages += [ffn2(layer, 0), mixer, ffn2(layer, 1)]
    build(nc, stages, x, out, **small)


WEIGHTS = ("ffn1_w_gate", "ffn1_w_up", "ffn1_w_down", "ffn1_post_g", "mix_post_g", "ffn2_w_gate", "ffn2_w_up",
           "ffn2_w_down", "ffn2_post_g", "rg_w_in", "rg_w_out", "w_kv", "w_fgate", "attn_w_q", "attn_w_o",
           "ffn_w_gate_up_2", "ffn_w_down_2", "gdn_w_in_2", "gdn_w_out_2", "sc_w_in_2", "sc_w_out_2",
           "nsa_w_in_2", "nsa_cmp_w1_2", "nsa_w_out_2")


def layout(inputs):
    import numpy as np

    def columns(a, p=P):
        return np.asarray(a).reshape(-1, p).T

    i = {k: np.asarray(v) for k, v in inputs.items()}
    norms = [i["ffn1_pre_g"][0], i["mix_pre_g"][0], i["ffn2_pre_g"][0], i["kv_norm_g"],
             i["ffn1_pre_g"][1], i["mix_pre_g"][1], i["ffn2_pre_g"][1]]
    for layer in range(4):
        norms += [i["ffn_norm_2"][layer, 0], i["mixer_norm_2"][layer], i["ffn_norm_2"][layer, 1]]
    rg_taps = i["rg_conv_w"][0].reshape(LRU_TAPS, LRU_BLOCKS, LRU_W).transpose(2, 1, 0).reshape(LRU_W, -1)
    rg_vectors = [columns(i[k][0], LRU_W) for k in ("rg_conv_b", "rg_b_a", "rg_b_x", "rg_lambda")]
    small = {
        "gains": np.concatenate([columns(g) for g in norms], 1),
        "rg_small": np.concatenate([rg_taps] + rg_vectors, 1),
        "rg_w_a": i["rg_w_a"][0], "rg_w_x": i["rg_w_x"][0], "b_fgate": i["b_fgate"],
        "gdn_taps": i["gdn_conv_w_2"].reshape(2, 4, 24, P).transpose(0, 3, 2, 1).reshape(2, P, 96),
        "gdn_A_log": i["gdn_A_log_2"], "gdn_dt_bias": i["gdn_dt_bias_2"], "gdn_out_norm": i["gdn_out_norm_2"],
        "sc_taps": i["sc_conv_w_2"][0].reshape(3, KD, P).transpose(2, 1, 0).reshape(P, 3 * KD),
        "positions": i["positions_2"][0].reshape(TOKS, P).T,
        "inv_freq": np.float32(1) / (10000.0 ** (np.arange(0, HEAD_DIM, 2) / HEAD_DIM)).astype(np.float32),
        "nsa_q_norm": i["nsa_q_norm_2"][0], "nsa_k_norm": i["nsa_k_norm_2"][0].reshape(-1),
        "nsa_b2": i["nsa_cmp_b2_2"][0].reshape(-1),
        "nsa_pe": i["nsa_cmp_pe_2"][0].reshape(2, 16, P).transpose(2, 0, 1).reshape(P, 32),
        "nsa_w2": i["nsa_cmp_w2_2"][0].reshape(-1, HEAD_DIM),
        "nsa_b1": i["nsa_cmp_b1_2"][0].reshape(4, P).T,
    }
    return {k: np.ascontiguousarray(v) for k, v in small.items()}


def kernel(**inputs):
    import numpy as np
    import concourse.bacc as _bacc
    from concourse.bass_utils import run_bass_kernel_spmd as _run

    nc = _bacc.Bacc("TRN2", target_bir_lowering=False, num_devices=1)
    arrays = {}

    def dram(name, a):
        arrays[name] = np.ascontiguousarray(a)
        return nc.dram_tensor(name, a.shape, mybir.dt.from_np(a.dtype), kind="ExternalInput").ap()

    x = dram("x", np.asarray(inputs["x"])[0])
    w = {k: dram(k, np.asarray(inputs[k])) for k in WEIGHTS}
    small = {k: dram(k, a) for k, a in layout(inputs).items()}
    out = nc.dram_tensor("out", (SEQ, D_MODEL), F32, kind="ExternalOutput").ap()
    model(nc, x, out, w, small)
    return _run(nc, [arrays], core_ids=[0]).results[0]["out"].reshape(1, SEQ, D_MODEL)
```

```python
from contextlib import ExitStack

import concourse.bass as bass
from concourse import mybir

F32 = mybir.dt.float32
F32R = mybir.dt.float32r
ALU = mybir.AluOpType
ACT = mybir.ActivationFunctionType
AX = mybir.AxisListType.X

P = 128
D_MODEL = 1024
SEQ = 256
TOKS = SEQ // P
KD = D_MODEL // P
D_FF = 2816
FCOLS = 256
CHUNKS = D_FF // FCOLS
RING = 3
SLAB = 2048
PCOLS = SLAB // KD
EPS = 1e-6
ARENA = 16384

ACC, GU, HT = 0, 4, 6
NORM_BANKS = (6, 7, 2, 3)


class Core:

    def __init__(self, nc, ctx):
        self.nc, self.ctx = nc, ctx
        self.sems = {}

        def sb(name, shape, dt=F32):
            return ctx.enter_context(nc.sbuf_tensor(name, shape, dt))

        self.sb = sb
        self.h = sb("h", [P, TOKS, D_MODEL])
        self.xn = sb("xn", [P, TOKS, D_MODEL])
        self.xT_hi = sb("xT_hi", [P, 2 * KD, SEQ], F32R)
        self.xT_lo = sb("xT_lo", [P, 2 * KD, SEQ], F32R)
        self.arena = sb("arena", [P, ARENA])
        self.mix_out = sb("mix_out", [P, TOKS, D_MODEL])
        self.raw = [sb(f"raw{r}", [P, SLAB]) for r in range(RING)]
        self.w_hi = [sb(f"w_hi{r}", [P, SLAB], F32R) for r in range(RING)]
        self.w_lo = [sb(f"w_lo{r}", [P, SLAB], F32R) for r in range(RING)]
        self.silu = sb("silu", [P, TOKS, FCOLS])
        self.hid = sb("hid", [P, TOKS, FCOLS])
        self.hidT_hi = sb("hidT_hi", [P, FCOLS // P, SEQ], F32R)
        self.hidT_lo = sb("hidT_lo", [P, FCOLS // P, SEQ], F32R)
        self.post_gain = sb("post_gain", [P, D_MODEL])
        self.ssq = sb("ssq", [P, TOKS * 2])
        self.ms = sb("ms", [P, TOKS])
        self.rms = sb("rms", [P, TOKS])
        self.rstd = sb("rstd", [P, TOKS])
        self.ident = sb("ident", [P, P])
        self.nsa_pos = sb("nsa_pos", [P, TOKS], mybir.dt.int32)
        self.ones = sb("ones", [P, P])
        self.upper = sb("upper", [P, P])
        self.causal = sb("causal", [P, 3 * P])
        self.bank = [ctx.enter_context(nc.psum_tensor(f"bank{b}", [P, 512], F32)) for b in range(8)]

    def sem(self, name):
        if name not in self.sems:
            self.sems[name] = self.ctx.enter_context(self.nc.semaphore(name))
        return self.sems[name]


class Chain:

    def __init__(self, eng, sem):
        self.eng, self.sem, self.n, self.past = eng, sem, 0, 0

    def __call__(self, ins):
        self.n += 1
        ins.then_inc(self.sem, 1)
        self.eng.wait_ge(self.sem, self.past + self.n)



def slab_number(base, i):
    return base + RING * i, base % RING, base // RING + i


def act_split(c, act, s):
    n, r, before = s
    if isinstance(n, int) and n >= c.slabs:
        return
    act.wait_ge(c.raw_landed[r], 32 * before + 32)
    if not (isinstance(n, int) and n < RING):
        act.wait_ge(c.sem("slab_used"), n - RING + 1)
    c.nc.scalar.activation(c.w_hi[r][:], c.raw[r][:], ACT.Copy).then_inc(c.sem("w_hi_split"), 1)


def dve_split(c, dve, s):
    n, r, before = s
    if isinstance(n, int) and n >= c.slabs:
        return
    dve.wait_ge(c.sem("w_hi_split"), n + 1)
    c.nc.vector.tensor_tensor(c.w_lo[r][:], c.raw[r][:], c.w_hi[r][:].bitcast(F32),
                              ALU.subtract).then_inc(c.sem("w_lo_split"), 1)


def sp_load(c, sp, s, pairs):
    n, r, before = s
    if not (isinstance(n, int) and n < RING):
        sp.wait_ge(c.sem("w_lo_split"), n - RING + 1)
    for dst, src in pairs:
        sp.dma_start(dst, src).then_inc(c.raw_landed[r], 16)


def pe_matmul3(c, out, x_hi, x_lo, w_hi, w_lo, start, stop, swap=False):
    mm = c.nc.tensor.matmul
    if swap:
        mm(out, w_hi, x_hi, start=start, stop=False)
        mm(out, w_hi, x_lo, start=False, stop=False)
        return mm(out, w_lo, x_hi, start=False, stop=stop)
    mm(out, x_hi, w_hi, start=start, stop=False)
    mm(out, x_hi, w_lo, start=False, stop=False)
    return mm(out, x_lo, w_hi, start=False, stop=stop)




def act_sum_squares(c, act, st):
    for t in range(TOKS):
        c.nc.scalar.activation(c.xn[:, t, :], c.h[:, t, :], ACT.Square,
                               accum_out=c.ssq[:, t:t + 1]).then_inc(c.sem("squares_summed"), 1)
    act.wait_ge(c.sem("mean_square"), st.norm + 1)
    c.nc.scalar.activation(c.rms[:], c.ms[:], ACT.Sqrt).then_inc(c.sem("rms_ready"), 1)


def act_norm(c, act, st):
    n = st.norm
    if st.kind != "ffn":
        if st.updates:
            act.wait_ge(c.sem("h_updated"), st.updates)
        else:
            act.wait_ge(c.sem("x_loaded"), 16)
        act_sum_squares(c, act, st)
    for k in range(KD):
        act.wait_ge(c.sem("xn_transposed"), 4 * n + k // 2 + 1)
        if k == 0 and n == 0:
            act.wait_ge(c.sem("gains_loaded"), 16)
        c.nc.scalar.activation(c.xT_hi[:, k, :], c.bank[NORM_BANKS[k // 2]][:, (k % 2) * SEQ:(k % 2 + 1) * SEQ],
                               ACT.Copy, scale=c.gains[:, n * KD + k:n * KD + k + 1]
                               ).then_inc(c.sem("xT_hi_ready"), 1)
    if st.kind == "ffn":
        act_sum_squares(c, act, st)


def dve_rstd(c, dve, st):
    dve.wait_ge(c.sem("squares_summed"), 2 * st.norm + 2)
    c.nc.vector.tensor_scalar(c.ms[:], c.ssq[:, 0:TOKS], 1.0 / D_MODEL, EPS, ALU.mult, ALU.add
                              ).then_inc(c.sem("mean_square"), 1)
    dve.wait_ge(c.sem("rms_ready"), st.norm + 1)
    c.nc.vector.reciprocal(c.rstd[:], c.rms[:]).then_inc(c.sem("rstd_ready"), 1)
    dve.wait_ge(c.sem("rstd_ready"), st.norm + 1)


def dve_norm(c, dve, st):
    n = st.norm
    if st.kind != "ffn":
        dve_rstd(c, dve, st)
        for t in range(TOKS):
            last = c.nc.vector.tensor_scalar(c.xn[:, t, :], c.h[:, t, :], c.rstd[:, t:t + 1], None, ALU.mult)
        last.then_inc(c.sem("xn_ready"), 1)
    for k in range(KD):
        dve.wait_ge(c.sem("xT_hi_ready"), KD * n + 2 * (k // 2) + 2)
        if k == 0 and n == 0:
            dve.wait_ge(c.sem("gains_loaded"), 16)
        c.nc.vector.scalar_tensor_tensor(
            c.xT_lo[:, k, :], c.bank[NORM_BANKS[k // 2]][:, (k % 2) * SEQ:(k % 2 + 1) * SEQ],
            c.gains[:, n * KD + k:n * KD + k + 1], c.xT_hi[:, k, :].bitcast(F32), ALU.mult, ALU.subtract
        ).then_inc(c.sem("xT_lo_ready"), 1)
    if st.kind == "ffn":
        dve_rstd(c, dve, st)


def pe_norm(c, pe, st):
    n = st.norm
    if n == 0:
        pe.wait_ge(c.sem("masks_made"), MASK_STEPS)
    if st.kind != "ffn":
        src = c.xn
        pe.wait_ge(c.sem("xn_ready"), st.mixer + 1)
    elif n == 0:
        src = c.h
        pe.wait_ge(c.sem("x_loaded"), 16)
    else:
        src = c.h
        pe.wait_ge(c.sem("h_updated"), st.updates)
    for g in range(KD // 2):
        for k in (2 * g, 2 * g + 1):
            for t in range(TOKS):
                last = c.nc.tensor.transpose(
                    c.bank[NORM_BANKS[g]][:, (k % 2) * SEQ + t * P:(k % 2) * SEQ + (t + 1) * P],
                    src[:, t, k * P:(k + 1) * P], c.ident[:])
        last.then_inc(c.sem("xn_transposed"), 1)



def ffn_views(c, st):
    def gate_up(r, half, j):
        raw = c.raw[r][:].rearrange("p (k n) -> p k n", k=KD // 2)
        rows = slice(half * D_MODEL // 2, (half + 1) * D_MODEL // 2)
        return [(raw[:, :, s * FCOLS:(s + 1) * FCOLS],
                 w[rows, bass.ds(off + j * FCOLS, FCOLS)].rearrange("(k p) n -> p k n", p=P))
                for s, (w, off) in enumerate((st.gate, st.up))]

    def down(r, j):
        raw = c.raw[r][:].rearrange("p (k n) -> p k n", k=FCOLS // P)
        return [(raw[:, q, :], st.down[bass.ds(j * FCOLS + q * P, P), :]) for q in range(FCOLS // P)]
    return gate_up, down


def sp_ffn(c, sp, st):
    gate_up, down = ffn_views(c, st)
    b = st.slab
    sp_load(c, sp, slab_number(b, 0), gate_up(b % RING, 0, 0))
    sp_load(c, sp, slab_number(b + 1, 0), gate_up((b + 1) % RING, 1, 0))
    with c.nc.sync.Fori(1, CHUNKS) as j:
        sp_load(c, sp, slab_number(b - 1, j), gate_up((b - 1) % RING, 0, j))
        sp_load(c, sp, slab_number(b, j), gate_up(b % RING, 1, j))
        sp_load(c, sp, slab_number(b + 1, j), down((b + 1) % RING, j - 1))
    e = b + 3 * CHUNKS - 1
    sp_load(c, sp, slab_number(e, 0), down(e % RING, CHUNKS - 1))


def pool_load_post_gain(c, pool, st):
    if st.post is not None:
        if st.updates:
            pool.wait_ge(c.sem("h_updated"), st.updates)
        pool.dma_start(c.post_gain[:], st.post.partition_broadcast(P)).then_inc(c.sem("post_gain_loaded"), 16)


def pe_ffn(c, pe, st):
    b, f0 = st.slab, st.ffn * CHUNKS
    tensor = c.nc.tensor

    def gate_up(s, half, chunk, first_norm=None):
        n, r, _ = s
        pe.wait_ge(c.sem("w_lo_split"), n + 1)
        for k4 in range(KD // 2):
            k = half * (KD // 2) + k4
            if first_norm is not None:
                pe.wait_ge(c.sem("xT_lo_ready"), KD * first_norm + k + 1)
            for t in range(TOKS):
                tok, w = slice(t * P, (t + 1) * P), slice(k4 * 512, (k4 + 1) * 512)
                last = pe_matmul3(c, c.bank[GU + t][:], c.xT_hi[:, k, tok], c.xT_lo[:, k, tok],
                                  c.w_hi[r][:, w], c.w_lo[r][:, w], k == 0, k == KD - 1)
        last.then_inc(c.sem("slab_used"), 1)

    def transpose_hidden(chunk):
        pe.wait_ge(c.sem("hidden_ready"), 2 * chunk + 2)
        for q in range(FCOLS // P):
            for t in range(TOKS):
                last = tensor.transpose(c.bank[HT][:, q * SEQ + t * P:q * SEQ + (t + 1) * P],
                                        c.hid[:, t, q * P:(q + 1) * P], c.ident[:])
        last.then_inc(c.sem("hidden_transposed"), 1)

    def down(s, chunk, start, stop):
        n, r, _ = s
        pe.wait_ge(c.sem("w_lo_split"), n + 1)
        pe.wait_ge(c.sem("hiddenT_lo_ready"), chunk + 1)
        for q in range(FCOLS // P):
            for t in range(TOKS):
                for m in range(2):
                    tok, w = slice(t * P, (t + 1) * P), slice(q * 1024 + m * 512, q * 1024 + (m + 1) * 512)
                    last = pe_matmul3(c, c.bank[ACC + 2 * t + m][:], c.hidT_hi[:, q, tok], c.hidT_lo[:, q, tok],
                                      c.w_hi[r][:, w], c.w_lo[r][:, w], start and q == 0, stop and q == FCOLS // P - 1)
        last.then_inc(c.sem("slab_used"), 1)

    gate_up(slab_number(b, 0), 0, f0, st.norm)
    gate_up(slab_number(b + 1, 0), 1, f0, st.norm)

    def body(j, start):
        pe.wait_ge(c.sem("hidden_ready"), 2 * (f0 - 1 + j) + 2)
        gate_up(slab_number(b - 1, j), 0, f0 + j)
        transpose_hidden(f0 - 1 + j)
        gate_up(slab_number(b, j), 1, f0 + j)
        down(slab_number(b + 1, j), f0 - 1 + j, start, False)

    body(1, True)
    with tensor.Fori(2, CHUNKS) as j:
        body(j, False)
    transpose_hidden(f0 + CHUNKS - 1)
    e = b + 3 * CHUNKS - 1
    down(slab_number(e, 0), f0 + CHUNKS - 1, False, True)


def act_ffn(c, act, st):
    b, f0 = st.slab, st.ffn * CHUNKS

    def silu(s_used, chunk):
        act.wait_ge(c.sem("slab_used"), s_used)
        for t in range(TOKS):
            c.nc.scalar.activation(c.silu[:, t, :], c.bank[GU + t][:, 0:FCOLS], ACT.Silu, scale=c.rstd[:, t:t + 1]
                                   ).then_inc(c.sem("silu_ready"), 1)

    def hidden_hi(chunk):
        act.wait_ge(c.sem("hidden_transposed"), chunk + 1)
        c.nc.scalar.activation(c.hidT_hi[:].rearrange("p q t -> p (q t)"), c.bank[HT][:], ACT.Copy
                               ).then_inc(c.sem("hiddenT_hi_ready"), 1)

    act_split(c, act, slab_number(b + 3, 0))
    act.wait_ge(c.sem("rstd_ready"), st.norm + 1)
    silu(b + 2, f0)
    act_split(c, act, slab_number(b + 4, 0))

    def body(j, last=False):
        hidden_hi(f0 - 1 + j)
        act_split(c, act, slab_number(b + 2, j))
        silu(b + 3 * j + 1, f0 + j)
        if last:
            hidden_hi(f0 + j)
        act_split(c, act, slab_number(b + 3, j))
        act_split(c, act, slab_number(b + 4, j))

    with c.nc.scalar.Fori(1, CHUNKS - 1) as j:
        body(j)
    body(CHUNKS - 1, last=True)
    act_residual(c, act, st)
    act_split(c, act, slab_number(b + 3 * CHUNKS + 2, 0))


def dve_ffn(c, dve, st):
    b, f0 = st.slab, st.ffn * CHUNKS
    vector = c.nc.vector

    def hidden(chunk):
        for t in range(TOKS):
            dve.wait_ge(c.sem("silu_ready"), 2 * chunk + t + 1)
            vector.scalar_tensor_tensor(c.hid[:, t, :], c.bank[GU + t][:, FCOLS:2 * FCOLS], c.rstd[:, t:t + 1],
                                        c.silu[:, t, :], ALU.mult, ALU.mult
                                        ).then_inc(c.sem("hidden_ready"), 1)

    def hidden_lo(chunk):
        dve.wait_ge(c.sem("hiddenT_hi_ready"), chunk + 1)
        vector.tensor_tensor(c.hidT_lo[:].rearrange("p q t -> p (q t)"), c.bank[HT][:],
                             c.hidT_hi[:].rearrange("p q t -> p (q t)").bitcast(F32), ALU.subtract
                             ).then_inc(c.sem("hiddenT_lo_ready"), 1)

    dve_split(c, dve, slab_number(b + 3, 0))
    hidden(f0)
    dve_split(c, dve, slab_number(b + 4, 0))

    def body(j, last=False):
        hidden_lo(f0 - 1 + j)
        dve_split(c, dve, slab_number(b + 2, j))
        hidden(f0 + j)
        if last:
            hidden_lo(f0 + j)
        dve_split(c, dve, slab_number(b + 3, j))
        dve_split(c, dve, slab_number(b + 4, j))

    with vector.Fori(1, CHUNKS - 1) as j:
        body(j)
    body(CHUNKS - 1, last=True)
    dve_residual(c, dve, st)
    dve_split(c, dve, slab_number(b + 3 * CHUNKS + 2, 0))



def residual_sources(c, st):
    parts = [(t, m) for t in range(TOKS) for m in range(2)]
    if st.kind == "ffn":
        return [(t, m, c.bank[ACC + 2 * t + m][:]) for t, m in parts], "slab_used", st.slab + 3 * CHUNKS
    return [(t, m, c.mix_out[:, t, m * 512:(m + 1) * 512]) for t, m in parts], "projection_read", st.step_end


def act_residual(c, act, st):
    if st.post is None:
        return
    parts, done, count = residual_sources(c, st)
    act.wait_ge(c.sem(done), count)
    for t, m, src in parts:
        c.nc.scalar.activation(c.xn[:, t, m * 512:(m + 1) * 512], src, ACT.Square,
                               accum_out=c.ssq[:, 2 * t + m:2 * t + m + 1]).then_inc(c.sem("post_squares"), 1)
    act.wait_ge(c.sem("post_mean_square"), st.post_index + 1)
    c.nc.scalar.activation(c.rms[:], c.ms[:], ACT.Sqrt).then_inc(c.sem("post_rms"), 1)


def dve_residual(c, dve, st):
    parts, done, count = residual_sources(c, st)
    vector, factor = c.nc.vector, 0.5 if st.kind == "ffn" else 1.0
    if st.post is None:
        dve.wait_ge(c.sem(done), count)
        for t, m, src in parts:
            out = c.h[:, t, m * 512:(m + 1) * 512]
            last = vector.scalar_tensor_tensor(out, src, factor, out, ALU.mult, ALU.add)
    else:
        dve.wait_ge(c.sem("post_squares"), 4 * st.post_index + 4)
        c.chain(vector.tensor_tensor(c.ms[:], c.ssq[:, 0:4:2], c.ssq[:, 1:4:2], ALU.add))
        vector.tensor_scalar(c.ms[:], c.ms[:], 1.0 / D_MODEL, EPS, ALU.mult, ALU.add
                             ).then_inc(c.sem("post_mean_square"), 1)
        dve.wait_ge(c.sem("post_rms"), st.post_index + 1)
        c.chain(vector.reciprocal(c.rstd[:], c.rms[:]))
        dve.wait_ge(c.sem("post_gain_loaded"), 16 * st.post_index + 16)
        for t, m, src in parts:
            cols = slice(m * 512, (m + 1) * 512)
            c.chain(vector.scalar_tensor_tensor(c.xn[:, t, cols], src, c.rstd[:, t:t + 1],
                                                c.post_gain[:, cols], ALU.mult, ALU.mult))
            last = vector.scalar_tensor_tensor(c.h[:, t, cols], c.xn[:, t, cols], factor, c.h[:, t, cols],
                                               ALU.mult, ALU.add)
    last.then_inc(c.sem("h_updated"), 1)



class Projection:

    def __init__(self, w, col0, steps, form, width=PCOLS, kp=P, slabs=1, operand_cols=(0, SEQ), two_banks=False, padded=False,
                 loop=True):
        self.loop = loop and slabs == 1 and steps >= 6
        self.two_banks = two_banks
        self.rows = P if padded else kp
        self.w, self.col0, self.steps, self.form, self.width = w, col0, steps, form, width
        self.kp, self.slabs, self.cols = kp, slabs, operand_cols


def step_loop(engine, pr, one):
    peeled = 1 if pr.step < 3 or pr.slab < RING else 0
    looped = pr.steps // 3 if pr.loop else 0

    def straight(s):
        one(s, [slab_number(pr.slab + s * pr.slabs + q, 0) for q in range(pr.slabs)], (pr.step + s) % 3, pr.step + s)

    if looped > peeled:
        for s in range(3 * peeled):
            straight(s)
        with engine.Fori(peeled, looped) as i:
            for r in range(3):
                one(3 * i + r, [slab_number(pr.slab + r, i)], (pr.step + r) % 3, pr.step + r + 3 * i)
    for s in range(3 * looped if looped > peeled else 0, pr.steps):
        straight(s)


def sp_project(c, sp, pr):
    def one(s, slabs, bank, g):
        for q, slab in enumerate(slabs):
            n = KD // 2
            raw = c.raw[slab[1]][0:pr.kp, 0:KD * pr.width].rearrange("p (k n) -> p k n", k=KD)
            row = q * KD * pr.kp
            sp_load(c, sp, slab, [(raw[:, f * n:(f + 1) * n, :],
                                   pr.w[row + f * n * pr.kp:row + (f + 1) * n * pr.kp,
                                        bass.ds(pr.col0 + s * pr.width, pr.width)].rearrange("(k p) n -> p k n", p=pr.kp))
                                  for f in range(2)])
    step_loop(c.nc.sync, pr, one)


def pe_project(c, pe, pr, after=None, ready=None):
    def one(s, slabs, bank, g):
        if not isinstance(g, int) or g >= 3:
            pe.wait_ge(c.sem("projection_read"), g - 2)
        if not pr.two_banks:
            for n, r, _ in slabs:
                pe.wait_ge(c.sem("w_lo_split"), n + 1)
        kt = KD * len(slabs)
        lo, hi = pr.cols
        tiles = {"tok": TOKS, "feat": 2, "rows": 1}[pr.form]
        if pr.two_banks:
            order = [(tile, k) for q in range(len(slabs)) for tile in range(tiles) for k in range(q * KD, (q + 1) * KD)]
        else:
            order = [(tile, k) for tile in range(tiles) for k in range(kt)]
        for tile, k in order:
            r = slabs[k // KD][1]
            base = (k % KD) * pr.width
            if pr.two_banks and tile == 0 and k % KD == 0:
                if ready is not None and s == 0:
                    ready(k // KD)
                pe.wait_ge(c.sem("w_lo_split"), slabs[k // KD][0] + 1)
            first, end = k == 0, k == kt - 1
            if pr.form == "tok":
                x = slice(tile * P, (tile + 1) * P)
                w = slice(base, base + pr.width)
                out = c.bank[bank][:, tile * pr.width:(tile + 1) * pr.width]
                if pr.two_banks:
                    out = c.bank[bank + 4 * tile][:, 0:pr.width]
            elif pr.form == "rows":
                x, w, out = slice(lo, hi), slice(base, base + pr.width), c.bank[bank][0:hi - lo, 0:pr.width]
            else:
                x = slice(lo, hi)
                w = slice(base + tile * pr.width // 2, base + (tile + 1) * pr.width // 2)
                out = c.bank[bank][0:pr.width // 2, tile * (hi - lo):(tile + 1) * (hi - lo)]
            last = pe_matmul3(c, out, c.xT_hi[0:pr.rows, k, x], c.xT_lo[0:pr.rows, k, x],
                              c.w_hi[r][0:pr.rows, w], c.w_lo[r][0:pr.rows, w], first, end, pr.form == "feat")
            if tile == tiles - 1 and k % KD == KD - 1:
                last.then_inc(c.sem("slab_used"), 1)
        if after is not None:
            after(s)
    step_loop(c.nc.tensor, pr, one)


def act_project(c, act, pr, first=None, after=None):
    def one(s, slabs, bank, g):
        if first is not None:
            act.wait_ge(c.sem("slab_used"), slabs[-1][0] + 1)
            first(s, projection_view(c, pr, bank))
        for n, r, before in slabs:
            act_split(c, act, (n + RING, r, before + 1))
        if after is not None:
            after(s)
    step_loop(c.nc.scalar, pr, one)


def projection_view(c, pr, bank):
    if pr.form == "tok":
        return c.bank[bank][:, 0:TOKS * pr.width].rearrange("p (t n) -> p t n", t=TOKS)
    if pr.form == "rows":
        return c.bank[bank][0:pr.cols[1] - pr.cols[0], 0:pr.width]
    return c.bank[bank][0:pr.width // 2, 0:2 * (pr.cols[1] - pr.cols[0])].rearrange("p (t n) -> p t n", t=2)


def dve_project(c, dve, pr, read, after=None):
    def one(s, slabs, bank, g):
        n, r, _ = slabs[-1]
        dve.wait_ge(c.sem("slab_used"), n + 1)
        if pr.two_banks:
            read(s, c.bank[bank][:, 0:pr.width], 0)
            read(s, c.bank[bank + 4][:, 0:pr.width], 1).then_inc(c.sem("projection_read"), 1)
        else:
            read(s, projection_view(c, pr, bank)).then_inc(c.sem("projection_read"), 1)
        for n, r, before in slabs:
            dve_split(c, dve, (n + RING, r, before + 1))
        if after is not None:
            after(s)
    step_loop(c.nc.vector, pr, one)


def tap(taps, n, j):
    return taps[:, bass.ds(n, 1), j:j + 1].rearrange("p a b -> p (a b)")


def act_first_tap(c, dst, taps, last_tap, bias=None):
    def first(s, view):
        for q in range(2):
            n = 2 * s + q
            if bias is None:
                last = c.nc.scalar.activation(dst[:, bass.ds(n, 1), :], view[:, q:q + 1, :], ACT.Copy,
                                              scale=tap(taps, n, last_tap))
            else:
                last = c.nc.scalar.activation(dst[:, bass.ds(n, 1), :], view[:, q:q + 1, :], ACT.Identity,
                                              scale=tap(taps, n, last_tap), bias=bias[:, bass.ds(n, 1)])
        last.then_inc(c.sem("first_tap"), 1)
    return first


def dve_shifted_taps(c, dve, dst, taps, last_tap, before):
    def read(s, view):
        dve.wait_ge(c.sem("first_tap"), before + s + 1)
        for j in range(last_tap - 1, -1, -1):
            back = last_tap - j
            for q in range(2):
                n = 2 * s + q
                last = c.nc.vector.scalar_tensor_tensor(dst[:, bass.ds(n, 1), back:], view[:, q:q + 1, 0:SEQ - back],
                                                        tap(taps, n, j), dst[:, bass.ds(n, 1), back:], ALU.mult, ALU.add)
            if j:
                last.then_inc(c.sem("tap_added"), 1)
                dve.wait_ge(c.sem("tap_added"), (last_tap - 1) * (before + s) + back)
        return last
    return read


def dve_add_to_h(c, pr):
    def read(s, view):
        out = c.h[:, :, bass.ds(s * pr.width, pr.width)]
        return c.nc.vector.tensor_tensor(out, view, out, ALU.add)
    return read



MASK_STEPS = 7
MASKED = -1e30

def pool_masks(c, pool):
    g = c.nc.gpsimd
    c.mask_sets = 0

    def step(ins):
        c.mask_sets += 1
        ins.then_inc(c.sem("masks_made"), 1)
        pool.wait_ge(c.sem("masks_made"), c.mask_sets)

    step(g.memset(c.ident[:], 0.0))
    step(g.affine_select(out=c.ident[:], in_=c.ident[:], compare_op=ALU.not_equal, fill=1.0, base=0,
                         pattern=[[-1, P]], channel_multiplier=1))
    step(g.memset(c.ones[:], 1.0))
    step(g.affine_select(out=c.upper[:], in_=c.ones[:], compare_op=ALU.is_ge, fill=0.0, base=0,
                         pattern=[[1, P]], channel_multiplier=-1))
    step(g.memset(c.causal[:], 0.0))
    for lo in (0, 2 * P):
        part = c.causal[:, lo:lo + P]
        step(g.affine_select(out=part, in_=part, compare_op=ALU.is_ge, fill=MASKED, base=0,
                             pattern=[[-1, P]], channel_multiplier=1))
    assert c.mask_sets == MASK_STEPS



def arena(c, off, *shape):
    n = 1
    for d in shape[1:]:
        n *= d
    assert off + n <= ARENA
    v = c.arena[0:shape[0], off:off + n]
    if len(shape) == 3:
        return v.rearrange("p (a b) -> p a b", a=shape[1])
    if len(shape) == 4:
        return v.rearrange("p (a b d) -> p a b d", a=shape[1], b=shape[2])
    return v


SC_TAPS = 3


def sc_views(c):
    class V:
        c_gate = arena(c, 0, P, KD, SEQ)
        z = arena(c, 2048, P, KD, SEQ)
        y = arena(c, 4096, P, KD, SEQ)
        gated = arena(c, 6144, P, KD, SEQ)
        taps = arena(c, 10240, P, KD, SC_TAPS)
    return V


def pool_sc(c, pool, st):
    v = sc_views(c)
    pool.wait_ge(c.sem("h_updated"), st.updates)
    pool.dma_start(v.taps.rearrange("p a b -> p (a b)"), c.small["sc_taps"]).then_inc(c.sem("sc_taps_loaded"), 16)


def pe_sc(c, pe, st):
    w_c, w_x, w_b, w_out = st.projections
    pe.wait_ge(c.sem("xT_lo_ready"), KD * (st.norm + 1))
    for pr in (w_c, w_x, w_b):
        pe_project(c, pe, pr)
    pe.wait_ge(c.sem("sc_gated_lo"), w_b.steps)
    pe_project(c, pe, w_out)


def act_sc(c, act, st):
    v, scalar = sc_views(c), c.nc.scalar
    w_c, w_x, w_b, w_out = st.projections
    act_project(c, act, w_c)
    act.wait_ge(c.sem("sc_taps_loaded"), 16)

    def first_tap(s):
        act.wait_ge(c.sem("projection_read"), w_x.step + s + 1)
        for k in (2 * s, 2 * s + 1):
            last = scalar.activation(v.y[:, k, :], v.z[:, k, :], ACT.Copy, scale=v.taps[:, k, SC_TAPS - 1:SC_TAPS])
        last.then_inc(c.sem("sc_first_tap"), 1)

    act_project(c, act, w_x, after=first_tap)
    act_project(c, act, w_b)
    act.wait_ge(c.sem("slab_used"), w_b.slab + w_b.steps)
    for s in range(w_b.steps):
        act.wait_ge(c.sem("projection_read"), w_b.step + s + 1)
        pair = slice(2 * s, 2 * s + 2)
        scalar.activation(c.xT_hi[:, pair, :], v.gated[:, pair, :], ACT.Copy).then_inc(c.sem("sc_gated_hi"), 1)
    act_project(c, act, w_out)


def dve_sc(c, dve, st):
    v, vector, chain = sc_views(c), c.nc.vector, c.chain
    w_c, w_x, w_b, w_out = st.projections

    def shifted_taps(s):
        dve.wait_ge(c.sem("sc_first_tap"), s + 1)
        for j in range(SC_TAPS - 2, -1, -1):
            back = SC_TAPS - 1 - j
            for k in (2 * s, 2 * s + 1):
                last = vector.scalar_tensor_tensor(v.y[:, k, back:], v.z[:, k, 0:SEQ - back], v.taps[:, k, j:j + 1],
                                                   v.y[:, k, back:], ALU.mult, ALU.add)
            chain(last)

    dve_project(c, dve, w_c, lambda s, view: vector.tensor_copy(v.c_gate[:, 2 * s:2 * s + 2, :], view))
    dve.wait_ge(c.sem("projection_read"), w_c.step + w_c.steps)
    dve_project(c, dve, w_x, lambda s, view: vector.tensor_tensor(
        v.z[:, 2 * s:2 * s + 2, :], v.c_gate[:, 2 * s:2 * s + 2, :], view, ALU.mult), after=shifted_taps)
    dve_project(c, dve, w_b, lambda s, view: vector.tensor_tensor(
        v.gated[:, 2 * s:2 * s + 2, :], v.y[:, 2 * s:2 * s + 2, :], view, ALU.mult))
    for s in range(w_b.steps):
        dve.wait_ge(c.sem("sc_gated_hi"), s + 1)
        pair = slice(2 * s, 2 * s + 2)
        vector.tensor_tensor(c.xT_lo[:, pair, :], v.gated[:, pair, :], c.xT_hi[:, pair, :].bitcast(F32), ALU.subtract
                             ).then_inc(c.sem("sc_gated_lo"), 1)
    dve_project(c, dve, w_out, dve_add_to_h(c, w_out))
    dve.wait_ge(c.sem("projection_read"), w_out.step + w_out.steps)
    vector.tensor_copy(c.ms[:], c.ms[:]).then_inc(c.sem("h_updated"), 1)



LOG1P_TERMS = 7


def dve_softplus_begin(c, x, mag, ready):
    c.nc.vector.scalar_tensor_tensor(mag, x, -1.0, x, ALU.mult, ALU.max).then_inc(c.sem(ready), 1)


def act_softplus_exp(c, act, mag, e, ready, count, done):
    act.wait_ge(c.sem(ready), count)
    c.nc.scalar.activation(e, mag, ACT.Exp, scale=-1.0).then_inc(c.sem(done), 1)


def dve_softplus_end(c, dve, x, e, s, s2, q, out, done, count):
    v, chain = c.nc.vector, c.chain
    dve.wait_ge(c.sem(done), count)
    chain(v.tensor_scalar(s, e, 2.0, None, ALU.add))
    chain(v.reciprocal(s, s))
    chain(v.tensor_tensor(s, s, e, ALU.mult))
    chain(v.tensor_tensor(s2, s, s, ALU.mult))
    chain(v.tensor_scalar(q, s2, 1.0 / (2 * LOG1P_TERMS + 1), None, ALU.mult))
    for term in range(LOG1P_TERMS - 1, 0, -1):
        chain(v.scalar_tensor_tensor(q, q, 1.0 / (2 * term + 1), s2, ALU.add, ALU.mult))
    chain(v.scalar_tensor_tensor(q, q, 1.0, s, ALU.add, ALU.mult))
    chain(v.tensor_scalar(s, x, 0.0, None, ALU.max))
    chain(v.scalar_tensor_tensor(out, q, 2.0, s, ALU.mult, ALU.add))



D_RNN = 1344
LRU_BLOCKS = 16
LRU_W = D_RNN // LRU_BLOCKS
LRU_TAPS = 4
LRU_HALVES = (slice(0, LRU_BLOCKS // 2), slice(LRU_BLOCKS // 2, LRU_BLOCKS))
LRU_C = 8.0


def rg_views(c):
    small = c.silu[0:LRU_W, :, :].rearrange("p a b -> p (a b)")
    temp = c.hid[0:LRU_W, :, :].rearrange("p a b -> p (a b)")
    n = LRU_BLOCKS

    class V:
        gate = arena(c, 0, LRU_W, n, SEQ)
        rec = arena(c, 4096, LRU_W, n, SEQ)
        y = arena(c, 8192, LRU_W, n, SEQ)
        i = arena(c, 12288, LRU_W, n, SEQ)
        taps = small[:, 0:n * LRU_TAPS].rearrange("p (n j) -> p n j", n=n)
        conv_b, b_a, b_x, lam = (small[:, n * (LRU_TAPS + q):n * (LRU_TAPS + q + 1)] for q in range(4))
        packed = small[:, 0:n * (LRU_TAPS + 4)]
        w_a = c.mix_out[0:LRU_W, :, :].rearrange("p a b -> p (a b)")[:, 0:D_RNN]
        w_x = c.xn[0:LRU_W, :, :].rearrange("p a b -> p (a b)")[:, 0:D_RNN]
        neg, mag, e, s, s2, q, sp, minus_sp = (temp[:, n * j:n * (j + 1)] for j in range(8))
    return V


def pool_rg(c, pool, st):
    v = rg_views(c)
    pool.wait_ge(c.sem("h_updated"), st.updates)
    pool.dma_start(v.packed, c.small["rg_small"]).then_inc(c.sem("rg_small_loaded"), 16)
    pool.dma_start(v.w_a.rearrange("p (n d) -> p n d", n=LRU_BLOCKS), c.small["rg_w_a"].rearrange("n p d -> p n d")
                   ).then_inc(c.sem("rg_w_a_loaded"), 16)
    pool_load_post_gain(c, pool, st)
    pool.wait_ge(c.sem("xn_transposed"), 4 * (st.norm + 1))
    pool.dma_start(v.w_x.rearrange("p (n d) -> p n d", n=LRU_BLOCKS), c.small["rg_w_x"].rearrange("n p d -> p n d")
                   ).then_inc(c.sem("rg_w_x_loaded"), 16)
    w_rec = st.projections[1]
    pool.wait_ge(c.sem("projection_read"), w_rec.step + w_rec.steps)
    for x in (c.xT_hi, c.xT_lo):
        c.nc.gpsimd.memset(x[64:P, :, :].bitcast(F32), 0.0).then_inc(c.sem("rg_padding"), 1)


def pe_rg(c, pe, st):
    v = rg_views(c)
    pe.wait_ge(c.sem("xT_lo_ready"), KD * (st.norm + 1))
    w_gate, w_rec, w_out = st.projections
    pe_project(c, pe, w_gate)

    def gates(g):
        pe.wait_ge(c.sem("projection_read"), w_rec.step + g + 1)
        if g >= 2:
            pe.wait_ge(c.sem("rg_gates_read"), g - 1)
        for w, b in ((v.w_a, 4 + g % 2), (v.w_x, 6 + g % 2)):
            for n in (2 * g, 2 * g + 1):
                last = c.nc.tensor.matmul(c.bank[b][0:LRU_W, (n % 2) * SEQ:(n % 2 + 1) * SEQ],
                                          w[:, n * LRU_W:(n + 1) * LRU_W], v.y[:, n, :], start=True, stop=True)
        last.then_inc(c.sem("rg_gates"), 1)

    pe.wait_ge(c.sem("rg_w_a_loaded"), 16)
    pe.wait_ge(c.sem("rg_w_x_loaded"), 16)
    pe_project(c, pe, w_rec, after=lambda s: gates(s - 1) if s else None)
    gates(w_rec.steps - 1)
    pe_project(c, pe, w_out, ready=lambda q: pe.wait_ge(c.sem("rg_operand_lo"), q + 1))


def act_rg(c, act, st):
    v, scalar, n_all = rg_views(c), c.nc.scalar, LRU_BLOCKS
    w_gate, w_rec, w_out = st.projections
    act_softplus_exp(c, act, v.mag, v.e, "rg_lambda_mag", 1, "rg_lambda_exp")
    act_project(c, act, w_gate)
    act.wait_ge(c.sem("rg_small_loaded"), 16)
    act.wait_ge(c.sem("projection_read"), w_gate.step + w_gate.steps)
    scalar.activation(v.gate, v.gate, ACT.Gelu_apprx_tanh).then_inc(c.sem("rg_gelu"), 1)

    def gates(g):
        act.wait_ge(c.sem("rg_gates"), g + 1)
        for out, b, bias in ((v.rec, 4 + g % 2, v.b_a), (v.i, 6 + g % 2, v.b_x)):
            for n in (2 * g, 2 * g + 1):
                last = scalar.activation(out[:, n, :], c.bank[b][0:LRU_W, (n % 2) * SEQ:(n % 2 + 1) * SEQ],
                                         ACT.Sigmoid, bias=bias[:, n:n + 1])
        last.then_inc(c.sem("rg_gates_read"), 1)

    act_project(c, act, w_rec, act_first_tap(c, v.y, v.taps, LRU_TAPS - 1, v.conv_b),
                after=lambda s: gates(s - 1) if s else None)
    gates(w_rec.steps - 1)
    act.wait_ge(c.sem("rg_gated_input"), 1)
    for half in LRU_HALVES:
        for n in range(half.start, half.stop):
            last = scalar.activation(v.y[:, n, :], v.rec[:, n, :], ACT.Exp, scale=v.minus_sp[:, n:n + 1])
        last.then_inc(c.sem("rg_a"), 1)
    act.wait_ge(c.sem("rg_a"), 2)
    for half in LRU_HALVES:
        for n in range(half.start, half.stop):
            last = scalar.activation(v.rec[:, n, :], v.rec[:, n, :], ACT.Tanh, scale=v.sp[:, n:n + 1])
        last.then_inc(c.sem("rg_tanh"), 1)
    for j, half in enumerate(LRU_HALVES):
        act.wait_ge(c.sem("rg_one_minus_a2"), j + 1)
        scalar.activation(v.rec[:, half, :], v.rec[:, half, :], ACT.Sqrt).then_inc(c.sem("rg_scale"), 1)
    act.wait_ge(c.sem("rg_padding"), 2)
    for j, half in enumerate(LRU_HALVES):
        act.wait_ge(c.sem("rg_operand"), j + 1)
        scalar.activation(c.xT_hi[0:LRU_W, half, :], v.rec[:, half, :], ACT.Copy).then_inc(c.sem("rg_operand_hi"), 1)
    act_project(c, act, w_out)
    act_residual(c, act, st)


def dve_rg(c, dve, st):
    v, vector, chain, n_all = rg_views(c), c.nc.vector, c.chain, LRU_BLOCKS
    w_gate, w_rec, w_out = st.projections
    dve.wait_ge(c.sem("rg_small_loaded"), 16)
    chain(vector.tensor_scalar(v.neg, v.lam, -1.0, None, ALU.mult))
    dve_softplus_begin(c, v.neg, v.mag, "rg_lambda_mag")
    dve_softplus_end(c, dve, v.neg, v.e, v.s, v.s2, v.q, v.sp, "rg_lambda_exp", 1)
    chain(vector.tensor_scalar(v.sp, v.sp, LRU_C, None, ALU.mult))
    chain(vector.tensor_scalar(v.minus_sp, v.sp, -1.0, None, ALU.mult))
    dve_project(c, dve, w_gate, lambda s, view: vector.tensor_copy(v.gate[:, bass.ds(s * 2, 2), :], view))

    def gated(g):
        dve.wait_ge(c.sem("rg_gates_read"), g + 1)
        pair = slice(2 * g, 2 * g + 2)
        return vector.tensor_tensor(v.i[:, pair, :], v.i[:, pair, :], v.y[:, pair, :], ALU.mult)

    dve_project(c, dve, w_rec, dve_shifted_taps(c, dve, v.y, v.taps, LRU_TAPS - 1, st.conv),
                after=lambda s: gated(s - 1) if s else None)
    gated(w_rec.steps - 1).then_inc(c.sem("rg_gated_input"), 1)
    square = [c.bank[g][0:LRU_W, :].rearrange("p (n t) -> p n t", n=2) for g in range(n_all // 2)]
    for j, half in enumerate(LRU_HALVES):
        dve.wait_ge(c.sem("rg_a"), j + 1)
        for g in range(half.start // 2, half.stop // 2):
            last = vector.tensor_tensor(square[g], v.y[:, 2 * g:2 * g + 2, :], v.y[:, 2 * g:2 * g + 2, :], ALU.mult)
    chain(last)
    for j, half in enumerate(LRU_HALVES):
        dve.wait_ge(c.sem("rg_tanh"), j + 1)
        for g in range(half.start // 2, half.stop // 2):
            part = v.rec[:, 2 * g:2 * g + 2, :]
            last = vector.scalar_tensor_tensor(part, square[g], 1.0, part, ALU.add, ALU.mult)
        last.then_inc(c.sem("rg_one_minus_a2"), 1)

    def low(j):
        dve.wait_ge(c.sem("rg_operand_hi"), j + 1)
        half = LRU_HALVES[j]
        vector.tensor_tensor(c.xT_lo[0:LRU_W, half, :], v.rec[:, half, :], c.xT_hi[0:LRU_W, half, :].bitcast(F32),
                             ALU.subtract).then_inc(c.sem("rg_operand_lo"), 1)

    for j, half in enumerate(LRU_HALVES):
        dve.wait_ge(c.sem("rg_scale"), j + 1)
        chain(vector.tensor_tensor(v.i[:, half, :], v.i[:, half, :], v.rec[:, half, :], ALU.mult))
        if j:
            low(0)
        for n in range(half.start, half.stop):
            last = vector.tensor_tensor_scan(v.rec[:, n, :], v.y[:, n, :], v.i[:, n, :], 0.0, ALU.mult, ALU.add)
        chain(last)
        if not j:
            dve.wait_ge(c.sem("rg_gelu"), 1)
        vector.tensor_tensor(v.rec[:, half, :], v.rec[:, half, :], v.gate[:, half, :], ALU.mult
                             ).then_inc(c.sem("rg_operand"), 1)
    low(1)
    dve_project(c, dve, w_out, lambda s, view, t: vector.tensor_copy(
        c.mix_out[:, t, bass.ds(s * w_out.width, w_out.width)], view))
    dve_residual(c, dve, st)



def pe_to_operand(c, pe, st, src, ready, count):
    m = st.operand
    pe.wait_ge(c.sem(ready), count)
    for g in range(KD // 2):
        for k in (2 * g, 2 * g + 1):
            for t in range(TOKS):
                last = c.nc.tensor.transpose(
                    c.bank[NORM_BANKS[g]][:, (k % 2) * SEQ + t * P:(k % 2) * SEQ + (t + 1) * P],
                    src[:, t, k * P:(k + 1) * P], c.ident[:])
        last.then_inc(c.sem("mix_transposed"), 1)


def act_to_operand(c, act, st):
    for g in range(KD // 2):
        act.wait_ge(c.sem("mix_transposed"), 4 * st.operand + g + 1)
        c.nc.scalar.activation(c.xT_hi[:, 2 * g:2 * g + 2, :].rearrange("p k t -> p (k t)"),
                               c.bank[NORM_BANKS[g]][:], ACT.Copy).then_inc(c.sem("mix_hi"), 1)


def dve_to_operand(c, dve, st):
    for g in range(KD // 2):
        dve.wait_ge(c.sem("mix_hi"), 4 * st.operand + g + 1)
        c.nc.vector.tensor_tensor(c.xT_lo[:, 2 * g:2 * g + 2, :].rearrange("p k t -> p (k t)"),
                                  c.bank[NORM_BANKS[g]][:],
                                  c.xT_hi[:, 2 * g:2 * g + 2, :].rearrange("p k t -> p (k t)").bitcast(F32),
                                  ALU.subtract).then_inc(c.sem("mix_lo"), 1)



HEADS = 16
HEAD_DIM = D_MODEL // HEADS
KEYS = P + 2 * P
S_BANK, PT_BANK, O_BANK = (4, 5), (6, 7), (2, 3)


class Heads:

    def __init__(self, c, off):
        self.s = [arena(c, off + KEYS * b, P, KEYS) for b in range(2)]
        self.p = [arena(c, off + KEYS * (2 + b), P, KEYS) for b in range(2)]
        self.pT = [arena(c, off + KEYS * (4 + b), P, KEYS) for b in range(2)]
        off += 6 * KEYS
        self.neg_max = arena(c, off, P, HEADS, TOKS)
        self.sum = arena(c, off + 32, P, HEADS, TOKS)
        self.coef = arena(c, off + 64, P, HEADS, TOKS)


def pe_heads(c, pe, a, first):
    tensor = c.nc.tensor

    def scores(h):
        g = first + h
        if g >= 2:
            pe.wait_ge(c.sem("scores_read"), g - 1)
        bank, q, k = c.bank[S_BANK[h % 2]], a.qT(h), a.kT(h)
        decay = a.minus_cT is not None
        for lo, n, t in ((0, P, 0), (P, 2 * P, 1)):
            last = tensor.matmul(bank[:, lo:lo + n], q[:, t * P:(t + 1) * P], k[:, 0:n], start=True, stop=not decay)
            if decay:
                last = tensor.matmul(bank[:, lo:lo + n], c.ident[0:HEADS, h:h + 1].broadcast_to([HEADS, P]), a.minus_cT[:, 0:n], start=False, stop=True)
        last.then_inc(c.sem("scores_done"), 1)

    def transposed(h):
        g, b = first + h, h % 2
        pe.wait_ge(c.sem("probs_ready"), g + 1)
        if g >= 2:
            pe.wait_ge(c.sem("probsT_ready"), g - 1)
        for j in range(3):
            last = tensor.transpose(c.bank[PT_BANK[b]][:, j * P:(j + 1) * P], a.w.p[b][:, j * P:(j + 1) * P], c.ident[:])
        last.then_inc(c.sem("probs_transposed"), 1)

    def weighted(h):
        g, b = first + h, h % 2
        pe.wait_ge(c.sem("probsT_ready"), g + 1)
        if g >= 2:
            pe.wait_ge(c.sem("head_out_read"), g - 1)
        out, pT = c.bank[O_BANK[b]], a.w.pT[b]
        tensor.matmul(out[:, 0:HEAD_DIM], pT[:, 0:P], a.value(0, h), start=True, stop=True)
        tensor.matmul(out[:, HEAD_DIM:2 * HEAD_DIM], pT[:, P:2 * P], a.value(0, h), start=True, stop=False)
        tensor.matmul(out[:, HEAD_DIM:2 * HEAD_DIM], pT[:, 2 * P:3 * P], a.value(1, h), start=False, stop=True
                      ).then_inc(c.sem("head_out"), 1)

    scores(0)
    scores(1)
    transposed(0)
    scores(2)
    for h in range(HEADS):
        if h + 1 < HEADS:
            transposed(h + 1)
        weighted(h)
        if h + 3 < HEADS:
            scores(h + 3)


def act_heads(c, act, a, first):
    def exps(h):
        g, b = first + h, h % 2
        act.wait_ge(c.sem("scores_read"), g + 1)
        if g >= 2:
            act.wait_ge(c.sem("probs_transposed"), g - 1)
        for t, lo, n in ((0, 0, P), (1, P, 2 * P)):
            last = c.nc.scalar.activation(a.w.p[b][:, lo:lo + n], a.w.s[b][:, lo:lo + n], ACT.Exp,
                                          bias=a.w.neg_max[:, h, t:t + 1], accum_out=a.w.sum[:, h, t:t + 1])
        last.then_inc(c.sem("probs_ready"), 1)

    def copied(h):
        g, b = first + h, h % 2
        act.wait_ge(c.sem("probs_transposed"), g + 1)
        if g >= 2:
            act.wait_ge(c.sem("head_out"), g - 1)
        c.nc.scalar.activation(a.w.pT[b], c.bank[PT_BANK[b]][:, 0:KEYS], ACT.Copy).then_inc(c.sem("probsT_ready"), 1)

    exps(0)
    exps(1)
    copied(0)
    for h in range(HEADS):
        if h + 1 < HEADS:
            copied(h + 1)
        if h + 2 < HEADS:
            exps(h + 2)


def dve_heads(c, dve, a, first):
    vector, chain = c.nc.vector, c.chain

    def masked(h):
        g, b = first + h, h % 2
        dve.wait_ge(c.sem("scores_done"), g + 1)
        if g >= 2:
            dve.wait_ge(c.sem("probs_ready"), g - 1)
        for t, lo, n in ((0, 0, P), (1, P, 2 * P)):
            add = a.c_q[:, t, h:h + 1] if a.c_q is not None else 0.0
            last = vector.scalar_tensor_tensor(a.w.s[b][:, lo:lo + n], c.bank[S_BANK[b]][:, lo:lo + n], add,
                                               c.causal[:, lo:lo + n], ALU.add, ALU.add)
        chain(last)
        for t, lo, n in ((0, 0, P), (1, P, 2 * P)):
            last = vector.tensor_reduce(a.w.neg_max[:, h, t:t + 1], a.w.s[b][:, lo:lo + n], AX, ALU.max, negate=True)
        last.then_inc(c.sem("scores_read"), 1)

    def out(h):
        g, b = first + h, h % 2
        dve.wait_ge(c.sem("head_out"), g + 1)
        chain(vector.reciprocal(a.w.coef[:, h, :], a.w.sum[:, h, :]))
        if a.gate is not None:
            chain(vector.tensor_tensor(a.w.coef[:, h, :], a.w.coef[:, h, :], a.gate(h), ALU.mult))
        for t in range(TOKS):
            src, dst = c.bank[O_BANK[b]][:, t * HEAD_DIM:(t + 1) * HEAD_DIM], a.out(t, h)
            if a.adds:
                last = vector.scalar_tensor_tensor(dst, src, a.w.coef[:, h, t:t + 1], dst, ALU.mult, ALU.add)
            else:
                last = vector.tensor_scalar(dst, src, a.w.coef[:, h, t:t + 1], None, ALU.mult)
        last.then_inc(c.sem("head_out_read"), 1)

    masked(0)
    masked(1)
    for h in range(HEADS):
        if h + 2 < HEADS:
            masked(h + 2)
        out(h)



def fa_views(c):
    class V:
        kT = arena(c, 0, P, KD, SEQ)
        v = arena(c, 2048, P, TOKS, D_MODEL)
        qT = arena(c, 4096, P, KD, SEQ)
        o = arena(c, 6144, P, TOKS, D_MODEL)
        b_f = arena(c, 10240, P, HEADS)
        minus_f, mag, e, s, s2, q, minus_lf, c_q = (arena(c, 10256 + 32 * j, P, TOKS, HEADS) for j in range(8))
        minus_cT = arena(c, 10512, HEADS, SEQ)
        heads = Heads(c, 10768)
    return V


def pool_kv(c, pool, st):
    pool.wait_ge(c.sem("h_updated"), st.updates)
    pool.dma_start(fa_views(c).b_f, c.small["b_fgate"].partition_broadcast(P)).then_inc(c.sem("b_f_loaded"), 16)


def pe_kv(c, pe, st):
    v, tensor = fa_views(c), c.nc.tensor
    pe.wait_ge(c.sem("xT_lo_ready"), KD * (st.norm + 1))
    for pr in st.projections:
        pe_project(c, pe, pr)
    pe.wait_ge(c.sem("log_f_ready"), 1)
    out = c.bank[7]
    tensor.matmul(out[:, 0:HEADS], c.upper[:], v.minus_lf[:, 0, :], start=True, stop=True)
    tensor.matmul(out[:, HEADS:2 * HEADS], c.ones[:], v.minus_lf[:, 0, :], start=True, stop=False)
    tensor.matmul(out[:, HEADS:2 * HEADS], c.upper[:], v.minus_lf[:, 1, :], start=False, stop=True
                  ).then_inc(c.sem("log_f_summed"), 1)
    pe.wait_ge(c.sem("minus_c_ready"), 1)
    for t in range(TOKS):
        last = tensor.transpose(c.bank[6][0:HEADS, t * P:(t + 1) * P], v.minus_lf[:, t, :], c.ident[:])
    last.then_inc(c.sem("minus_c_transposed"), 1)
    pe.wait_ge(c.sem("minus_cT_ready"), 1)


def act_kv(c, act, st):
    v = fa_views(c)
    for pr in st.projections:
        act_project(c, act, pr)
    act_softplus_exp(c, act, v.mag, v.e, "f_mag", 1, "f_exp")


def dve_kv(c, dve, st):
    v, vector, chain = fa_views(c), c.nc.vector, c.chain
    k, val, f = st.projections
    dve_project(c, dve, k, lambda s, view: vector.tensor_copy(v.kT[:, bass.ds(s * 2, 2), :], view))
    dve_project(c, dve, val, lambda s, view: vector.tensor_copy(v.v[:, :, bass.ds(s * PCOLS, PCOLS)], view))
    dve.wait_ge(c.sem("b_f_loaded"), 16)
    dve_project(c, dve, f, lambda s, view: vector.tensor_tensor(
        v.minus_f, view, v.b_f.unsqueeze(1).broadcast_to([P, TOKS, HEADS]), ALU.add))
    dve.wait_ge(c.sem("projection_read"), f.step + 1)
    chain(vector.tensor_scalar(v.minus_f, v.minus_f, -1.0, None, ALU.mult))
    dve_softplus_begin(c, v.minus_f, v.mag, "f_mag")
    dve_softplus_end(c, dve, v.minus_f, v.e, v.s, v.s2, v.q, v.minus_lf, "f_exp", 1)
    vector.tensor_copy(v.q, v.q).then_inc(c.sem("log_f_ready"), 1)
    dve.wait_ge(c.sem("log_f_summed"), 1)
    minus_c = c.bank[7][:, 0:TOKS * HEADS].rearrange("p (t h) -> p t h", t=TOKS)
    vector.tensor_scalar(v.c_q, minus_c, -1.0, None, ALU.mult)
    vector.tensor_copy(v.minus_lf, minus_c).then_inc(c.sem("minus_c_ready"), 1)
    dve.wait_ge(c.sem("minus_c_transposed"), 1)
    vector.tensor_copy(v.minus_cT, c.bank[6][0:HEADS, 0:SEQ]).then_inc(c.sem("minus_cT_ready"), 1)


def fa_heads(c):
    f = fa_views(c)

    class A:
        w, minus_cT, c_q, gate, adds = f.heads, f.minus_cT, f.c_q, None, False

        @staticmethod
        def qT(h):
            return f.qT[h % 2 * HEAD_DIM:(h % 2 + 1) * HEAD_DIM, h // 2, :]

        @staticmethod
        def kT(h):
            return f.kT[h % 2 * HEAD_DIM:(h % 2 + 1) * HEAD_DIM, h // 2, :]

        @staticmethod
        def value(t, h):
            return f.v[:, t, h * HEAD_DIM:(h + 1) * HEAD_DIM]

        @staticmethod
        def out(t, h):
            return f.o[:, t, h * HEAD_DIM:(h + 1) * HEAD_DIM]
    return A


def pe_fa(c, pe, st):
    v = fa_views(c)
    pe.wait_ge(c.sem("xT_lo_ready"), KD * (st.norm + 1))
    pe_project(c, pe, st.projections[0])
    pe.wait_ge(c.sem("projection_read"), st.projections[1].step)
    pe_heads(c, pe, fa_heads(c), st.heads)
    pe_to_operand(c, pe, st, v.o, "head_out_read", st.heads + HEADS)
    pe.wait_ge(c.sem("mix_lo"), 4 * (st.operand + 1))
    pe_project(c, pe, st.projections[1])


def act_fa(c, act, st):
    act_project(c, act, st.projections[0])
    act_heads(c, act, fa_heads(c), st.heads)
    act_to_operand(c, act, st)
    act_project(c, act, st.projections[1])
    act_residual(c, act, st)


def dve_fa(c, dve, st):
    v, vector = fa_views(c), c.nc.vector
    w_q, w_o = st.projections
    dve_project(c, dve, w_q, lambda s, view: vector.tensor_scalar(v.qT[:, bass.ds(s * 2, 2), :], view,
                                                                  HEAD_DIM ** -0.5, None, ALU.mult))
    dve_heads(c, dve, fa_heads(c), st.heads)
    dve_to_operand(c, dve, st)
    dve_project(c, dve, w_o, lambda s, view: vector.tensor_copy(c.mix_out[:, :, bass.ds(s * PCOLS, PCOLS)], view))
    dve_residual(c, dve, st)



G_HEADS = 8
G_DIM = 128
G_CHUNK = 64
G_TAPS = 4
LEVELS = (1, 2, 4, 8, 16, 32)


def gdn_views(c):
    used = [12288]

    def small(parts, *free):
        n = 1
        for d in free:
            n *= d
        used[0] += n
        assert used[0] <= 13312
        return arena(c, used[0] - n, parts, *free)

    def tile(n):
        return arena(c, n * 1024 if n < 6 else 13312 + (n - 6) * 1024, P, G_HEADS, P)

    masks = c.post_gain[:, :].rearrange("p (m i) -> p m i", m=8)

    class V:
        cv = arena(c, 6144, P, 24, SEQ)
        sq = arena(c, 0, P, 24, SEQ)
        kbe, kd, vb, X, Y, AT, attnT, T, decay = (tile(n) for n in range(9))
        u, wT = X, AT
        state = c.xn[:, 0, :].rearrange("p (h d) -> p h d", h=G_HEADS)
        o = c.xn[:, 1, :].rearrange("p (h d) -> p h d", h=G_HEADS)
        gate = c.mix_out
        pair = [masks[:, m, :] for m in range(6)]
        lower, upper = masks[:, 6, :], masks[:, 7, :]
        ab = small(P, TOKS, 2 * G_HEADS)
        beta = small(P, TOKS, G_HEADS)
        x, mag, e, s, s2, q, g = (small(P, TOKS, G_HEADS) for _ in range(7))
        select = small(P, 31)
        qk_rT = small(16, SEQ)
        log_decay, eg, kds, beg = (small(P, G_HEADS) for _ in range(4))
        gcT = small(G_HEADS, P)
        elast = small(P, G_HEADS, 2)
        a_log, dt = small(P, G_HEADS), small(P, G_HEADS)
        out_norm = small(P, G_DIM)
        taps = small(P, 24, G_TAPS)
        o_r = small(P, G_HEADS)
    return V


def flat(ap):
    return ap.rearrange("p a b -> p (a b)")


def over(ap, n):
    return ap.unsqueeze(2).broadcast_to([ap.shape[0], ap.shape[1], n])


def per_head(ap, heads=G_HEADS):
    return ap.unsqueeze(1).broadcast_to([ap.shape[0], heads, ap.shape[1]])


def half_heads(ap, b):
    return ap[:, 4 * b:4 * b + 4, :]


def bank_heads(c, b):
    return c.bank[b][:].rearrange("p (h d) -> p h d", h=4)


def pool_gdn(c, pool, st):
    v, g, u = gdn_views(c), c.nc.gpsimd, st.turn
    pool.wait_ge(c.sem("h_updated"), st.updates)
    for dst, src in ((flat(v.taps), c.small["gdn_taps"][u]), (v.a_log, c.small["gdn_A_log"][u].partition_broadcast(P)),
                     (v.dt, c.small["gdn_dt_bias"][u].partition_broadcast(P)),
                     (v.out_norm, c.small["gdn_out_norm"][u].partition_broadcast(P))):
        pool.dma_start(dst, src).then_inc(c.sem("gdn_small_loaded"), 16)
    if u:
        return
    made = [0]

    def step(ins):
        made[0] += 1
        ins.then_inc(c.sem("gdn_masks"), 1)
        pool.wait_ge(c.sem("gdn_masks"), made[0])

    def blocks(out, b):
        view = out.rearrange("p (a r) -> p a r", r=b)
        step(g.memset(out, 1.0))
        step(g.affine_select(out=view, in_=view, compare_op=ALU.is_ge, fill=0.0, base=0,
                             pattern=[[-b, P // b], [0, b]], channel_multiplier=1))
        step(g.affine_select(out=view, in_=view, compare_op=ALU.is_ge, fill=0.0, base=b - 1,
                             pattern=[[b, P // b], [0, b]], channel_multiplier=-1))

    for m, b in enumerate(LEVELS):
        blocks(v.pair[m], b)
    blocks(v.lower, G_CHUNK)
    step(g.affine_select(out=v.upper, in_=v.lower, compare_op=ALU.is_ge, fill=0.0, base=0,
                         pattern=[[1, P]], channel_multiplier=-1))
    for m in range(len(LEVELS) - 1):
        step(g.tensor_tensor(out=v.pair[m], in0=v.pair[m + 1], in1=v.pair[m], op=ALU.subtract))
    step(g.tensor_tensor(out=v.pair[5], in0=v.lower, in1=v.pair[5], op=ALU.subtract))
    step(g.affine_select(out=v.lower, in_=v.lower, compare_op=ALU.is_ge, fill=0.0, base=0,
                         pattern=[[-1, P]], channel_multiplier=1))
    assert made[0] == GDN_MASK_STEPS


GDN_MASK_STEPS = 3 * 7 + 1 + 5 + 1 + 1


def gdn_level_count(z, m, b):
    return 2 * ((len(LEVELS) - 1) * z + m - 1) + b + 1


def pe_gdn(c, pe, st):
    v, tensor, u = gdn_views(c), c.nc.tensor, st.turn
    heads = range(G_HEADS)
    mm, tr = tensor.matmul, tensor.transpose
    pe.wait_ge(c.sem("xT_lo_ready"), KD * (st.norm + 1))
    qkv, ab, gate, w_out = st.projections

    def norms():
        pe.wait_ge(c.sem("gdn_squares"), qkv.steps * (u + 1))
        for n in range(16):
            last = mm(c.bank[3][0:16, 0:SEQ], v.select[:, 15 - n:31 - n], v.sq[:, n, :], start=n == 0, stop=n == 15)
        last.then_inc(c.sem("gdn_norms"), 1)

    pe_project(c, pe, qkv)
    pe_project(c, pe, ab)
    pe_project(c, pe, gate, after=lambda s: norms() if s == 0 else None)
    pe.wait_ge(c.sem("gdn_qk_rT"), u + 1)
    for p in range(8):
        if p >= 4:
            pe.wait_ge(c.sem("gdn_scaled"), 8 * u + p - 3)
        for n in (2 * p, 2 * p + 1):
            last = mm(c.bank[4 + p % 4][:, (n % 2) * SEQ:(n % 2 + 1) * SEQ],
                      c.ident[0:16, n:n + 1].broadcast_to([16, P]), v.qk_rT, start=True, stop=True)
        last.then_inc(c.sem("gdn_factors"), 1)
    if u == 0:
        pe.wait_ge(c.sem("gdn_masks"), GDN_MASK_STEPS)
    pe.wait_ge(c.sem("gdn_scaled"), 8 * u + 8)
    pe.wait_ge(c.sem("gdn_g_ready"), u + 1)
    for t in range(TOKS):
        z, tok = TOKS * u + t, slice(t * P, (t + 1) * P)
        if z:
            pe.wait_ge(c.sem("gdn_o_read"), z)
        mm(c.bank[3][:, 0:G_HEADS], v.upper, v.g[:, t, :], start=True, stop=True)
        mm(c.bank[3][:, G_HEADS:2 * G_HEADS], v.lower, v.g[:, t, :], start=True, stop=True
           ).then_inc(c.sem("gdn_gc"), 1)
        for h in heads:
            tr(c.bank[4 + h // 4][:, (h % 4) * P:(h % 4 + 1) * P], v.cv[:, 8 + h, tok], c.ident[:])
        for h in heads:
            last = tr(c.bank[6 + h // 4][:, (h % 4) * P:(h % 4 + 1) * P], v.cv[:, 16 + h, tok], c.ident[:])
        last.then_inc(c.sem("gdn_kv_transposed"), 1)
        pe.wait_ge(c.sem("gdn_gc_sums"), z + 1)
        tr(c.bank[3][0:G_HEADS, 0:P], v.log_decay, c.ident[:]).then_inc(c.sem("gdn_gc_transposed"), 1)
        pe.wait_ge(c.sem("gdn_gcT"), z + 1)
        for h in heads:
            last = mm(c.bank[h // 4][:, (h % 4) * P:(h % 4 + 1) * P],
                      c.ident[0:G_HEADS, h:h + 1].broadcast_to([G_HEADS, P]), v.gcT, start=True, stop=True)
        last.then_inc(c.sem("gdn_gc_spread"), 1)
        pe.wait_ge(c.sem("gdn_kv_read"), z + 1)
        for h in heads:
            mm(c.bank[4 + h // 4][:, (h % 4) * P:(h % 4 + 1) * P], v.cv[:, 8 + h, tok], v.cv[:, 8 + h, tok],
               start=True, stop=True)
        for h in heads:
            last = mm(c.bank[6 + h // 4][:, (h % 4) * P:(h % 4 + 1) * P], v.cv[:, h, tok], v.cv[:, 8 + h, tok],
                      start=True, stop=True)
        last.then_inc(c.sem("gdn_products"), 1)
        pe.wait_ge(c.sem("gdn_masked"), z + 1)
        for h in heads:
            tr(c.bank[h // 4][:, (h % 4) * P:(h % 4 + 1) * P], v.T[:, h, :], c.ident[:])
        for h in heads:
            last = tr(c.bank[2 + h // 4][:, (h % 4) * P:(h % 4 + 1) * P], v.attnT[:, h, :], c.ident[:])
        last.then_inc(c.sem("gdn_transposed"), 1)
        for m in range(1, len(LEVELS)):
            for b in range(2):
                w = gdn_level_count(z, m, b)
                pe.wait_ge(c.sem("gdn_level_ready"), w)
                for h in range(4 * b, 4 * b + 4):
                    last = mm(c.bank[b][:, (h % 4) * P:(h % 4 + 1) * P], v.decay[:, h, :], v.X[:, h, :],
                              start=True, stop=True)
                last.then_inc(c.sem("gdn_ax"), 1)
            for b in range(2):
                w = gdn_level_count(z, m, b)
                pe.wait_ge(c.sem("gdn_T_ready"), w)
                for h in range(4 * b, 4 * b + 4):
                    last = mm(c.bank[4 + b][:, (h % 4) * P:(h % 4 + 1) * P], v.T[:, h, :], v.Y[:, h, :],
                              start=True, stop=True)
                if m < len(LEVELS) - 1:
                    for h in range(4 * b, 4 * b + 4):
                        last = mm(c.bank[6 + b][:, (h % 4) * P:(h % 4 + 1) * P], v.Y[:, h, :], v.T[:, h, :],
                                  start=True, stop=True)
                last.then_inc(c.sem("gdn_joined"), 1)
        for b in range(2):
            pe.wait_ge(c.sem("gdn_inverse"), 2 * z + b + 1)
            for h in range(4 * b, 4 * b + 4):
                mm(c.bank[b][:, (h % 4) * P:(h % 4 + 1) * P], v.Y[:, h, :], v.vb[:, h, :], start=True, stop=True)
            for h in range(4 * b, 4 * b + 4):
                last = mm(c.bank[2 + b][:, (h % 4) * P:(h % 4 + 1) * P], v.kbe[:, h, :], v.Y[:, h, :],
                          start=True, stop=True)
            last.then_inc(c.sem("gdn_uw"), 1)
        for k in range(2):
            x, row = 2 * z + k, slice(G_CHUNK * k, G_CHUNK * (k + 1))
            ctok = slice(t * P + G_CHUNK * k, t * P + G_CHUNK * (k + 1))
            pe.wait_ge(c.sem("gdn_state"), x + 1)
            if k == 0:
                pe.wait_ge(c.sem("gdn_uw_read"), z + 1)
            for h in heads:
                last = mm(c.bank[h // 4][row, (h % 4) * P:(h % 4 + 1) * P], v.wT[:, h, row], v.state[:, h, :],
                          start=True, stop=True)
            last.then_inc(c.sem("gdn_ws"), 1)
            for h in heads:
                mm(c.bank[2 + h // 4][row, (h % 4) * P:(h % 4 + 1) * P], v.cv[:, h, ctok], v.state[:, h, :],
                   start=True, stop=True)
            pe.wait_ge(c.sem("gdn_v_new"), x + 1)
            for h in heads:
                last = mm(c.bank[6 + h // 4][:, (h % 4) * P:(h % 4 + 1) * P], v.kd[row, h, :], v.T[row, h, :],
                          start=True, stop=True)
            last.then_inc(c.sem("gdn_kv_new"), 1)
            for h in heads:
                last = mm(c.bank[4 + h // 4][row, (h % 4) * P:(h % 4 + 1) * P], v.attnT[row, h, row], v.T[row, h, :],
                          start=True, stop=True)
            if k == 1:
                last.then_inc(c.sem("gdn_o"), 1)
    pe_to_operand(c, pe, st, c.mix_out, "gdn_out", 2 * u + 2)
    pe.wait_ge(c.sem("mix_lo"), 4 * (st.operand + 1))
    pe_project(c, pe, st.projections[3])


def act_gdn(c, act, st):
    v, scalar, u = gdn_views(c), c.nc.scalar, st.turn
    qkv, ab, gate, w_out = st.projections
    act.wait_ge(c.sem("gdn_small_loaded"), 64 * (u + 1))

    def activated(s):
        act.wait_ge(c.sem("projection_read"), qkv.step + s + 1)
        tiles = v.cv[:, bass.ds(2 * s, 2), :]
        scalar.activation(tiles, tiles, ACT.Silu).then_inc(c.sem("gdn_activated"), 1)
        act.wait_ge(c.sem("gdn_activated"), qkv.steps * u + s + 1)
        scalar.activation(v.sq[:, bass.ds(2 * s, 2), :], v.cv[:, bass.ds(2 * s, 2), :], ACT.Square
                          ).then_inc(c.sem("gdn_squares"), 1)

    act_project(c, act, qkv, act_first_tap(c, v.cv, v.taps, G_TAPS - 1), after=activated)
    act_project(c, act, ab)
    scalar.activation(v.a_log, v.a_log, ACT.Exp).then_inc(c.sem("gdn_exp_a"), 1)
    act_softplus_exp(c, act, v.mag, v.e, "gdn_mag", u + 1, "gdn_exp")
    scalar.activation(v.beta, v.ab[:, :, G_HEADS:2 * G_HEADS], ACT.Sigmoid).then_inc(c.sem("gdn_beta"), 1)

    def norms(s):
        if s == 1:
            act.wait_ge(c.sem("gdn_qk_ms"), u + 1)
            scalar.activation(v.qk_rT, v.qk_rT, ACT.Sqrt).then_inc(c.sem("gdn_qk_root"), 1)

    act_project(c, act, gate, after=norms)
    act.wait_ge(c.sem("projection_read"), gate.step + gate.steps)
    scalar.activation(v.gate[:], v.gate[:], ACT.Silu).then_inc(c.sem("gdn_silu_gate"), 1)
    for t in range(TOKS):
        z = TOKS * u + t
        act.wait_ge(c.sem("gdn_gc_sums"), z + 1)
        scalar.activation(v.eg, v.log_decay, ACT.Exp).then_inc(c.sem("gdn_eg"), 1)
        scalar.activation(v.kds, v.kds, ACT.Exp).then_inc(c.sem("gdn_kds"), 1)
        act.wait_ge(c.sem("gdn_gc_transposed"), z + 1)
        scalar.activation(v.gcT, c.bank[3][0:G_HEADS, 0:P], ACT.Copy).then_inc(c.sem("gdn_gcT"), 1)
        act.wait_ge(c.sem("gdn_gc_spread"), z + 1)
        for b in range(2):
            last = scalar.activation(half_heads(v.elast, b), bank_heads(c, b)[:, :, G_CHUNK - 1::G_CHUNK], ACT.Exp)
        last.then_inc(c.sem("gdn_elast"), 1)
        act.wait_ge(c.sem("gdn_gaps"), z + 1)
        scalar.activation(flat(v.decay), flat(v.decay), ACT.Exp, scale=-1.0).then_inc(c.sem("gdn_decay"), 1)
        act.wait_ge(c.sem("gdn_transposed"), z + 1)
        for b in range(2):
            last = scalar.activation(half_heads(v.attnT, b), bank_heads(c, 2 + b), ACT.Copy)
        last.then_inc(c.sem("gdn_attnT"), 1)
        for m in range(1, len(LEVELS)):
            for b in range(2):
                act.wait_ge(c.sem("gdn_ax"), gdn_level_count(z, m, b))
                scalar.activation(half_heads(v.T, b), bank_heads(c, b), ACT.Copy).then_inc(c.sem("gdn_T_ready"), 1)
        for b in range(2):
            act.wait_ge(c.sem("gdn_uw"), 2 * z + b + 1)
            last = scalar.activation(half_heads(v.wT, b), bank_heads(c, 2 + b), ACT.Copy)
        last.then_inc(c.sem("gdn_wT"), 1)
        act.wait_ge(c.sem("gdn_o_ms"), z + 1)
        scalar.activation(v.o_r, v.o_r, ACT.Sqrt).then_inc(c.sem("gdn_o_root"), 1)
    act_to_operand(c, act, st)
    act_project(c, act, w_out)


def dve_gdn(c, dve, st):
    v, vector, chain, u = gdn_views(c), c.nc.vector, c.chain, st.turn
    qkv, ab, gate, w_out = st.projections
    tt, tsc, stt = vector.tensor_tensor, vector.tensor_scalar, vector.scalar_tensor_tensor
    dve.wait_ge(c.sem("gdn_small_loaded"), 64 * (u + 1))
    chain(vector.memset(v.select, 0.0))
    vector.memset(v.select[:, 15:16], 1.0)
    dve_project(c, dve, qkv, dve_shifted_taps(c, dve, v.cv, v.taps, G_TAPS - 1, st.conv))
    dve_project(c, dve, ab, lambda s, view: vector.tensor_copy(v.ab, view))
    dve.wait_ge(c.sem("projection_read"), ab.step + 1)
    chain(tt(v.x, v.ab[:, :, 0:G_HEADS], per_head(v.dt, TOKS), ALU.add))
    dve_softplus_begin(c, v.x, v.mag, "gdn_mag")

    def norms(s):
        if s == 1:
            dve.wait_ge(c.sem("gdn_norms"), u + 1)
            tsc(v.qk_rT, c.bank[3][0:16, 0:SEQ], EPS, None, ALU.add).then_inc(c.sem("gdn_qk_ms"), 1)
        if s == 2:
            dve.wait_ge(c.sem("gdn_qk_root"), u + 1)
            chain(vector.reciprocal(v.qk_rT, v.qk_rT))
            tsc(v.qk_rT[0:G_HEADS, :], v.qk_rT[0:G_HEADS, :], G_DIM ** -0.5, None, ALU.mult
                ).then_inc(c.sem("gdn_qk_rT"), 1)

    dve_project(c, dve, gate, lambda s, view: vector.tensor_copy(v.gate[:, :, bass.ds(s * PCOLS, PCOLS)], view),
                after=norms)
    dve_softplus_end(c, dve, v.x, v.e, v.s, v.s2, v.q, v.g, "gdn_exp", u + 1)
    dve.wait_ge(c.sem("gdn_exp_a"), u + 1)
    stt(v.g, v.g, -1.0, per_head(v.a_log, TOKS), ALU.mult, ALU.mult).then_inc(c.sem("gdn_g_ready"), 1)
    for p in range(8):
        dve.wait_ge(c.sem("gdn_factors"), 8 * u + p + 1)
        tiles = v.cv[:, 2 * p:2 * p + 2, :]
        tt(tiles, tiles, c.bank[4 + p % 4][:].rearrange("p (n t) -> p n t", n=2), ALU.mult
           ).then_inc(c.sem("gdn_scaled"), 1)
    dve.wait_ge(c.sem("gdn_activated"), qkv.steps * (u + 1))
    vector.memset(flat(v.state), 0.0).then_inc(c.sem("gdn_state"), 1)
    for t in range(TOKS):
        z = TOKS * u + t
        dve.wait_ge(c.sem("gdn_gc"), z + 1)
        vector.tensor_copy(v.log_decay, c.bank[3][:, 0:G_HEADS])
        tt(v.kds, c.bank[3][:, G_HEADS:2 * G_HEADS], v.g[:, t, :], ALU.subtract).then_inc(c.sem("gdn_gc_sums"), 1)
        dve.wait_ge(c.sem("gdn_eg"), z + 1)
        dve.wait_ge(c.sem("gdn_beta"), u + 1)
        chain(tt(v.beg, v.beta[:, t, :], v.eg, ALU.mult))
        dve.wait_ge(c.sem("gdn_kds"), z + 1)
        dve.wait_ge(c.sem("gdn_kv_transposed"), z + 1)
        for b in range(2):
            tt(half_heads(v.kbe, b), bank_heads(c, 4 + b), over(v.beg[:, 4 * b:4 * b + 4], P), ALU.mult)
            tt(half_heads(v.kd, b), bank_heads(c, 4 + b), over(v.kds[:, 4 * b:4 * b + 4], P), ALU.mult)
            last = tt(half_heads(v.vb, b), bank_heads(c, 6 + b), over(v.beta[:, t, 4 * b:4 * b + 4], P), ALU.mult)
        last.then_inc(c.sem("gdn_kv_read"), 1)
        dve.wait_ge(c.sem("gdn_elast"), z + 1)
        for h in range(G_HEADS):
            last = tsc(v.decay[:, h, :], c.bank[h // 4][:, (h % 4) * P:(h % 4 + 1) * P], v.log_decay[:, h:h + 1], 0.0,
                       ALU.subtract, ALU.max)
        last.then_inc(c.sem("gdn_gaps"), 1)
        dve.wait_ge(c.sem("gdn_decay"), z + 1)
        if z == 0:
            dve.wait_ge(c.sem("gdn_masks"), GDN_MASK_STEPS)
        chain(tt(v.decay, v.decay, per_head(v.lower), ALU.mult))
        dve.wait_ge(c.sem("gdn_products"), z + 1)
        for b in range(2):
            tt(half_heads(v.attnT, b), bank_heads(c, 6 + b), half_heads(v.decay, b), ALU.mult)
            last = tt(half_heads(v.T, b), bank_heads(c, 4 + b), half_heads(v.decay, b), ALU.mult)
        chain(last)
        tt(v.T, v.T, over(v.beta[:, t, :], P), ALU.mult).then_inc(c.sem("gdn_masked"), 1)
        dve.wait_ge(c.sem("gdn_masked"), z + 1)
        chain(tt(v.X, v.T, per_head(v.pair[0]), ALU.mult))
        last = stt(v.X, v.X, -1.0, per_head(c.ident[:]), ALU.mult, ALU.add)
        dve.wait_ge(c.sem("gdn_attnT"), z + 1)
        for b in range(2):
            last = vector.tensor_copy(half_heads(v.AT, b), bank_heads(c, b))
        chain(last)
        chain(tt(v.Y, v.AT, per_head(v.pair[0]), ALU.mult))
        chain(stt(v.Y, v.Y, -1.0, per_head(c.ident[:]), ALU.mult, ALU.add))
        for b in range(2):
            tt(half_heads(v.decay, b), half_heads(v.AT, b), per_head(v.pair[1], 4), ALU.mult
               ).then_inc(c.sem("gdn_level_ready"), 1)
        for m in range(1, len(LEVELS)):
            for b in range(2):
                dve.wait_ge(c.sem("gdn_joined"), gdn_level_count(z, m, b))
                last = tt(half_heads(v.Y, b), half_heads(v.Y, b), bank_heads(c, 4 + b), ALU.subtract)
                if m < len(LEVELS) - 1:
                    tt(half_heads(v.X, b), half_heads(v.X, b), bank_heads(c, 6 + b), ALU.subtract)
                    tt(half_heads(v.decay, b), half_heads(v.AT, b), per_head(v.pair[m + 1], 4), ALU.mult
                       ).then_inc(c.sem("gdn_level_ready"), 1)
                else:
                    last.then_inc(c.sem("gdn_inverse"), 1)
        dve.wait_ge(c.sem("gdn_wT"), z + 1)
        for b in range(2):
            last = vector.tensor_copy(half_heads(v.u, b), bank_heads(c, b))
        last.then_inc(c.sem("gdn_uw_read"), 1)
        dve.wait_ge(c.sem("gdn_uw_read"), z + 1)
        for k in range(2):
            x, row = 2 * z + k, slice(G_CHUNK * k, G_CHUNK * (k + 1))
            dve.wait_ge(c.sem("gdn_ws"), x + 1)
            for b in range(2):
                last = tt(half_heads(v.T, b)[row], half_heads(v.u, b)[row], bank_heads(c, b)[row], ALU.subtract)
            last.then_inc(c.sem("gdn_v_new"), 1)
            dve.wait_ge(c.sem("gdn_kv_new"), x + 1)
            chain(tt(v.state, v.state, over(v.elast[:, :, k], P), ALU.mult))
            for b in range(2):
                last = tt(half_heads(v.state, b), half_heads(v.state, b), bank_heads(c, 6 + b), ALU.add)
            if x % 4 < 3:
                last.then_inc(c.sem("gdn_state"), 1)
        dve.wait_ge(c.sem("gdn_o"), z + 1)
        for b in range(2):
            last = tt(half_heads(v.o, b), bank_heads(c, 2 + b), over(v.eg[:, 4 * b:4 * b + 4], P), ALU.mult)
        chain(last)
        for b in range(2):
            last = tt(half_heads(v.o, b), half_heads(v.o, b), bank_heads(c, 4 + b), ALU.add)
        last.then_inc(c.sem("gdn_o_read"), 1)
        dve.wait_ge(c.sem("gdn_o_read"), z + 1)
        chain(tt(v.T, v.o, v.o, ALU.mult))
        chain(vector.tensor_reduce(v.o_r, v.T, AX, ALU.add))
        tsc(v.o_r, v.o_r, 1.0 / G_DIM, EPS, ALU.mult, ALU.add).then_inc(c.sem("gdn_o_ms"), 1)
        dve.wait_ge(c.sem("gdn_o_root"), z + 1)
        chain(vector.reciprocal(v.o_r, v.o_r))
        chain(tt(v.o, v.o, over(v.o_r, P), ALU.mult))
        chain(tt(v.o, v.o, per_head(v.out_norm), ALU.mult))
        dve.wait_ge(c.sem("gdn_silu_gate"), u + 1)
        gated = v.gate[:, t, :].rearrange("p (h d) -> p h d", h=G_HEADS)
        tt(gated, gated, v.o, ALU.mult).then_inc(c.sem("gdn_out"), 1)
    dve_to_operand(c, dve, st)
    dve_project(c, dve, w_out, dve_add_to_h(c, w_out))
    dve.wait_ge(c.sem("projection_read"), w_out.step + w_out.steps)
    vector.tensor_copy(c.ms[:], c.ms[:]).then_inc(c.sem("h_updated"), 1)



N_KV = 4
N_GROUP = HEADS // N_KV
CMP_BLOCK, CMP_STRIDE = 32, 16
N_CMP = SEQ // CMP_STRIDE - CMP_BLOCK // CMP_STRIDE + 1
CMP_TILES = CMP_BLOCK * HEAD_DIM // P
CMP_COLS = N_KV * N_CMP
PAD = 32
Q_COLS, KC, VC, KS, VS, KW, VW, GATES = 1024, 1024, 1280, 1536, 1792, 2048, 2304, 2560
NSA_IN = GATES + 3 * HEADS
PI = 3.141592653589793
ROUND = 12582912.0
TURN_A, TURN_B = 6.28125, 0.0019350051879882812
TURN_C = 2 * PI - TURN_A - TURN_B


def nsa_views(c):
    used = [15456]

    def small(parts, *free):
        n = 1
        for d in free:
            n *= d
        used[0] += n
        return arena(c, used[0] - n, parts, *free)

    silu, hid = flat(c.silu[:]), flat(c.hid[:])
    mix, xn = flat(c.mix_out[:]), flat(c.xn[:])

    class V:
        p = arena(c, 0, P, TOKS, NSA_IN)
        qr = arena(c, 5216, P, TOKS, D_MODEL)
        kT = [arena(c, 5216 + 1024 * j, P, N_KV, SEQ) for j in range(2)]
        qnT = arena(c, 7264, P, KD, SEQ)
        qrT = arena(c, 9312, P, KD, SEQ)
        dup = [arena(c, 11360 + 1024 * j, P, TOKS * N_KV, 2 * HEAD_DIM) for j in range(4)]
        heads = Heads(c, 11360)
        blk = mix.rearrange("p (k n) -> p k n", k=CMP_TILES)
        pc = mix[:, 0:1024].rearrange("p (a n) -> p a n", n=PAD)
        pcT = mix[:, 1024:2048].rearrange("p (a q) -> p a q", q=P)
        vcd = xn[:, 0:1024].rearrange("p (g n) -> p g n", g=N_KV)
        tmp = [xn[:, 1024 + 512 * j:1536 + 512 * j] for j in range(2)]
        hid_rows = [xn[0:CMP_COLS, 1024 + 512 * j:1024 + 512 * j + 256] for j in range(2)]
        w2 = small(P, 4, HEAD_DIM)
        hidT = [small(P, 2, CMP_COLS) for _ in range(2)]
        cos, sin = small(P, TOKS, 32), small(P, TOKS, 32)
        gates = small(P, TOKS, 3 * HEADS)
        b1 = small(P, 4)
        ms = silu[:, 0:48].rearrange("p (t n) -> p t n", t=TOKS)
        sc = hid[:, 0:480].rearrange("p (a n) -> p a n", n=N_CMP)
        q_norm, k_norm = silu[:, 64:128], silu[:, 128:320].rearrange("p (a n) -> p a n", a=3)
        b2 = silu[:, 320:448].rearrange("p (a n) -> p a n", a=2)
        pe = silu[:, 448:480].rearrange("p (a n) -> p a n", a=2)
        inv = silu[:, 480:512]
        ang, turns = (flat(c.hid[:])[:, 64 * j:64 * (j + 1)].rearrange("p (t n) -> p t n", t=TOKS) for j in (0, 1))
        posf = hid[:, 128:130]
        kcn = arena(c, 5728, N_CMP, N_KV, HEAD_DIM)
        kc2 = arena(c, 5216, N_CMP, N_KV, 2 * HEAD_DIM)
        kc_ms = hid[:, 500:504]
        small_0 = flat(small(P, 160, 1))
        cmax, csum = small_0[:, 0:32], small_0[:, 32:64]
        cmask = small_0[:, 64:64 + TOKS * N_CMP].rearrange("p (t n) -> p t n", t=TOKS)
        seen = small_0[:, 94:96]
        kcT = small_0[:, 96:96 + 64].rearrange("p (g n) -> p g n", g=N_KV)
        pos = c.nsa_pos[:]
    assert used[0] <= ARENA, used
    return V


def pool_nsa(c, pool, st):
    v, g = nsa_views(c), c.nc.gpsimd
    pool.wait_ge(c.sem("h_updated"), st.updates)
    s = c.small
    for dst, src in ((v.pos, s["positions"]), (v.inv, s["inv_freq"].partition_broadcast(P)),
                     (v.q_norm, s["nsa_q_norm"].partition_broadcast(P)),
                     (flat(v.k_norm), s["nsa_k_norm"].partition_broadcast(P)),
                     (flat(v.b2), s["nsa_b2"].partition_broadcast(P)), (flat(v.pe), s["nsa_pe"]),
                     (v.w2, s["nsa_w2"].rearrange("(a p) n -> p a n", p=P)), (v.b1, s["nsa_b1"])):
        pool.dma_start(dst, src).then_inc(c.sem("nsa_small_loaded"), 16)
    n = [0]

    def step(ins):
        n[0] += 1
        ins.then_inc(c.sem("nsa_masks"), 1)
        pool.wait_ge(c.sem("nsa_masks"), n[0])

    step(g.memset(v.small_0[:, 64:96], 0.0))
    for t in range(TOKS):
        part = v.cmask[:, t, :]
        step(g.affine_select(out=part, in_=part, compare_op=ALU.is_ge, fill=MASKED, base=P * t - CMP_BLOCK + 1,
                             pattern=[[-CMP_STRIDE, N_CMP]], channel_multiplier=1))
    step(g.memset(v.seen, 1.0))
    step(g.affine_select(out=v.seen, in_=v.seen, compare_op=ALU.is_ge, fill=0.0, base=1 - CMP_BLOCK,
                         pattern=[[P, TOKS]], channel_multiplier=1))
    assert n[0] == NSA_MASK_STEPS


NSA_MASK_STEPS = 5


def nsa_heads(c, branch):
    f = nsa_views(c)
    gates = f.gates.rearrange("p t (h i) -> p t h i", i=3)
    v0 = (VS, VW)[branch]

    class A:
        w, minus_cT, c_q, adds = f.heads, None, None, True

        @staticmethod
        def gate(h):
            return gates[:, :, h, branch + 1]

        @staticmethod
        def qT(h):
            return f.qrT[h % 2 * HEAD_DIM:(h % 2 + 1) * HEAD_DIM, h // 2, :]

        @staticmethod
        def kT(h):
            return f.kT[branch][h % 2 * HEAD_DIM:(h % 2 + 1) * HEAD_DIM, h // N_GROUP, :]

        @staticmethod
        def value(t, h):
            at = v0 + h // N_GROUP * HEAD_DIM
            return f.p[:, t, at:at + HEAD_DIM]

        @staticmethod
        def out(t, h):
            return f.p[:, t, h * HEAD_DIM:(h + 1) * HEAD_DIM]
    return A


NSA_BANKS = (4, 5, 6, 7)


def pe_nsa(c, pe, st):
    v, tensor = nsa_views(c), c.nc.tensor
    mm, tr = tensor.matmul, tensor.transpose
    w_in, w_gates, w1k, w1v, w_out = st.projections

    def transpose_wide(src):
        for k in range(KD):
            for t in range(TOKS):
                last = tr(c.bank[NSA_BANKS[k // 2]][:, (k % 2) * SEQ + t * P:(k % 2) * SEQ + (t + 1) * P],
                          src[:, t, k * P:(k + 1) * P], c.ident[:])
        return last

    def transpose_dup(src, banks):
        for h in range(N_KV):
            for t in range(TOKS):
                last = tr(c.bank[banks[h // 2]][:, (h % 2) * SEQ + t * P:(h % 2) * SEQ + (t + 1) * P],
                          src[:, t * N_KV + h, :], c.ident[:])
        return last

    pe.wait_ge(c.sem("xT_lo_ready"), KD * (st.norm + 1))
    pe_project(c, pe, w_in)
    pe_project(c, pe, w_gates)
    pe.wait_ge(c.sem("nsa_c_dup"), 1)
    transpose_dup(v.dup[0], NSA_BANKS[0:2])
    transpose_dup(v.dup[1], NSA_BANKS[2:4]).then_inc(c.sem("nsa_transposed"), 1)
    pe.wait_ge(c.sem("nsa_blk_lo"), 1)
    pe_project(c, pe, w1k)
    pe_project(c, pe, w1v)
    pe.wait_ge(c.sem("projection_read"), w1v.step + 1)
    for i in range(2):
        for k in range(2):
            at = (2 * i + k) * CMP_COLS
            last = tr(c.bank[3][:, at:at + CMP_COLS], v.hid_rows[i][:, k * P:(k + 1) * P],
                      c.ident[0:CMP_COLS, 0:CMP_COLS])
    last.then_inc(c.sem("nsa_hid_transposed"), 1)
    pe.wait_ge(c.sem("nsa_qn"), 1)
    transpose_wide(v.p).then_inc(c.sem("nsa_transposed"), 1)
    pe.wait_ge(c.sem("nsa_hidden"), 1)
    out = c.bank[3]
    for h in range(N_KV):
        for k in range(2):
            mm(out[0:N_CMP, h * HEAD_DIM:(h + 1) * HEAD_DIM], v.hidT[0][:, k, h * N_CMP:(h + 1) * N_CMP],
               v.w2[:, k, :], start=k == 0, stop=k == 1)
    for i in range(N_GROUP):
        for h in range(N_KV):
            for k in range(2):
                last = mm(out[PAD * i:PAD * i + N_CMP, 256 + h * HEAD_DIM:256 + (h + 1) * HEAD_DIM],
                          v.hidT[1][:, k, h * N_CMP:(h + 1) * N_CMP], v.w2[:, 2 + k, :], start=k == 0, stop=k == 1)
    last.then_inc(c.sem("nsa_compressed"), 1)
    pe.wait_ge(c.sem("nsa_kc_normed"), 1)
    for h in range(N_KV):
        last = tr(out[:, h * 16:h * 16 + N_CMP], v.kc2[:, h, :], c.ident[0:N_CMP, 0:N_CMP])
    last.then_inc(c.sem("nsa_kc_transposed"), 1)
    pe.wait_ge(c.sem("nsa_qr"), 1)
    pe.wait_ge(c.sem("nsa_brought"), 1)
    transpose_wide(v.qr).then_inc(c.sem("nsa_transposed"), 1)
    pe.wait_ge(c.sem("nsa_k_dup"), 1)
    pe.wait_ge(c.sem("nsa_brought"), 2)
    transpose_dup(v.dup[2], NSA_BANKS[0:2])
    transpose_dup(v.dup[3], NSA_BANKS[2:4]).then_inc(c.sem("nsa_transposed"), 1)
    pe.wait_ge(c.sem("nsa_kcT"), 1)
    pe.wait_ge(c.sem("nsa_brought"), 3)
    for t in range(TOKS):
        for h in range(HEADS):
            half = slice(h % 2 * HEAD_DIM, (h % 2 + 1) * HEAD_DIM)
            at = (t * HEADS + h) // 2 * 16
            last = mm(c.bank[4 + h % 2][:, at:at + N_CMP], v.qnT[half, h // 2, t * P:(t + 1) * P],
                      v.kcT[half, h // N_GROUP, 0:N_CMP], start=True, stop=True)
    last.then_inc(c.sem("nsa_c_scores"), 1)
    pe.wait_ge(c.sem("nsa_c_probs"), 1)
    for a in range(TOKS * N_KV):
        last = tr(c.bank[6 + a // N_KV][:, a % N_KV * P:(a % N_KV + 1) * P],
                  flat(v.pc)[:, a * P:(a + 1) * P], c.ident[:])
    last.then_inc(c.sem("nsa_c_probs_transposed"), 1)
    pe.wait_ge(c.sem("nsa_c_probsT"), 1)
    for a in range(TOKS * N_KV):
        last = mm(c.bank[2 + a // 2][:, a % 2 * 256:(a % 2 + 1) * 256], v.pcT[:, a, :], v.vcd[:, a % N_KV, :],
                  start=True, stop=True)
    last.then_inc(c.sem("nsa_c_out"), 1)
    pe.wait_ge(c.sem("nsa_c_added"), 1)
    pe_heads(c, pe, nsa_heads(c, 0), st.heads)
    pe_heads(c, pe, nsa_heads(c, 1), st.heads + HEADS)
    pe_to_operand(c, pe, st, v.p, "head_out_read", st.heads + 2 * HEADS)
    pe.wait_ge(c.sem("mix_lo"), 4 * (st.operand + 1))
    pe_project(c, pe, w_out)


def act_nsa(c, act, st):
    v, scalar = nsa_views(c), c.nc.scalar
    w_in, w_gates, w1k, w1v, w_out = st.projections
    act_project(c, act, w_in)
    act_project(c, act, w_gates)
    act.wait_ge(c.sem("nsa_angles"), 1)
    scalar.activation(v.sin, v.turns, ACT.Sin).then_inc(c.sem("nsa_sin_cos"), 1)
    scalar.activation(v.cos, v.ang, ACT.Sin).then_inc(c.sem("nsa_sin_cos"), 1)
    act.wait_ge(c.sem("nsa_blk"), 1)
    scalar.activation(c.xT_hi[:, 0:CMP_TILES, 0:2 * CMP_COLS], v.blk[:, :, 0:2 * CMP_COLS], ACT.Copy
                      ).then_inc(c.sem("nsa_blk_hi"), 1)
    act_project(c, act, w1k)
    act_project(c, act, w1v)
    act.wait_ge(c.sem("nsa_ms"), 1)
    scalar.activation(v.ms, v.ms, ACT.Sqrt).then_inc(c.sem("nsa_root"), 1)
    act.wait_ge(c.sem("nsa_hid_transposed"), 1)
    for i in range(2):
        for k in range(2):
            at = (2 * i + k) * CMP_COLS
            last = scalar.activation(v.hidT[i][:, k, :], c.bank[3][:, at:at + CMP_COLS], ACT.Gelu_apprx_tanh,
                                     bias=v.b1[:, 2 * i + k:2 * i + k + 1])
    last.then_inc(c.sem("nsa_hidden"), 1)
    act.wait_ge(c.sem("nsa_gates_in"), 1)
    scalar.activation(v.gates, v.p[:, :, GATES:NSA_IN], ACT.Sigmoid).then_inc(c.sem("nsa_gates"), 1)

    def bring(dst, transposed, scale=1.0):
        act.wait_ge(c.sem("nsa_transposed"), transposed)
        for b in range(4):
            last = scalar.activation(dst(b), c.bank[NSA_BANKS[b]][:], ACT.Copy, scale=scale)
        last.then_inc(c.sem("nsa_brought"), 1)

    bring(lambda b: flat(v.qnT[:, 2 * b:2 * b + 2, :]), 2, HEAD_DIM ** -0.5)
    act.wait_ge(c.sem("nsa_ms"), 2)
    scalar.activation(v.kc_ms[0:N_CMP], v.kc_ms[0:N_CMP], ACT.Sqrt).then_inc(c.sem("nsa_root"), 1)
    bring(lambda b: flat(v.qrT[:, 2 * b:2 * b + 2, :]), 3, HEAD_DIM ** -0.5)
    bring(lambda b: flat(v.kT[b // 2][:, 2 * (b % 2):2 * (b % 2) + 2, :]), 4)
    act.wait_ge(c.sem("nsa_c_shifted"), 1)
    scalar.activation(v.sc, v.sc, ACT.Exp).then_inc(c.sem("nsa_c_exp"), 1)
    act.wait_ge(c.sem("nsa_c_probs_transposed"), 1)
    for t in range(TOKS):
        last = scalar.activation(flat(v.pcT[:, N_KV * t:N_KV * (t + 1), :]), c.bank[6 + t][:], ACT.Copy)
    last.then_inc(c.sem("nsa_c_probsT"), 1)
    act_heads(c, act, nsa_heads(c, 0), st.heads)
    act_heads(c, act, nsa_heads(c, 1), st.heads + HEADS)
    act_to_operand(c, act, st)
    act_project(c, act, w_out)


def dve_nsa(c, dve, st):
    v, vector, chain = nsa_views(c), c.nc.vector, c.chain
    w_in, w_gates, w1k, w1v, w_out = st.projections
    tt, tsc, stt, copy = vector.tensor_tensor, vector.tensor_scalar, vector.scalar_tensor_tensor, vector.tensor_copy
    dve_project(c, dve, w_in, lambda s, view: copy(v.p[:, :, bass.ds(s * PCOLS, PCOLS)], view))
    dve_project(c, dve, w_gates, lambda s, view: copy(v.p[:, :, GATES:NSA_IN], view))
    dve.wait_ge(c.sem("projection_read"), w_gates.step + 1)
    vector.memset(v.vcd, 0.0).then_inc(c.sem("nsa_gates_in"), 1)

    def by_head(lo, n, t=None):
        part = v.p[:, :, lo:lo + n * HEAD_DIM] if t is None else v.p[:, t, lo:lo + n * HEAD_DIM]
        return part.rearrange("p t (h d) -> p t h d" if t is None else "p (h d) -> p h d", d=HEAD_DIM)

    for j, lo in ((0, KC), (1, VC)):
        for t in range(TOKS):
            for r in range(2):
                last = copy(v.dup[j][:, t * N_KV:(t + 1) * N_KV, r * HEAD_DIM:(r + 1) * HEAD_DIM], by_head(lo, N_KV, t))
    last.then_inc(c.sem("nsa_c_dup"), 1)

    dve.wait_ge(c.sem("nsa_small_loaded"), 128)
    chain(copy(v.posf, v.pos))
    for t in range(TOKS):
        last = tsc(v.ang[:, t, :], v.inv, v.posf[:, t:t + 1], None, ALU.mult)
    chain(last)
    chain(tsc(v.turns, v.ang, 1.0 / (2 * PI), None, ALU.mult))
    chain(tsc(v.turns, v.turns, ROUND, None, ALU.add))
    chain(tsc(v.turns, v.turns, -ROUND, None, ALU.add))
    for part in (TURN_A, TURN_B, TURN_C):
        chain(stt(v.ang, v.turns, -part, v.ang, ALU.mult, ALU.add))
    chain(tsc(v.turns, v.ang, 3.1415925, -3.1415925, ALU.min, ALU.max))
    chain(stt(v.ang, v.turns, -1.0, v.turns, ALU.mult, ALU.max))
    tsc(v.ang, v.ang, -1.0, PI / 2, ALU.mult, ALU.add).then_inc(c.sem("nsa_angles"), 1)

    dve.wait_ge(c.sem("nsa_transposed"), 1)
    for i in range(2):
        for b in range(2):
            for half in range(2):
                rows = slice(half * HEAD_DIM, (half + 1) * HEAD_DIM)
                src = c.bank[NSA_BANKS[2 * i + b]][rows].rearrange("p (h m s) -> p h m s", h=2, s=CMP_STRIDE)
                for kg in range(2):
                    at = i * CMP_COLS + 2 * b * N_CMP
                    ks = slice(kg * 8, kg * 8 + 8)
                    for hh in range(2):
                        out = v.blk[rows, ks, at + hh * N_CMP:at + (hh + 1) * N_CMP]
                        last = tt(out, src[:, hh, kg:kg + N_CMP, half::2].rearrange("p n k -> p k n"),
                                  over(v.pe[rows, i, ks], N_CMP), ALU.add)
    last.then_inc(c.sem("nsa_blk"), 1)
    dve.wait_ge(c.sem("nsa_blk_hi"), 1)
    tt(c.xT_lo[:, 0:CMP_TILES, 0:2 * CMP_COLS], v.blk[:, :, 0:2 * CMP_COLS],
       c.xT_hi[:, 0:CMP_TILES, 0:2 * CMP_COLS].bitcast(F32), ALU.subtract).then_inc(c.sem("nsa_blk_lo"), 1)

    sq = v.qr
    for t in range(TOKS):
        part = v.p[:, t, 0:Q_COLS]
        last = tt(sq[:, t, :], part, part, ALU.mult)
    chain(last)
    for t in range(TOKS):
        last = vector.tensor_reduce(v.ms[:, t, 0:HEADS], sq[:, t, :].rearrange("p (h d) -> p h d", d=HEAD_DIM), AX, ALU.add)
    chain(last)
    for t in range(TOKS):
        for j, lo in ((0, KS), (1, KW)):
            part = v.p[:, t, lo:lo + 256]
            last = tt(sq[:, t, 256 * j:256 * (j + 1)], part, part, ALU.mult)
    chain(last)
    for t in range(TOKS):
        last = vector.tensor_reduce(v.ms[:, t, HEADS:HEADS + 8],
                                    sq[:, t, 0:512].rearrange("p (h d) -> p h d", d=HEAD_DIM), AX, ALU.add)
    chain(last)
    tsc(v.ms, v.ms, 1.0 / HEAD_DIM, EPS, ALU.mult, ALU.add).then_inc(c.sem("nsa_ms"), 1)
    dve_project(c, dve, w1k, lambda s, view: copy(v.hid_rows[0], view))
    dve_project(c, dve, w1v, lambda s, view: copy(v.hid_rows[1], view))
    dve.wait_ge(c.sem("nsa_root"), 1)
    chain(vector.reciprocal(v.ms, v.ms))
    parts = [(by_head(lo, n, t), v.ms[:, t, a:a + n], n, g) for t in range(TOKS)
             for lo, n, a, g in ((0, HEADS, 0, v.q_norm), (KS, N_KV, HEADS, v.k_norm[:, 1, :]),
                                 (KW, N_KV, HEADS + N_KV, v.k_norm[:, 2, :]))]
    for x, r, n, g in parts:
        last = tt(x, x, over(r, HEAD_DIM), ALU.mult)
    chain(last)
    for x, r, n, g in parts:
        last = tt(x, x, per_head(g, n), ALU.mult)
    last.then_inc(c.sem("nsa_qn"), 1)

    dve.wait_ge(c.sem("nsa_compressed"), 1)
    comp = c.bank[3][:, 0:512].rearrange("p (a h d) -> p a h d", a=2, d=HEAD_DIM)
    chain(tt(v.kcn, comp[0:N_CMP, 0], per_head(v.b2[0:N_CMP, 0, :], N_KV), ALU.add))
    for i in range(N_GROUP):
        rows = slice(PAD * i, PAD * i + N_CMP)
        chain(tt(v.vcd[rows, :, i * HEAD_DIM:(i + 1) * HEAD_DIM], comp[rows, 1],
                 per_head(v.b2[rows, 1, :], N_KV), ALU.add))
    chain(tt(v.kc2[:, :, 0:HEAD_DIM], v.kcn, v.kcn, ALU.mult))
    chain(vector.tensor_reduce(v.kc_ms[0:N_CMP], v.kc2[:, :, 0:HEAD_DIM], AX, ALU.add))
    tsc(v.kc_ms[0:N_CMP], v.kc_ms[0:N_CMP], 1.0 / HEAD_DIM, EPS, ALU.mult, ALU.add).then_inc(c.sem("nsa_ms"), 1)
    dve.wait_ge(c.sem("nsa_root"), 2)
    chain(vector.reciprocal(v.kc_ms[0:N_CMP], v.kc_ms[0:N_CMP]))
    chain(tt(v.kcn, v.kcn, over(v.kc_ms[0:N_CMP], HEAD_DIM), ALU.mult))
    for r in range(2):
        last = tt(v.kc2[:, :, r * HEAD_DIM:(r + 1) * HEAD_DIM], v.kcn, per_head(v.k_norm[0:N_CMP, 0, :], N_KV), ALU.mult)
    last.then_inc(c.sem("nsa_kc_normed"), 1)
    dve.wait_ge(c.sem("nsa_kc_transposed"), 1)
    copy(v.kcT[:, :, 0:N_CMP], c.bank[3][:, 0:64].rearrange("p (g n) -> p g n", g=N_KV)[:, :, 0:N_CMP]
         ).then_inc(c.sem("nsa_kcT"), 1)

    dve.wait_ge(c.sem("nsa_sin_cos"), 2)
    half = HEAD_DIM // 2

    def rotate(x, dst, n, t):
        cos, sin = per_head(v.cos[:, t, :], n), per_head(v.sin[:, t, :], n)
        a, b = (v.tmp[j][:, 0:n * half].rearrange("p (h d) -> p h d", d=half) for j in range(2))
        x1, x2, o1, o2 = x[:, :, 0:half], x[:, :, half:HEAD_DIM], dst[:, :, 0:half], dst[:, :, half:HEAD_DIM]
        tt(a, x2, sin, ALU.mult)
        tt(b, x1, sin, ALU.mult)
        tt(o1, x1, cos, ALU.mult)
        chain(tt(o2, x2, cos, ALU.mult))
        tt(o1, o1, a, ALU.subtract)
        return tt(o2, o2, b, ALU.add)

    for t in range(TOKS):
        last = rotate(by_head(0, HEADS, t), v.qr[:, t, :].rearrange("p (h d) -> p h d", d=HEAD_DIM), HEADS, t)
        if t < TOKS - 1:
            chain(last)
    last.then_inc(c.sem("nsa_qr"), 1)
    dve.wait_ge(c.sem("nsa_qr"), 1)
    for j, lo in ((2, KS), (3, KW)):
        for t in range(TOKS):
            dst = v.dup[j][:, t * N_KV:(t + 1) * N_KV, :]
            chain(rotate(by_head(lo, N_KV, t), dst[:, :, 0:HEAD_DIM], N_KV, t))
            last = copy(dst[:, :, HEAD_DIM:2 * HEAD_DIM], dst[:, :, 0:HEAD_DIM])
    last.then_inc(c.sem("nsa_k_dup"), 1)

    dve.wait_ge(c.sem("nsa_c_scores"), 1)
    dve.wait_ge(c.sem("nsa_masks"), NSA_MASK_STEPS)
    for odd in range(2):
        scores = c.bank[4 + odd][:, 0:256].rearrange("p (t h n) -> p t h n", t=TOKS, n=16)
        for t in range(TOKS):
            last = tt(v.sc[:, t * HEADS + odd:(t + 1) * HEADS:2, :], scores[:, t, :, 0:N_CMP],
                      per_head(v.cmask[:, t, :], HEADS // 2), ALU.add)
    chain(last)
    chain(vector.tensor_reduce(v.cmax, v.sc, AX, ALU.max))
    tt(v.sc, v.sc, over(v.cmax, N_CMP), ALU.subtract).then_inc(c.sem("nsa_c_shifted"), 1)
    chain(vector.memset(v.pc, 0.0))
    dve.wait_ge(c.sem("nsa_c_exp"), 1)
    chain(vector.tensor_reduce(v.csum, v.sc, AX, ALU.add))
    chain(vector.reciprocal(v.csum, v.csum))
    dve.wait_ge(c.sem("nsa_gates"), 1)
    gate = v.gates.rearrange("p t (h i) -> p t h i", i=3)[:, :, :, 0]
    csum = v.csum.rearrange("p (t h) -> p t h", t=TOKS)
    chain(tt(csum, csum, gate, ALU.mult))
    chain(tt(csum, csum, over(v.seen, HEADS), ALU.mult))
    tt(v.pc[:, :, 0:N_CMP], v.sc, over(v.csum, N_CMP), ALU.mult).then_inc(c.sem("nsa_c_probs"), 1)
    dve.wait_ge(c.sem("nsa_c_out"), 1)
    for b in range(4):
        last = copy(v.p[:, b // 2, b % 2 * 512:(b % 2 + 1) * 512], c.bank[2 + b][:])
    last.then_inc(c.sem("nsa_c_added"), 1)
    dve.wait_ge(c.sem("nsa_c_added"), 1)
    dve_heads(c, dve, nsa_heads(c, 0), st.heads)
    dve.wait_ge(c.sem("head_out_read"), st.heads + HEADS)
    dve_heads(c, dve, nsa_heads(c, 1), st.heads + HEADS)
    dve_to_operand(c, dve, st)
    dve_project(c, dve, w_out, dve_add_to_h(c, w_out))
    dve.wait_ge(c.sem("projection_read"), w_out.step + w_out.steps)
    vector.tensor_copy(c.ms[:], c.ms[:]).then_inc(c.sem("h_updated"), 1)

def sp_projections(c, sp, st):
    for pr in st.projections:
        sp_project(c, sp, pr)


KINDS = ("ffn", "rg", "kv", "fa", "gdn", "sc", "nsa")
SP_STAGES = {k: sp_projections for k in KINDS} | {"ffn": sp_ffn}
PE_STAGES = dict(zip(KINDS, (pe_ffn, pe_rg, pe_kv, pe_fa, pe_gdn, pe_sc, pe_nsa)))
ACT_STAGES = dict(zip(KINDS, (act_ffn, act_rg, act_kv, act_fa, act_gdn, act_sc, act_nsa)))
DVE_STAGES = dict(zip(KINDS, (dve_ffn, dve_rg, dve_kv, dve_fa, dve_gdn, dve_sc, dve_nsa)))
POOL_STAGES = dict(zip(KINDS, (pool_load_post_gain, pool_rg, pool_kv, pool_load_post_gain, pool_gdn, pool_sc, pool_nsa)))


class Stage:

    def __init__(self, kind, projections=(), post=None, gate=None, up=None, down=None):
        self.kind, self.projections, self.post = kind, projections, post
        self.gate, self.up, self.down = gate, up, down


def number(stages):
    slab = norm = ffn = updates = post = step = operand = heads = conv = 0
    seen = {}
    for st in stages:
        st.slab, st.norm, st.ffn, st.updates, st.post_index = slab, norm, ffn, updates, post
        st.turn = seen.get(st.kind, 0)
        seen[st.kind] = st.turn + 1
        st.operand, st.heads, st.conv, st.mixer = operand, heads, conv, norm - ffn
        conv += {"gdn": 12, "rg": LRU_BLOCKS // 2}.get(st.kind, 0)
        operand += st.kind in ("fa", "gdn", "nsa")
        heads += {"fa": HEADS, "nsa": 2 * HEADS}.get(st.kind, 0)
        for pr in st.projections:
            pr.slab, pr.step = slab, step
            slab, step = slab + pr.steps * pr.slabs, step + pr.steps
        st.step_end = step
        if st.kind == "ffn":
            slab, ffn = slab + 3 * CHUNKS, ffn + 1
        if st.kind != "kv":
            updates, post = updates + 1, post + (st.post is not None)
        norm += 1
    return slab, norm


def build(nc, stages, x, out, **small):
    slabs, norms = number(stages)
    with ExitStack() as ctx:
        c = Core(nc, ctx)
        c.slabs, c.small = slabs, small
        c.gains = c.sb("gain_cols", [P, small["gains"].shape[1]])
        c.raw_landed = [c.sem(f"raw_landed{r}") for r in range(RING)]
        block = ctx.enter_context(nc.Block())

        @block.sync
        def _(sp):
            sp.dma_start(c.h[:], x.rearrange("(t p) d -> p t d", p=P)).then_inc(c.sem("x_loaded"), 16)
            sp.dma_start(c.gains[:], small["gains"]).then_inc(c.sem("gains_loaded"), 16)
            for st in stages:
                SP_STAGES[st.kind](c, sp, st)
            sp.wait_ge(c.sem("h_updated"), stages[-1].updates + 1)
            sp.dma_start(out.rearrange("(t p) d -> p t d", p=P), c.h[:]).then_inc(c.sem("out_stored"), 16)
            sp.wait_ge(c.sem("out_stored"), 16)

        @block.gpsimd
        def _(pool):
            pool_masks(c, pool)
            for st in stages:
                POOL_STAGES[st.kind](c, pool, st)

        @block.scalar
        def _(act):
            for n in range(RING):
                act_split(c, act, slab_number(n, 0))
            for st in stages:
                act_norm(c, act, st)
                ACT_STAGES[st.kind](c, act, st)

        @block.vector
        def _(dve):
            c.chain = Chain(dve, c.sem("dve_chain"))
            for n in range(RING):
                dve_split(c, dve, slab_number(n, 0))
            for st in stages:
                dve_norm(c, dve, st)
                DVE_STAGES[st.kind](c, dve, st)

        @block.tensor
        def _(pe):
            for st in stages:
                pe_norm(c, pe, st)
                PE_STAGES[st.kind](c, pe, st)


def model(nc, x, out, w, small):
    P_ = Projection

    def ffn1(name, layer):
        return Stage("ffn", gate=(w[name + "_w_gate"][layer], 0), up=(w[name + "_w_up"][layer], 0),
                     down=w[name + "_w_down"][layer], post=w[name + "_post_g"][layer])

    def ffn2(layer, half):
        gate_up = w["ffn_w_gate_up_2"][layer, half]
        return Stage("ffn", gate=(gate_up, 0), up=(gate_up, D_FF), down=w["ffn_w_down_2"][layer, half])

    def gdn(turn):
        w_in = w["gdn_w_in_2"][turn]
        return Stage("gdn", projections=[P_(w_in, 0, 12, "feat", loop=False), P_(w_in, 4096, 1, "tok", width=16),
                                         P_(w_in, 3072, 4, "tok"), P_(w["gdn_w_out_2"][turn], 0, 4, "tok")])

    recurrent = Stage("rg", post=w["mix_post_g"][0],
                      projections=[P_(w["rg_w_in"][0], 0, LRU_BLOCKS // 2, "feat", width=2 * LRU_W),
                                   P_(w["rg_w_in"][0], D_RNN, LRU_BLOCKS // 2, "feat", width=2 * LRU_W, loop=False),
                                   P_(w["rg_w_out"][0], 0, 4, "tok", kp=LRU_W, slabs=2, two_banks=True, padded=True)])
    shared_kv = Stage("kv", projections=[P_(w["w_kv"], 0, 4, "feat"), P_(w["w_kv"], D_MODEL, 4, "tok"),
                                         P_(w["w_fgate"], 0, 1, "tok", width=HEADS)])
    forgetting = Stage("fa", post=w["mix_post_g"][1],
                       projections=[P_(w["attn_w_q"][0], 0, 4, "feat"), P_(w["attn_w_o"][0], 0, 4, "tok")])
    w_sc = w["sc_w_in_2"][0]
    short_conv = Stage("sc", projections=[P_(w_sc, D_MODEL, 4, "feat"), P_(w_sc, 2 * D_MODEL, 4, "feat"),
                                          P_(w_sc, 0, 4, "feat"), P_(w["sc_w_out_2"][0], 0, 4, "tok")])
    w_nsa, w_cmp = w["nsa_w_in_2"][0], w["nsa_cmp_w1_2"][0]
    sparse = Stage("nsa", projections=[P_(w_nsa, 0, 10, "tok"), P_(w_nsa, GATES, 1, "tok", width=3 * HEADS),
                                       P_(w_cmp[0], 0, 1, "rows", slabs=2, operand_cols=(0, CMP_COLS)),
                                       P_(w_cmp[1], 0, 1, "rows", slabs=2, operand_cols=(CMP_COLS, 2 * CMP_COLS)),
                                       P_(w["nsa_w_out_2"][0], 0, 4, "tok")])
    stages = [ffn1("ffn1", 0), recurrent, ffn1("ffn2", 0), shared_kv, ffn1("ffn1", 1), forgetting, ffn1("ffn2", 1)]
    for layer, mixer in enumerate((gdn(0), short_conv, sparse, gdn(1))):
        stages += [ffn2(layer, 0), mixer, ffn2(layer, 1)]
    build(nc, stages, x, out, **small)


WEIGHTS = ("ffn1_w_gate", "ffn1_w_up", "ffn1_w_down", "ffn1_post_g", "mix_post_g", "ffn2_w_gate", "ffn2_w_up",
           "ffn2_w_down", "ffn2_post_g", "rg_w_in", "rg_w_out", "w_kv", "w_fgate", "attn_w_q", "attn_w_o",
           "ffn_w_gate_up_2", "ffn_w_down_2", "gdn_w_in_2", "gdn_w_out_2", "sc_w_in_2", "sc_w_out_2",
           "nsa_w_in_2", "nsa_cmp_w1_2", "nsa_w_out_2")


def layout(inputs):
    import numpy as np

    def columns(a, p=P):
        return np.asarray(a).reshape(-1, p).T

    i = {k: np.asarray(v) for k, v in inputs.items()}
    norms = [i["ffn1_pre_g"][0], i["mix_pre_g"][0], i["ffn2_pre_g"][0], i["kv_norm_g"],
             i["ffn1_pre_g"][1], i["mix_pre_g"][1], i["ffn2_pre_g"][1]]
    for layer in range(4):
        norms += [i["ffn_norm_2"][layer, 0], i["mixer_norm_2"][layer], i["ffn_norm_2"][layer, 1]]
    rg_taps = i["rg_conv_w"][0].reshape(LRU_TAPS, LRU_BLOCKS, LRU_W).transpose(2, 1, 0).reshape(LRU_W, -1)
    rg_vectors = [columns(i[k][0], LRU_W) for k in ("rg_conv_b", "rg_b_a", "rg_b_x", "rg_lambda")]
    small = {
        "gains": np.concatenate([columns(g) for g in norms], 1),
        "rg_small": np.concatenate([rg_taps] + rg_vectors, 1),
        "rg_w_a": i["rg_w_a"][0], "rg_w_x": i["rg_w_x"][0], "b_fgate": i["b_fgate"],
        "gdn_taps": i["gdn_conv_w_2"].reshape(2, 4, 24, P).transpose(0, 3, 2, 1).reshape(2, P, 96),
        "gdn_A_log": i["gdn_A_log_2"], "gdn_dt_bias": i["gdn_dt_bias_2"], "gdn_out_norm": i["gdn_out_norm_2"],
        "sc_taps": i["sc_conv_w_2"][0].reshape(3, KD, P).transpose(2, 1, 0).reshape(P, 3 * KD),
        "positions": i["positions_2"][0].reshape(TOKS, P).T,
        "inv_freq": np.float32(1) / (10000.0 ** (np.arange(0, HEAD_DIM, 2) / HEAD_DIM)).astype(np.float32),
        "nsa_q_norm": i["nsa_q_norm_2"][0], "nsa_k_norm": i["nsa_k_norm_2"][0].reshape(-1),
        "nsa_b2": i["nsa_cmp_b2_2"][0].reshape(-1),
        "nsa_pe": i["nsa_cmp_pe_2"][0].reshape(2, 16, P).transpose(2, 0, 1).reshape(P, 32),
        "nsa_w2": i["nsa_cmp_w2_2"][0].reshape(-1, HEAD_DIM),
        "nsa_b1": i["nsa_cmp_b1_2"][0].reshape(4, P).T,
    }
    return {k: np.ascontiguousarray(v) for k, v in small.items()}


def kernel(**inputs):
    import numpy as np
    import concourse.bacc as _bacc
    from concourse.bass_utils import run_bass_kernel_spmd as _run

    nc = _bacc.Bacc("TRN2", target_bir_lowering=False, num_devices=1)
    arrays = {}

    def dram(name, a):
        arrays[name] = np.ascontiguousarray(a)
        return nc.dram_tensor(name, a.shape, mybir.dt.from_np(a.dtype), kind="ExternalInput").ap()

    x = dram("x", np.asarray(inputs["x"])[0])
    w = {k: dram(k, np.asarray(inputs[k])) for k in WEIGHTS}
    small = {k: dram(k, a) for k, a in layout(inputs).items()}
    out = nc.dram_tensor("out", (SEQ, D_MODEL), F32, kind="ExternalOutput").ap()
    model(nc, x, out, w, small)
    return _run(nc, [arrays], core_ids=[0]).results[0]["out"].reshape(1, SEQ, D_MODEL)
```
